# Optimizing a Trainium2 kernel written in Bass

```python
import math
import jax, jax.numpy as jnp
from jax import lax
import numpy as np

D_MODEL = 1024
BATCH = 1
SEQ = 512
DEPTH = 1
DEC_BATCH = 8
DEC_SEQ = 1
PAST_LEN = 4096
PAGE_SIZE = 128

A_WIDTH = D_MODEL
A_GROUPS = 8
A_GROUP_DIM = A_WIDTH // A_GROUPS
A_CHUNK = 128
B_DK = 128
B_DV = 128
B_HEADS = D_MODEL // B_DV
B_QK = B_HEADS * B_DK
B_V = B_HEADS * B_DV
C_QKV = 2 * B_QK + B_V
B_CONV = 4
B_CHUNK = 64
N_MEM = 256
M_HEADS = 4
M_HEAD_DIM = D_MODEL // M_HEADS
M_Q = M_HEADS * M_HEAD_DIM
N_GROUPS = 4
EXP_PER_GROUP = 8
N_EXPERTS = N_GROUPS * EXP_PER_GROUP
TOP_K = 2
D_EXPERT = 512
EPS = 1e-6
PROJ_SIZES = (A_WIDTH, A_WIDTH, C_QKV, B_V, B_HEADS, B_HEADS, M_Q, 3 * D_MODEL)
PROJ_WIDTH = 2 * A_WIDTH + C_QKV + B_V + 2 * B_HEADS + M_Q + 3 * D_MODEL

kernel_name = 'hybrid_gmlp_gdn_memxattn_hiermoe_step'

F32 = jnp.float32

def split_cols(t, sizes):
    out, start = [], 0
    for s in sizes:
        out.append(t[..., start:start + s])
        start += s
    return out

def rmsnorm(x, g):
    xf = x.astype(F32)
    y = xf * lax.rsqrt(jnp.mean(xf * xf, axis=-1, keepdims=True) + EPS) * g.astype(F32)
    return y.astype(x.dtype)

def l2norm(t):
    tf = t.astype(F32)
    return tf * lax.rsqrt(jnp.sum(tf * tf, axis=-1, keepdims=True) + EPS)

def chunk_spatial_gate(u, v, w_s, b_s):
    bsz, L, _ = v.shape
    pad = (-L) % A_CHUNK
    n = (L + pad) // A_CHUNK
    vc = jnp.pad(v, ((0, 0), (0, pad), (0, 0))).reshape(bsz, n, A_CHUNK, A_GROUPS, A_GROUP_DIM)
    causal = jnp.tril(jnp.ones((A_CHUNK, A_CHUNK), bool))
    ws = jnp.where(causal, w_s, 0.0).astype(v.dtype)
    sv = jnp.einsum('gij,bnjgc->bnigc', ws, vc) + b_s.T.astype(v.dtype)[None, None, :, :, None]
    sv = sv.reshape(bsz, n * A_CHUNK, A_WIDTH)[:, :L]
    return u * sv

def gated_delta_rule(q, k, v, g, beta, s0):
    bsz, L, H, _ = q.shape
    dv = v.shape[-1]
    C = math.gcd(B_CHUNK, L)
    n = L // C

    def chunks(t):
        return t.reshape(bsz, n, C, H, -1).transpose(1, 0, 3, 2, 4)

    def chunks_h(t):
        return t.reshape(bsz, n, C, H).transpose(1, 0, 3, 2)

    qc, kc, vc = chunks(q), chunks(k), chunks(v)
    gc, bc = chunks_h(g), chunks_h(beta)
    G = jnp.cumsum(gc, axis=-1)
    incl = jnp.tril(jnp.ones((C, C), bool))
    strict = jnp.tril(jnp.ones((C, C), bool), -1)
    decay = jnp.where(incl, jnp.exp(jnp.where(incl, G[..., :, None] - G[..., None, :], 0.0)), 0.0)
    kb = kc * bc[..., None]
    m = jnp.where(strict, jnp.einsum('nbhik,nbhjk->nbhij', kb, kc) * decay, 0.0)
    rhs = jnp.concatenate([vc * bc[..., None], kb * jnp.exp(G)[..., None]], axis=-1)
    sol = lax.linalg.triangular_solve(m + jnp.eye(C, dtype=m.dtype), rhs,
                                      left_side=True, lower=True, unit_diagonal=True)
    vt, wk = sol[..., :dv], sol[..., dv:]
    attn = jnp.einsum('nbhik,nbhjk->nbhij', qc, kc) * decay
    qg = qc * jnp.exp(G)[..., None]
    kd = kc * jnp.exp(G[..., -1:] - G)[..., None]
    gl = jnp.exp(G[..., -1])

    def step(S, xs):
        vt_i, wk_i, attn_i, qg_i, kd_i, gl_i = xs
        u = vt_i - jnp.einsum('bhck,bhkv->bhcv', wk_i, S)
        o = jnp.einsum('bhck,bhkv->bhcv', qg_i, S) + jnp.einsum('bhij,bhjv->bhiv', attn_i, u)
        S = S * gl_i[..., None, None] + jnp.einsum('bhck,bhcv->bhkv', kd_i, u)
        return S, o

    s_new, o = lax.scan(step, s0, (vt, wk, attn, qg, kd, gl))
    o = o.transpose(1, 0, 3, 2, 4).reshape(bsz, L, H, dv)
    return o, s_new

def memory_kv(mem, norm_mem, w_mem_kv):
    bsz = mem.shape[0]
    kv = rmsnorm(mem, norm_mem) @ w_mem_kv
    mk, mv = split_cols(kv, (M_Q, M_Q))
    return (mk.reshape(bsz, N_MEM, M_HEADS, M_HEAD_DIM), mv.reshape(bsz, N_MEM, M_HEADS, M_HEAD_DIM))

def memory_attend(q_m, mem_k, mem_v):
    bsz, L, _ = q_m.shape
    q = q_m.reshape(bsz, L, M_HEADS, M_HEAD_DIM)
    s = jnp.einsum('blhd,bmhd->bhlm', q, mem_k.astype(q.dtype)).astype(F32) * (M_HEAD_DIM ** -0.5)
    pr = jax.nn.softmax(s, axis=-1).astype(q.dtype)
    o = jnp.einsum('bhlm,bmhd->blhd', pr, mem_v.astype(q.dtype))
    return o.reshape(bsz, L, M_Q)

def hier_moe(h, p):
    bsz, L, D = h.shape
    t = h.reshape(-1, D)
    grp_logits = (t @ p['w_router_group'] + p['b_router_group']).astype(F32)
    grp_prob = jax.nn.softmax(grp_logits, axis=-1)
    g_idx = jnp.argmax(grp_logits, axis=-1)
    p_g = jnp.take_along_axis(grp_prob, g_idx[:, None], axis=-1)
    exp_logits = (t @ p['w_router_expert'] + p['b_router_expert']).astype(F32)
    exp_logits = exp_logits.reshape(-1, N_GROUPS, EXP_PER_GROUP)
    in_grp = jnp.take_along_axis(exp_logits, g_idx[:, None, None], axis=1)[:, 0]
    top_v, top_i = lax.top_k(in_grp, TOP_K)
    w_top = jax.nn.softmax(top_v, axis=-1) * p_g
    w_exp = jnp.sum(jax.nn.one_hot(top_i, EXP_PER_GROUP, dtype=F32) * w_top[..., None], axis=1)
    combine = (jax.nn.one_hot(g_idx, N_GROUPS, dtype=F32)[:, :, None] * w_exp[:, None, :]).astype(h.dtype)
    y = jnp.zeros_like(t)
    for gi in range(N_GROUPS):
        gate = jnp.einsum('td,edf->tef', t, p['w_exp_gate'][gi])
        up = jnp.einsum('td,edf->tef', t, p['w_exp_up'][gi])
        act = jax.nn.silu(gate) * up * combine[:, gi, :, None]
        y = y + jnp.einsum('tef,efd->td', act, p['w_exp_down'][gi])
    return y.reshape(bsz, L, D)

def hybrid_layer(x, mem_k, mem_v, s0, conv_buf, p):
    bsz, L, _ = x.shape
    h = rmsnorm(x, p['norm_mix'])
    proj = h @ p['w_in']
    a_u, a_v, qkv_pre, z, beta_l, alpha_l, q_m, gate_l = split_cols(proj, PROJ_SIZES)
    a_u = jax.nn.gelu(a_u)
    a_v = rmsnorm(jax.nn.gelu(a_v), p['norm_a_v'])
    o_a = chunk_spatial_gate(a_u, a_v, p['w_s'], p['b_s'])
    ext = jnp.concatenate([conv_buf.astype(qkv_pre.dtype), qkv_pre], axis=1)
    conv = sum(p['w_conv'][j] * ext[:, j:j + L] for j in range(B_CONV))
    new_buf = ext[:, L:]
    qkv = jax.nn.silu(conv)
    q, k, v = split_cols(qkv, (B_QK, B_QK, B_V))
    q = l2norm(q.reshape(bsz, L, B_HEADS, B_DK)) * (B_DK ** -0.5)
    k = l2norm(k.reshape(bsz, L, B_HEADS, B_DK))
    v = v.reshape(bsz, L, B_HEADS, B_DV).astype(F32)
    beta = jax.nn.sigmoid(beta_l.astype(F32))
    g = -jnp.exp(p['a_log'].astype(F32)) * jax.nn.softplus(alpha_l.astype(F32) + p['dt_bias'].astype(F32))
    o_b, s_new = gated_delta_rule(q, k, v, g, beta, s0.astype(F32))
    o_b = rmsnorm(o_b.astype(x.dtype), p['norm_gdn_out']) * jax.nn.silu(z.reshape(bsz, L, B_HEADS, B_DV))
    o_b = o_b.reshape(bsz, L, B_V)
    o_c = memory_attend(q_m, mem_k, mem_v)
    gates = jax.nn.sigmoid((gate_l + p['b_gate']).astype(F32)).astype(x.dtype)
    g_a, g_b, g_c = split_cols(gates, (D_MODEL, D_MODEL, D_MODEL))
    x = x + (g_a * o_a + g_b * o_b + g_c * o_c) @ p['w_o']
    x = x + hier_moe(rmsnorm(x, p['norm_ffn']), p)
    return x, s_new.astype(s0.dtype), new_buf, a_v

def setup_inputs(seed: int = 0) -> dict:
    key = jax.random.key(seed)
    ks = jax.random.split(key, 32)

    def nrm(k, shape, scale=1.0):
        return jax.random.normal(k, shape, F32) * scale

    def gain(k, shape):
        return 1.0 + 0.1 * jax.random.normal(k, shape, F32)

    dt = jnp.exp(jax.random.uniform(ks[10], (DEPTH, B_HEADS), F32, math.log(1e-3), math.log(1e-1)))
    return {
        'x_prompt': nrm(ks[0], (BATCH, SEQ, D_MODEL)),
        'x_sample': nrm(ks[1], (DEC_BATCH, DEC_SEQ, D_MODEL)),
        'mem_prompt': nrm(ks[2], (BATCH, N_MEM, D_MODEL)),
        'cache_mem_k': nrm(ks[3], (DEPTH, DEC_BATCH, N_MEM, M_HEADS, M_HEAD_DIM)),
        'cache_mem_v': nrm(ks[4], (DEPTH, DEC_BATCH, N_MEM, M_HEADS, M_HEAD_DIM)),
        'state_gdn': nrm(ks[5], (DEPTH, DEC_BATCH, B_HEADS, B_DK, B_DV), 0.3),
        'state_conv': nrm(ks[6], (DEPTH, DEC_BATCH, B_CONV - 1, C_QKV)),
        'norm_mix': gain(ks[7], (DEPTH, D_MODEL)),
        'w_in': nrm(ks[8], (DEPTH, D_MODEL, PROJ_WIDTH), D_MODEL ** -0.5),
        'b_gate': nrm(ks[9], (DEPTH, 3 * D_MODEL), 0.1),
        'w_s': nrm(ks[11], (DEPTH, A_GROUPS, A_CHUNK, A_CHUNK), A_CHUNK ** -0.5),
        'b_s': nrm(ks[12], (DEPTH, A_GROUPS, A_CHUNK), 0.1),
        'norm_a_v': gain(ks[13], (DEPTH, A_WIDTH)),
        'w_conv': nrm(ks[14], (DEPTH, B_CONV, C_QKV), B_CONV ** -0.5),
        'a_log': jnp.log(jax.random.uniform(ks[15], (DEPTH, B_HEADS), F32, 1.0, 16.0)),
        'dt_bias': dt + jnp.log(-jnp.expm1(-dt)),
        'norm_gdn_out': gain(ks[16], (DEPTH, B_DV)),
        'norm_mem': gain(ks[17], (DEPTH, D_MODEL)),
        'w_mem_kv': nrm(ks[18], (DEPTH, D_MODEL, 2 * M_Q), D_MODEL ** -0.5),
        'w_o': nrm(ks[19], (DEPTH, D_MODEL, D_MODEL), D_MODEL ** -0.5),
        'norm_ffn': gain(ks[20], (DEPTH, D_MODEL)),
        'w_router_group': nrm(ks[21], (DEPTH, D_MODEL, N_GROUPS), D_MODEL ** -0.5),
        'b_router_group': nrm(ks[22], (DEPTH, N_GROUPS), 0.01),
        'w_router_expert': nrm(ks[23], (DEPTH, D_MODEL, N_EXPERTS), D_MODEL ** -0.5),
        'b_router_expert': nrm(ks[24], (DEPTH, N_EXPERTS), 0.01),
        'w_exp_gate': nrm(ks[25], (DEPTH, N_GROUPS, EXP_PER_GROUP, D_MODEL, D_EXPERT), D_MODEL ** -0.5),
        'w_exp_up': nrm(ks[26], (DEPTH, N_GROUPS, EXP_PER_GROUP, D_MODEL, D_EXPERT), D_MODEL ** -0.5),
        'w_exp_down': nrm(ks[27], (DEPTH, N_GROUPS, EXP_PER_GROUP, D_EXPERT, D_MODEL), D_EXPERT ** -0.5),
        'norm_final': gain(ks[28], (D_MODEL,)),
    }

def reference(x_prompt, x_sample, mem_prompt, cache_mem_k, cache_mem_v, state_gdn, state_conv,
              norm_mix, w_in, b_gate, w_s, b_s, norm_a_v, w_conv, a_log, dt_bias, norm_gdn_out,
              norm_mem, w_mem_kv, w_o, norm_ffn, w_router_group, b_router_group, w_router_expert,
              b_router_expert, w_exp_gate, w_exp_up, w_exp_down, norm_final):
    bp = x_prompt.shape[0]
    y_p, y_s = x_prompt, x_sample
    mk_list, mv_list, sp_list, cp_list, ss_list, cs_list, vs_list = [], [], [], [], [], [], []
    for l in range(DEPTH):
        p = dict(norm_mix=norm_mix[l], w_in=w_in[l], b_gate=b_gate[l], w_s=w_s[l], b_s=b_s[l],
                 norm_a_v=norm_a_v[l], w_conv=w_conv[l], a_log=a_log[l], dt_bias=dt_bias[l],
                 norm_gdn_out=norm_gdn_out[l], w_o=w_o[l], norm_ffn=norm_ffn[l],
                 w_router_group=w_router_group[l], b_router_group=b_router_group[l],
                 w_router_expert=w_router_expert[l], b_router_expert=b_router_expert[l],
                 w_exp_gate=w_exp_gate[l], w_exp_up=w_exp_up[l], w_exp_down=w_exp_down[l])
        mk_p, mv_p = memory_kv(mem_prompt, norm_mem[l], w_mem_kv[l])
        s0_p = jnp.zeros((bp, B_HEADS, B_DK, B_DV), x_prompt.dtype)
        buf_p = jnp.zeros((bp, B_CONV - 1, C_QKV), x_prompt.dtype)
        y_p, s_p, c_p, _ = hybrid_layer(y_p, mk_p, mv_p, s0_p, buf_p, p)
        y_s, s_s, c_s, v_s = hybrid_layer(y_s, cache_mem_k[l], cache_mem_v[l], state_gdn[l], state_conv[l], p)
        mk_list.append(mk_p)
        mv_list.append(mv_p)
        sp_list.append(s_p)
        cp_list.append(c_p)
        ss_list.append(s_s)
        cs_list.append(c_s)
        vs_list.append(v_s)
    y_prompt = rmsnorm(y_p, norm_final)
    y_sample = rmsnorm(y_s, norm_final)
    return (y_prompt, y_sample, jnp.stack(mk_list), jnp.stack(mv_list), jnp.stack(sp_list),
            jnp.stack(cp_list), jnp.stack(ss_list), jnp.stack(cs_list), jnp.stack(vs_list))


_drawn_inputs = setup_inputs


def setup_inputs(seed=0):
    import zlib

    import numpy as np

    out = dict(_drawn_inputs(seed))
    spreads = {}
    factors = {'b_router_expert': 4.237}
    for name, (base, spread) in spreads.items():
        noise = np.random.default_rng([zlib.crc32(name.encode()), seed]).standard_normal(out[name].shape)
        drawn = base * np.exp(spread * noise) if base else spread * noise
        out[name] = __import__('jax').numpy.asarray(drawn.astype(out[name].dtype))
    for name, factor in factors.items():
        out[name] = (out[name] * factor).astype(out[name].dtype)
    return out
```

```python
from contextlib import ExitStack

import numpy as np
import concourse.bass as bass
from concourse import mybir

F32 = mybir.dt.float32
F32R = mybir.dt.float32r
I32 = mybir.dt.int32
ALU = mybir.AluOpType
ACT = mybir.ActivationFunctionType
AX = mybir.AxisListType

D = 1024
SEQ = 512
NS = 8
T = SEQ + NS
HALF = T // 2
KD = D // 128
NM = 256
NH = 8
MH = 4
CH = 128
NCH = SEQ // CH
BLK = 256
NG, EPG = 4, 8
NE = NG * EPG
DE = 512
CAP = 64
TT, NT = 104, 5
EPS = 1e-6
RW = 32

BLOCKS = [("av", 4), ("au", 4), ("mk", 4), ("mv", 4), ("ga", 4), ("qm", 4), ("gb", 4), ("z", 4),
          ("gc", 4), ("qkv", 12), ("wo", 4)]
BLOCK_KIND = [name for name, n in BLOCKS for _ in range(n)]
FIRST_BLOCK = {name: BLOCK_KIND.index(name) for name, _ in BLOCKS}
NBLK = len(BLOCK_KIND)
WO_BLOCK = FIRST_BLOCK["wo"]
WO_TILE = 2 * WO_BLOCK
QKV_TILE = 2 * FIRST_BLOCK["qkv"]

CONST = {}
_at = 0
for _n, _w in [("ident", 128), ("ones", 128), ("triu", 128), ("strict", 128), ("first_t", 128),
               ("merge", 6 * 128), ("slots", CAP), ("rounds", 8), ("desc4", 4), ("desc8", 8),
               ("eps", 1), ("eps128", 1)]:
    CONST[_n] = (_at, _at + _w)
    _at += _w
NCONST = _at
PARAM = {}
_at = 0
for _n, _w in [("norm_mix", 8), ("norm_mem", 8), ("norm_ffn", 8), ("norm_final", 8), ("norm_a_v", 8),
               ("norm_gdn", 1), ("b_gate", 24), ("w_conv", 96), ("ws00", 8), ("bs0", 8),
               ("a_log", 8), ("dt_bias", 8), ("b_router", NG + NE)]:
    PARAM[_n] = (_at, _at + _w)
    _at += _w
NPARAM = _at


def make_constants():
    c = np.zeros((128, NCONST), np.float32)
    p, f = np.arange(128)[:, None], np.arange(128)[None, :]

    def put(name, value):
        a, b = CONST[name]
        c[:, a:b] = value

    put("ident", p == f)
    put("ones", 1.0)
    put("triu", p <= f)
    put("strict", p < f)

    def below(s):
        return (p // (2 * s) == f // (2 * s)) & (p // s % 2 == 1) & (f // s % 2 == 0)

    put("first_t", below(1).T)
    put("merge", np.concatenate([below(s) for s in (2, 4, 8, 16, 32, 64)], axis=1))
    put("slots", np.arange(CAP))
    put("rounds", CAP * np.arange(1, 9))
    put("desc4", np.arange(4, 0, -1))
    put("desc8", np.arange(8, 0, -1))
    put("eps", EPS)
    put("eps128", 128 * EPS)
    return c


def make_schedule():
    after = {}

    def put(j, *events):
        after.setdefault(j, []).extend(events)

    put(3, ("m_sumsq",))
    put(9, ("a_sumsq",))
    for c in range(NCH):
        put(16 + 2 * c, ("a_turn", c))
    for g in range(0, NH, 2):
        put(24 + g, ("a_mix", g))
    put(44, ("ba",))
    put(46, ("cumsum",))
    for i in range(4):
        put(49 + i, ("s_score", 2 * i), ("s_score", 2 * i + 1))
    put(53, ("s_rows",))
    put(54, ("s_cols",))
    for i in range(8):
        put(55 + i // 3, ("s_value", i))
    for h in range(MH):
        put(58 + 3 * h, ("p_score", h))
        put(59 + 3 * h, ("p_turn", h))
        put(60 + 3 * h, ("p_value", h))
    out = [("x_sumsq",)]
    for j in range(WO_TILE):
        out.append(("tile", j))
        out += after.get(j, [])
    out += [("conv_s",)] + [("l2", t) for t in range(2 * NH)]
    out += [("sd_bcast",), ("sd_state",), ("sd_ktok",), ("sd_utok",)] + [("sd_outer", h) for h in range(NH)]
    out += [("delta", c) for c in range(NCH)]
    out += [("o_norm", h) for h in range(NH)]
    out += [("m_split",)]
    out += [("tile", j) for j in range(WO_TILE, 2 * NBLK)]
    out += [("f_sumsq",), ("router",), ("h_turn",), ("rank",), ("moe",), ("final",)]
    return out


SCHEDULE = make_schedule()
SIDE = {}
for _e in SCHEDULE:
    _k = {"s_score": ("s_score",), "s_value": ("s_value",)}.get(_e[0], _e)
    if _e[0] in ("x_sumsq", "m_sumsq", "a_sumsq", "a_turn", "a_mix", "ba", "cumsum", "s_score", "s_rows",
                 "s_cols", "s_value", "p_score", "p_turn", "p_value", "sd_bcast", "sd_state", "sd_ktok",
                 "sd_utok", "sd_outer") and _k not in SIDE:
        SIDE[_k] = len(SIDE)

NO_SIDE_MM = (("s_score",), ("s_value",))
SIDE_MM = {_e: 1 + sum(SIDE[_f] < SIDE[_e] and _f not in NO_SIDE_MM for _f in SIDE) for _e in SIDE}
PE_STEPS = (["grow", "brow", "kk", "kq", "turn_k", "turn_v", "turn_u"]
            + [f"{m}{l}" for l in range(6) for m in ("mt", "tx")] + ["wk", "uu", "oo", "ss"])
DVE_STEPS = (["arg", "bs", "mt", "u1", "at", "qg"]
             + [f"{m}{l}" for l in range(6) for m in ("x", "tu")] + ["o", "s"])
ACT_STEPS = ["eg", "dt", "kb", "kd", "vb", "t1", "nw", "u"]


def build_step(nc, a, o):
    ctx = ExitStack()
    with ctx:
        def sem(name):
            return ctx.enter_context(nc.semaphore(name))

        base = (nc.sbuf_base + 63) // 64 * 64
        room = (nc.sbuf_usable_end - 64 - base) // 4
        words = {}
        at = 0
        for name, n in [("FIX", 3520), ("RA", 24 * T), ("M", 8 * T), ("ZG", 8 * T), ("HT", 16 * T),
                        ("CQ", 8 * T), ("MKV", 4096), ("RAW", 4096), ("SPL", 8192)]:
            words[name] = at
            at += n
        assert at <= room, (at, room)
        fix = [0]

        def place(name, shape, region, off=0, dt=F32):
            return nc.alloc_sbuf_tensor_at(name, shape, dt, offset=base + 4 * (words[region] + off))

        def fixed(name, shape, dt=F32):
            n = int(np.prod(shape[1:]))
            n = (n + 7) // 8 * 8
            t = place(name, shape, "FIX", fix[0], dt)
            fix[0] += n
            assert fix[0] <= 3520, fix[0]
            return t

        consts = fixed("consts", [128, NCONST])
        params = fixed("params", [128, NPARAM])
        rstd = fixed("rstd", [128, T])
        ba = fixed("ba", [128, NT, 16])
        gate_g = fixed("gate_g", [128, NT, NH])
        beta = fixed("beta", [128, NT, NH])
        tmp_g = fixed("tmp_g", [128, 2, NT, NH])
        cum_g = fixed("cum_g", [128, NCH, NH])
        dec_end = fixed("dec_end", [128, NCH, NH])
        dec_kd = fixed("dec_kd", [128, NCH, NH])
        dec_kb = fixed("dec_kb", [128, NCH, NH])
        neg_a = fixed("neg_a", [128, NH])
        small = fixed("small", [128, 4, 4])
        s_small = fixed("s_small", [32, 4])
        s_rhs = fixed("s_rhs", [NS, 2, NS, NH])
        s_bc = fixed("s_bc", [128, 2, NS, NH])
        s_qk = fixed("s_qk", [128, NH, NS])
        s_u = fixed("s_u", [128, NH, NS])
        s_tmp = fixed("s_tmp", [128, NH, NS])
        s_eg = fixed("s_eg", [NS, NH])
        n_rounds = fixed("n_rounds", [1, 8], I32)

        def const(name, rows=128):
            x, y = CONST[name]
            return consts[0:rows, x:y]

        def param(name, i=None, n=1):
            x, y = PARAM[name]
            return params[:, x:y] if i is None else params[:, x + i:x + i + n]

        x_in = place("x_in", [128, KD, T], "RA")
        x_sq = place("x_sq", [128, KD, T], "RA", 8 * T)
        av = place("av", [128, KD, T], "RA")
        au = place("au", [128, KD, T], "RA", 8 * T)
        a_sq = place("a_sq", [128, KD, T], "RA", 16 * T)
        av_tok = place("av_tok", [128, NCH, D], "RA", 16 * T)
        prob = place("prob", [128, NCH, NM], "RA")
        prob_t = place("prob_t", [128, 2, SEQ], "RA", 1024)
        kv_ring = place("kv_ring", [128, 4, 2048], "RA", 2048)
        w_ba = place("w_ba", [128, KD, 16], "RA", 10240)
        w_ba_h = place("w_ba_h", [128, KD, 16], "RA", 10368, F32R)
        w_ba_l = place("w_ba_l", [128, KD, 16], "RA", 10496, F32R)
        s_sc = place("s_sc", [128, 64], "RA", 10624)
        s_pr = place("s_pr", [32, NM], "RA", 10688)
        s_prt = place("s_prt", [128, 64], "RA", 10944)
        qkv = place("qkv", [128, 24, T], "RA")
        mem_h = place("mem_h", [128, KD, NM], "M", 0, F32R)
        mem_l = place("mem_l", [128, KD, NM], "M", 2048, F32R)
        mrg = place("mrg", [128, KD, T], "M")
        x1 = place("x1", [128, KD, T], "M")
        ws_t = place("ws_t", [128, NH, CH], "ZG")
        bs_row = place("bs_row", [1, NH, CH], "ZG", 1024)
        zg = place("zg", [128, KD, T], "ZG")
        h2 = place("h2", [128, KD, T], "ZG")
        ht_h = place("ht_h", [128, KD, T], "HT", 0, F32R)
        ht_l = place("ht_l", [128, KD, T], "HT", 8 * T, F32R)
        dl = [[place(f"dl{h}_{n}", [128, 4, 128], "HT", (11 * h + n) * 512) for n in range(11)]
              for h in range(2)]
        h2t_h = place("h2t_h", [TT, NT, D], "HT", 0, F32R)
        h2t_l = place("h2t_l", [TT, NT, D], "HT", NT * D, F32R)
        mem = place("mem", [128, KD, NM], "CQ")
        mem_sq = place("mem_sq", [128, KD, NM], "CQ", 2048)
        qc = place("qc", [128, KD, T], "CQ")
        xpad = [place(f"xpad{i}", [128, 528], "CQ", i * 528) for i in range(2)]
        cacc = [place(f"cacc{i}", [128, T], "CQ", 1056 + i * T) for i in range(2)]
        cvs = place("cvs", [128, 24, 4, NS], "CQ", 2112)
        cvs_sum = place("cvs_sum", [128, 24, NS], "CQ", 2880)
        l2sq = [place(f"l2sq{i}", [128, T], "CQ", i * T) for i in range(4)]
        l2rn = [place(f"l2rn{i}", [128, T], "CQ", (4 + i) * T) for i in range(4)]
        osq = [place(f"osq{i}", [128, T], "HT", (8 + i) * T) for i in range(4)]
        orn = [place(f"orn{i}", [128, T], "HT", (12 + i) * T) for i in range(4)]
        x_res = place("x_res", [128, KD, T], "CQ")
        mk = place("mk", [128, KD, NM], "MKV")
        mv = place("mv", [128, 2, D], "MKV", 2048)
        st = place("st", [128, NH, 128], "MKV")
        ext = place("ext", [128, 24, 4, NS], "MKV", 1024)
        convp = place("convp", [128, 24, 3], "MKV", 1792)
        w_r = place("w_r", [128, KD, NG + NE], "MKV")
        w_r_h = place("w_r_h", [128, KD, NG + NE], "MKV", 288, F32R)
        w_r_l = place("w_r_l", [128, KD, NG + NE], "MKV", 576, F32R)
        raw = [place(f"raw{i}", [128, KD, BLK], "RAW", 2048 * i) for i in range(2)]
        w_h = [place(f"w_h{i}", [128, KD, BLK], "SPL", 4096 * i, F32R) for i in range(2)]
        w_l = [place(f"w_l{i}", [128, KD, BLK], "SPL", 4096 * i + 2048, F32R) for i in range(2)]
        k_tok = place("k_tok", [NS, NH, 128], "RAW")
        u_tok = place("u_tok", [NS, NH, 128], "RAW", 1024)
        u_diag = [place(f"u_diag{i}", [NS, NS, 128], "RAW", 2048 + 1024 * i) for i in range(2)]
        s0 = place("s0", [128, NH, NS, 128], "SPL")
        fsq = place("fsq", [128, KD, T], "RA")
        ew = [(place(f"e{i}_gate", [128, KD, DE], r), place(f"e{i}_up", [128, KD, DE], r, 4096),
               place(f"e{i}_down", [128, DE // 128, D], r, 8192)) for i, r in enumerate(("RA", "RAW"))]
        moe_at = [0]

        def moe_buf(name, shape, dt=F32):
            t = place(name, shape, "MKV", 864 + moe_at[0], dt)
            moe_at[0] += (int(np.prod(shape[1:])) + 7) // 8 * 8
            assert moe_at[0] <= 4096 - 864
            return t

        lg = moe_buf("lg", [TT, NT, NG + NE])
        r8 = moe_buf("r8", [TT, NT, 8, 4])
        ing = moe_buf("ing", [TT, NT, EPG])
        ing2 = moe_buf("ing2", [TT, NT, EPG])
        oh1 = moe_buf("oh1", [TT, NT, EPG])
        oh2 = moe_buf("oh2", [TT, NT, EPG])
        w8 = moe_buf("w8", [TT, NT, EPG])
        prod32 = moe_buf("prod32", [TT, NT, NG, EPG])
        comb = moe_buf("comb", [TT, NT, NE])
        hit = moe_buf("hit", [TT, NT, NE])
        rank = moe_buf("rank", [TT, NT, NE])
        cnt = moe_buf("cnt", [128, NE + 16])
        zoff = [0]

        def moe_z(name, shape, dt=F32):
            t = place(name, shape, "ZG", zoff[0], dt)
            zoff[0] += (int(np.prod(shape[1:])) + 7) // 8 * 8
            assert zoff[0] <= 8 * T
            return t

        sel = [moe_z(f"sel{i}", [TT, NT, CAP], F32R) for i in range(2)]
        sel_w = moe_z("sel_w", [TT, NT, 2 * CAP])
        xt = [moe_buf(f"xt{i}", [128, KD, CAP]) for i in range(2)]
        sg = moe_z("sg", [128, 4, CAP])
        act_t = [moe_z(f"act_t{i}", [128, 4, CAP]) for i in range(2)]
        y_t = moe_z("y_t", [128, KD, 2 * CAP])
        y_tok = place("y_tok", [128, D], "HT", 2 * NT * D)
        sel_t = place("sel_t", [128, NT, TT], "HT", 2 * NT * D + D)

        pp = [ctx.enter_context(nc.psum_tensor(f"pp{i}", [128, 2, 512], F32)) for i in range(4)]
        side = pp[3]
        bank = [[pp[2 * h + i // 2][:, i % 2, :].rearrange("p (u n) -> p u n", u=4) for i in range(4)]
                for h in range(2)]

        const_in = sem("const_in")
        x_loaded, mem_loaded, ws_loaded = sem("x_loaded"), sem("mem_loaded"), sem("ws_loaded")
        raw_loaded = [sem(f"raw_loaded{i}") for i in range(2)]
        hi_ready, lo_ready = sem("w_hi_ready"), sem("w_lo_ready")
        tile_mm = sem("tile_mm")
        psum_free = [sem(f"psum_free{i}") for i in range(3)]
        tile_act = sem("tile_act")
        sq_ready, sqrt_done = sem("sq_ready"), sem("sqrt_done")
        h_norm, h_hi, h_lo = sem("h_norm"), sem("h_hi"), sem("h_lo")
        side_mm, side_free = sem("side_mm"), sem("side_free")
        a_normed, a_sq_ready = sem("a_normed"), sem("a_sq_ready")
        wba_loaded, wba_hi, wba_split = sem("wba_loaded"), sem("wba_hi"), sem("wba_split")
        ws_masked = sem("ws_masked")
        g_step, g_act = sem("g_step"), sem("g_act")
        kv_loaded = [sem(f"kv_loaded{i}") for i in range(4)]
        kv_used = sem("kv_used")
        soft_max, soft_exp, soft_norm = sem("soft_max"), sem("soft_exp"), sem("soft_norm")
        out_mem, out_av, out_conv, out_st, out_y = (sem(n) for n in
                                                    ("out_mem", "out_av", "out_conv", "out_st", "out_y"))
        out_s0 = sem("out_s0")
        ext_loaded, ext_ready = sem("ext_loaded"), sem("ext_ready")
        conv_copy, conv_mul, conv_sum, conv_silu = (sem(n) for n in ("conv_copy", "conv_mul", "conv_sum",
                                                                     "conv_silu"))
        conv_zero, convs_sum, convs_silu, gc_added = (sem(n) for n in ("conv_zero", "convs_sum", "convs_silu",
                                                                       "gc_added"))
        l2_sq, l2_mm, l2_sqrt, l2_done = sem("l2_sq"), sem("l2_mm"), sem("l2_sqrt"), sem("l2_done")
        on_sq, on_mm, on_sqrt, on_done = sem("on_sq"), sem("on_mm"), sem("on_sqrt"), sem("on_done")
        s0_loaded = sem("s0_loaded")
        sd_rhs, sd_u, sd_o, sd_diag, sd_dec, sd_new = (sem(n) for n in ("sd_rhs", "sd_u", "sd_o", "sd_diag",
                                                                       "sd_dec", "sd_new"))
        delta_pe = [sem(f"delta_pe{i}") for i in range(2)]
        delta_dve = [sem(f"delta_dve{i}") for i in range(2)]
        delta_act = [sem(f"delta_act{i}") for i in range(2)]
        st_zero = sem("st_zero")
        xres_loaded, wr_loaded, wr_hi, wr_split = (sem(n) for n in
                                                   ("xres_loaded", "wr_loaded", "wr_hi", "wr_split"))
        x1_ready = sem("x1_ready")
        router_mm, ht_mm, ht_hi, ht_lo = sem("router_mm"), sem("ht_mm"), sem("ht_hi"), sem("ht_lo")
        lg_ready, lg_exp, hit_ready, rank_mm, rounds_set = (sem(n) for n in (
            "lg_ready", "lg_exp", "hit_ready", "rank_mm", "rounds_set"))
        eg_loaded = [sem(f"eg_loaded{i}") for i in range(2)]
        eu_loaded = [sem(f"eu_loaded{i}") for i in range(2)]
        ed_loaded = [sem(f"ed_loaded{i}") for i in range(2)]
        sc_free = sem("sc_free")
        sel_ready, selw_ready, gather_mm, xt_ready = (sem(n) for n in ("sel_ready", "selw_ready",
                                                                       "gather_mm", "xt_ready"))
        gu_mm, silu_done, act_ready, y_mm, y_ready = (sem(n) for n in ("gu_mm", "silu_done", "act_ready",
                                                                       "y_mm", "y_ready"))
        turn_mm, turn_out, sc_mm = (sem(n) for n in ("turn_mm", "turn_out", "sc_mm"))
        moe_zero, fin_mm, fin_sq, fin_done, rank_moved = (sem(n) for n in (
            "moe_zero", "fin_mm", "fin_sq", "fin_done", "rank_moved"))
        dve_chain = sem("dve_chain")
        act_chain = sem("act_chain")

        QKV_DONE = 2 * NBLK
        block = ctx.enter_context(nc.Block())

        def pe_at(hh, c, step):
            return c * len(PE_STEPS) + PE_STEPS.index(step) + 1

        def dve_at(hh, c, step):
            return c * len(DVE_STEPS) + DVE_STEPS.index(step) + 1

        def act_at(hh, c, step):
            return c * len(ACT_STEPS) + ACT_STEPS.index(step) + 1

        def kind(j):
            return BLOCK_KIND[j // 2], j - 2 * FIRST_BLOCK[BLOCK_KIND[j // 2]]

        def out_of_psum(eng, j):
            eng.wait_ge(psum_free[j % 3], j // 3 + 1)

        @block.sync
        def _(sp):
            def load_block(b):
                if b >= 2:
                    sp.wait_ge(lo_ready, b - 1)
                sp.dma_start(raw[b % 2][:], a["w_blk"][b].rearrange("p (k n) -> p k n", k=KD))\
                    .then_inc(raw_loaded[b % 2], 16)

            def load_kv(n):
                if n >= 4:
                    sp.wait_ge(kv_used, n - 3)
                src = a["cache_k"][n] if n < NS else a["cache_v"][n - NS]
                sp.dma_start(kv_ring[:, n % 4, :], src).then_inc(kv_loaded[n % 4], 16)

            def load_expert(used, e, i):
                g, u, d = ew[i]
                sp.wait_ge(gu_mm, used)
                sp.dma_start(g[:], a["w_gate"][bass.ds(e, 1)].rearrange("o p (k n) -> (o p) k n", k=KD))\
                    .then_inc(eg_loaded[i], 16)
                sp.dma_start(u[:], a["w_up"][bass.ds(e, 1)].rearrange("o p (k n) -> (o p) k n", k=KD))\
                    .then_inc(eu_loaded[i], 16)
                sp.wait_ge(y_mm, used)
                sp.dma_start(d[:], a["w_down"][bass.ds(e, 1)].rearrange("o p (k n) -> (o p) k n", k=4))\
                    .then_inc(ed_loaded[i], 16)

            sp.dma_start(consts[:], a["consts"]).then_inc(const_in, 16)
            sp.dma_start(params[:], a["params"]).then_inc(const_in, 16)
            sp.dma_start(x_in[:], a["x_t"].rearrange("p (k n) -> p k n", k=KD)).then_inc(x_loaded, 16)
            sp.dma_start(mem[:], a["mem_t"].rearrange("p (k n) -> p k n", k=KD)).then_inc(mem_loaded, 16)
            load_block(0)
            load_block(1)
            sp.dma_start(ws_t[:], a["ws_t"].rearrange("p (k n) -> p k n", k=NH)).then_inc(ws_loaded, 16)
            sp.dma_start(bs_row[:], a["bs"].rearrange("p (k n) -> p k n", k=NH)).then_inc(ws_loaded, 16)
            for ev in SCHEDULE:
                if ev[0] == "tile":
                    j = ev[1]
                    b = j // 2
                    if j % 2 == 0 and 2 <= b + 2 < WO_BLOCK:
                        load_block(b + 2)
                    if j == 15:
                        sp.wait_ge(a_normed, 8)
                        sp.dma_start(o["av"].rearrange("p (k n) -> p k n", k=KD), av[:, :, SEQ:T])\
                            .then_inc(out_av, 16)
                    if j == 31:
                        for i in range(29, 32):
                            out_of_psum(sp, i)
                        sp.dma_start(o["mk"].rearrange("p (k n) -> p k n", k=KD), mk[:]).then_inc(out_mem, 16)
                        sp.dma_start(o["mv"].rearrange("p (k n) -> p k n", k=2), mv[:]).then_inc(out_mem, 16)
                    if j == 39:
                        for i in range(37, 40):
                            out_of_psum(sp, i)
                        sp.wait_ge(out_av, 16)
                        sp.dma_start(w_ba[:], a["w_ba"].rearrange("p (k n) -> p k n", k=KD))\
                            .then_inc(wba_loaded, 16)
                        for n in range(4):
                            load_kv(n)
                    if j == QKV_TILE - 1:
                        sp.wait_ge(side_free, SIDE[("p_value", MH - 1)] + 1)
                        sp.wait_ge(out_mem, 32)
                        sp.dma_start(ext[:, :, 0:3, :],
                                     a["state_conv"].rearrange("p (t j b) -> p t j b", t=24, j=3))\
                            .then_inc(ext_loaded, 16)
                elif ev[0] in ("s_score", "s_value"):
                    n = ev[1] + (NS if ev[0] == "s_value" else 0)
                    if n + 4 < 2 * NS:
                        load_kv(n + 4)
                elif ev[0] == "conv_s":
                    sp.wait_ge(ext_ready, 24)
                    sp.dma_start(o["conv_s"].rearrange("p (t j b) -> p t j b", t=24, j=3), ext[:, :, 1:4, :])\
                        .then_inc(out_conv, 16)
                    sp.dma_start(o["conv_p"].rearrange("p (t j) -> p t j", t=24), convp[:]).then_inc(out_conv, 16)
                    sp.wait_ge(tile_mm, WO_TILE)
                    sp.dma_start(s0[:], a["state_gdn"].rearrange("p (h b n) -> p h b n", h=NH, b=NS))\
                        .then_inc(s0_loaded, 16)
                elif ev == ("sd_outer", NH - 1):
                    sp.wait_ge(sd_new, NH)
                    sp.dma_start(o["gdn_s"].rearrange("p (h b n) -> p h b n", h=NH, b=NS), s0[:])\
                        .then_inc(out_s0, 16)
                    load_block(WO_BLOCK)
                    load_block(WO_BLOCK + 1)
                elif ev[0] == "delta" and ev[1] == NCH - 1:
                    for hh in range(2):
                        sp.wait_ge(delta_dve[hh], dve_at(hh, NCH - 1, "s"))
                        sp.wait_ge(delta_pe[hh], pe_at(hh, NCH - 1, "ss"))
                    sp.dma_start(o["gdn_p"].rearrange("p (h n) -> p h n", h=NH), st[:]).then_inc(out_st, 16)
                    sp.dma_start(x_res[:], a["x_t"].rearrange("p (k n) -> p k n", k=KD))\
                        .then_inc(xres_loaded, 16)
                    sp.wait_ge(out_st, 16)
                    sp.dma_start(w_r[:], a["w_router"].rearrange("p (k n) -> p k n", k=KD))\
                        .then_inc(wr_loaded, 16)
            load_block(WO_BLOCK + 2)
            load_block(WO_BLOCK + 3)
            sp.wait_ge(on_done, 8)
            sp.wait_ge(out_conv, 16 * 2)
            g, u, d = ew[0]
            sp.dma_start(g[:], a["w_gate"][0].rearrange("p (k n) -> p k n", k=KD)).then_inc(eg_loaded[0], 16)
            sp.dma_start(u[:], a["w_up"][0].rearrange("p (k n) -> p k n", k=KD)).then_inc(eu_loaded[0], 16)
            sp.dma_start(d[:], a["w_down"][0].rearrange("p (k n) -> p k n", k=4)).then_inc(ed_loaded[0], 16)
            sp.wait_ge(tile_mm, 2 * NBLK)
            g, u, d = ew[1]
            sp.dma_start(g[:], a["w_gate"][1].rearrange("p (k n) -> p k n", k=KD)).then_inc(eg_loaded[1], 16)
            sp.dma_start(u[:], a["w_up"][1].rearrange("p (k n) -> p k n", k=KD)).then_inc(eu_loaded[1], 16)
            sp.dma_start(d[:], a["w_down"][1].rearrange("p (k n) -> p k n", k=4)).then_inc(ed_loaded[1], 16)
            with sp.Fori(1, NE // 2) as p:
                for i in range(2):
                    load_expert(p * 2 + i - 1, p * 2 + i, i)
            sp.wait_ge(rounds_set, 1)
            rounds = sp.value_load(n_rounds[0:1, 0:1], min_val=1, max_val=9)
            with sp.If(rounds > 1):
                with sp.Fori(1, rounds) as r:
                    with sp.Fori(0, NE // 2) as p:
                        for i in range(2):
                            load_expert(r * NE + p * 2 + i - 1, p * 2 + i, i)
            for k in range(KD):
                sp.wait_ge(fin_done, k + 1)
                sp.dma_start(o["y"][:, k * T:(k + 1) * T], x1[:, k, :]).then_inc(out_y, 16)
            sp.wait_ge(out_y, 16 * KD)
            sp.wait_ge(out_mem, 32)
            sp.wait_ge(out_av, 16)
            sp.wait_ge(out_st, 16)
            sp.wait_ge(out_conv, 32)
            sp.wait_ge(out_s0, 16)

        @block.tensor
        def _(pe):
            mm = nc.tensor.matmul

            def begin(ev):
                n = SIDE[ev]
                if n:
                    pe.wait_ge(side_free, n)

            def sum_rows(out, src, ready, base_count, n, start=0):
                for k in range(KD):
                    pe.wait_ge(ready, base_count + k + 1)
                    for hf in range(2):
                        w = n // 2
                        last = mm(out[:, hf, 0:w], const("ones"), src[:, k, hf * w:(hf + 1) * w],
                                  start=(k == 0), stop=(k == KD - 1))
                return last

            def tile(j):
                b, i = j // 2, j % 2
                what, _t = kind(j)
                s = b % 2
                ps = pp[j % 3]
                if i == 0:
                    pe.wait_ge(lo_ready, b + 1)
                if j >= WO_TILE + 3:
                    pe.wait_ge(x1_ready, j - WO_TILE - 2)
                elif j >= 3 and j < WO_TILE:
                    pe.wait_ge(psum_free[j % 3], j // 3)
                need = {"mk": 16, "mv": 16, "wo": 24}.get(what, 8)
                pe.wait_ge(h_lo, need)
                if what == "mv":
                    ms = slice(i * 128, (i + 1) * 128)
                    n = 0
                    for k in range(KD):
                        for m_, w_ in ((mem_h, w_h), (mem_h, w_l), (mem_l, w_h)):
                            last = mm(ps[:, 0, 0:BLK], m_[:, k, ms], w_[s][:, k, :],
                                      start=(n == 0), stop=(n == 3 * KD - 1))
                            n += 1
                    last.then_inc(tile_mm, 1)
                    return
                cs = slice(i * 128, (i + 1) * 128)
                if what == "mk":
                    moving = [(ps[:, 0, 0:NM], slice(0, NM))]
                    xh, xl = mem_h, mem_l
                else:
                    moving = [(ps[:, hf, 0:HALF], slice(hf * HALF, (hf + 1) * HALF)) for hf in range(2)]
                    xh, xl = ht_h, ht_l
                for k in range(KD):
                    for q, (w_, x_) in enumerate(((w_h, xh), (w_h, xl), (w_l, xh))):
                        for dst, ts in moving:
                            last = mm(dst, w_[s][:, k, cs], x_[:, k, ts],
                                      start=(k == 0 and q == 0), stop=(k == KD - 1 and q == 2))
                last.then_inc(tile_mm, 1)

            def delta(c):
                cs = slice(c * CH, (c + 1) * CH)

                def each(step, fn):
                    for hh in range(2):
                        last = fn(hh)
                        last.then_inc(delta_pe[hh], 1)

                def wd(hh, step, cc=c):
                    pe.wait_ge(delta_dve[hh], dve_at(hh, cc, step))

                def wa(hh, step, cc=c):
                    pe.wait_ge(delta_act[hh], act_at(hh, cc, step))

                def four(hh, out, lhs, rhs):
                    for u in range(4):
                        last = mm(out[:, u, :], lhs(4 * hh + u, u), rhs(4 * hh + u, u), start=True, stop=True)
                    return last

                def q_(h):
                    return qkv[:, h, cs]

                def k_(h):
                    return qkv[:, NH + h, cs]

                def v_(h):
                    return qkv[:, 2 * NH + h, cs]

                def turn(hh, out, src):
                    for u in range(4):
                        last = nc.tensor.transpose(out[:, u, :], src(4 * hh + u, u), const("ident"))
                    return last

                def grow(hh):
                    if c:
                        wa(hh, "u", c - 1)
                    return four(hh, bank[hh][0], lambda h, u: gate_g[:, c, h:h + 1].to_broadcast([128, 128]),
                                lambda h, u: const("triu"))

                def brow(hh):
                    if c:
                        wd(hh, "o", c - 1)
                    return four(hh, bank[hh][1], lambda h, u: beta[:, c, h:h + 1].to_broadcast([128, 128]),
                                lambda h, u: const("ident"))

                def kk(hh):
                    if c:
                        wd(hh, "s", c - 1)
                    return four(hh, bank[hh][2], lambda h, u: k_(h), lambda h, u: k_(h))

                def kq(hh):
                    if c:
                        wa(hh, "nw", c - 1)
                    return four(hh, bank[hh][3], lambda h, u: k_(h), lambda h, u: q_(h))

                def turn_k(hh):
                    wd(hh, "arg")
                    wa(hh, "eg")
                    return turn(hh, bank[hh][0], lambda h, u: k_(h))

                def turn_v(hh):
                    wd(hh, "bs")
                    return turn(hh, bank[hh][1], lambda h, u: v_(h))

                def turn_u(hh):
                    wd(hh, "u1")
                    return turn(hh, bank[hh][2], lambda h, u: dl[hh][3][:, u, :])

                if c == 0:
                    pe.wait_ge(side_free, len(SIDE))
                    pe.wait_ge(l2_sqrt, 2 * NH)
                each("grow", grow)
                each("brow", brow)
                each("kk", kk)
                each("kq", kq)
                each("turn_k", turn_k)
                each("turn_v", turn_v)
                each("turn_u", turn_u)
                for l in range(6):
                    def m_t(hh):
                        if l == 0:
                            wa(hh, "t1")
                        else:
                            wd(hh, f"tu{l - 1}")
                        return four(hh, bank[hh][2], lambda h, u: dl[hh][1][:, u, :],
                                    lambda h, u: dl[hh][2][:, u, :])

                    def t_x(hh):
                        wd(hh, f"x{l}")
                        if l == 0:
                            wd(hh, "at")
                        four(hh, bank[hh][3], lambda h, u: dl[hh][3][:, u, :],
                             lambda h, u: dl[hh][4][:, u, :])
                        return four(hh, bank[hh][2], lambda h, u: dl[hh][4][:, u, :],
                                    lambda h, u: dl[hh][3][:, u, :])

                    each(f"mt{l}", m_t)
                    each(f"tx{l}", t_x)

                def wk(hh):
                    wd(hh, "tu5")
                    wa(hh, "vb")
                    return four(hh, bank[hh][3], lambda h, u: dl[hh][5][:, u, :],
                                lambda h, u: dl[hh][3][:, u, :])

                def uu(hh):
                    wa(hh, "nw")
                    if c:
                        wd(hh, "s", c - 1)
                    else:
                        pe.wait_ge(st_zero, 1)
                    for u in range(4):
                        mm(bank[hh][0][:, u, :], dl[hh][3][:, u, :], dl[hh][7][:, u, :], start=True, stop=False)
                        last = mm(bank[hh][0][:, u, :], dl[hh][9][:, u, :], st[:, 4 * hh + u, :],
                                  start=False, stop=True)
                    return last

                def oo(hh):
                    wa(hh, "u")
                    wd(hh, "qg")
                    for u in range(4):
                        mm(bank[hh][1][:, u, :], st[:, 4 * hh + u, :], dl[hh][8][:, u, :], start=True, stop=False)
                        last = mm(bank[hh][1][:, u, :], dl[hh][10][:, u, :], dl[hh][0][:, u, :],
                                  start=False, stop=True)
                    return last

                def ss(hh):
                    return four(hh, bank[hh][2], lambda h, u: dl[hh][6][:, u, :],
                                lambda h, u: dl[hh][10][:, u, :])

                each("wk", wk)
                each("uu", uu)
                each("oo", oo)
                each("ss", ss)

            def gather(j, pair, e0):
                n = pair * 2 + j
                pe.wait_ge(sel_ready, n + 1)
                pe.wait_ge(xt_ready, n + 1)
                xb = pp[0][:, 0, :].rearrange("p (k n) -> p k n", k=KD)
                for k in range(KD):
                    for t in range(NT):
                        for q, src in enumerate((h2t_h, h2t_l)):
                            last = mm(xb[:, k, :], src[:, t, k * 128:(k + 1) * 128], sel[j][:, t, :],
                                      start=(t == 0 and q == 0), stop=(t == NT - 1 and q == 1))
                last.then_inc(gather_mm, 1)

            def gate_up(j, pair):
                n = pair * 2 + j
                pe.wait_ge(xt_ready, n + 2)
                pe.wait_ge(act_ready, n + 1)
                g, u, _ = ew[j]
                gb = pp[0][:, 1, :].rearrange("p (a f n) -> p a f n", a=2, f=4)
                for which, (w, loaded) in enumerate(((g, eg_loaded), (u, eu_loaded))):
                    pe.wait_ge(loaded[j], (pair + 1) * 16)
                    for f in range(4):
                        for k in range(KD):
                            last = mm(gb[:, which, f, :], w[:, k, f * 128:(f + 1) * 128], xt[j][:, k, :],
                                      start=(k == 0), stop=(k == KD - 1))
                last.then_inc(gu_mm, 1)

            def down(j, pair):
                n = pair * 2 + j
                pe.wait_ge(act_ready, n + 2)
                pe.wait_ge(y_ready, n + 1)
                pe.wait_ge(ed_loaded[j], (pair + 1) * 16)
                yb = pp[1][:, 0, :].rearrange("p (k n) -> p k n", k=KD)
                for k in range(KD):
                    for f in range(4):
                        last = mm(yb[:, k, :], ew[j][2][:, f, k * 128:(k + 1) * 128], act_t[j][:, f, :],
                                  start=(f == 0), stop=(f == 3))
                last.then_inc(y_mm, 1)

            def scatter(pair, dc0, dc1):
                pe.wait_ge(turn_out, pair * 4 + 1)
                for dc in range(dc0, dc1):
                    pe.wait_ge(sc_free, pair * KD + dc + 1)
                    for hf in range(2):
                        last = mm(pp[2 + dc % 2][:, hf, 0:HALF], y_tok[:, dc * 128:(dc + 1) * 128],
                                  sel_t[:].rearrange("p t n -> p (t n)")[:, hf * HALF:(hf + 1) * HALF],
                                  start=True, stop=True)
                    last.then_inc(sc_mm, 1)

            def turns(pair):
                tb = pp[1][:, 1, :]
                pe.wait_ge(selw_ready, pair * 2 + 2)
                for i, ts in enumerate((range(0, 4), range(4, 5))):
                    pe.wait_ge(turn_out, pair * 4 + i + 1)
                    for t in ts:
                        last = nc.tensor.transpose(tb[:, (t % 4) * TT:(t % 4 + 1) * TT], sel_w[:, t, :],
                                                   const("ident")[0:TT, 0:TT])
                    last.then_inc(turn_mm, 1)
                pe.wait_ge(y_ready, pair * 2 + 3)
                for i in range(2):
                    pe.wait_ge(turn_out, pair * 4 + 3 + i)
                    for k in range(4 * i, 4 * i + 4):
                        last = nc.tensor.transpose(tb[:, (k % 4) * 128:(k % 4 + 1) * 128], y_t[:, k, :],
                                                   const("ident"))
                    last.then_inc(turn_mm, 1)

            pe.wait_ge(const_in, 32)
            for ev in SCHEDULE:
                e = ev[0]
                if e == "tile":
                    tile(ev[1])
                elif e == "x_sumsq":
                    begin(ev)
                    sum_rows(side, x_sq, sq_ready, 0, T).then_inc(side_mm, 1)
                elif e == "m_sumsq":
                    begin(ev)
                    sum_rows(side, mem_sq, sq_ready, 8, NM).then_inc(side_mm, 1)
                elif e == "a_sumsq":
                    begin(ev)
                    sum_rows(side, a_sq, a_sq_ready, 0, T).then_inc(side_mm, 1)
                elif e == "a_turn":
                    begin(ev)
                    pe.wait_ge(a_normed, 8)
                    c = ev[1]
                    for g in range(NH):
                        last = nc.tensor.transpose(side[:, g // 4, (g % 4) * 128:(g % 4 + 1) * 128],
                                                   av[:, g, c * CH:(c + 1) * CH], const("ident"))
                    last.then_inc(side_mm, 1)
                elif e == "a_mix":
                    begin(ev)
                    pe.wait_ge(ws_masked, 1)
                    pe.wait_ge(side_free, SIDE[("a_turn", NCH - 1)] + 1)
                    for i in range(2):
                        g = ev[1] + i
                        ob = side[:, i, :].rearrange("p (c n) -> p c n", c=NCH)
                        mm(ob, const("ones", 1), bs_row[0:1, g:g + 1, :].to_broadcast([1, NCH, CH]),
                           start=True, stop=False)
                        for c in range(NCH):
                            last = mm(ob[:, c, :], av_tok[:, c, g * 128:(g + 1) * 128], ws_t[:, g, :],
                                      start=False, stop=(c == NCH - 1))
                    last.then_inc(side_mm, 1)
                elif e == "ba":
                    begin(ev)
                    pe.wait_ge(wba_split, 1)
                    for t in range(NT):
                        ts = slice(t * CH, min((t + 1) * CH, T))
                        rows = ts.stop - ts.start
                        n = 0
                        for k in range(KD):
                            for x_, w_ in ((ht_h, w_ba_h), (ht_h, w_ba_l), (ht_l, w_ba_h)):
                                last = mm(side[0:rows, 0, t * 16:(t + 1) * 16], x_[:, k, ts], w_[:, k, :],
                                          start=(n == 0), stop=(n == 3 * KD - 1))
                                n += 1
                    last.then_inc(side_mm, 1)
                elif e == "cumsum":
                    begin(ev)
                    pe.wait_ge(g_step, 3)
                    gp = gate_g[:, 0:NCH, :].rearrange("p c h -> p (c h)")
                    mm(side[:, 0, 0:32], const("triu"), gp, start=True, stop=True)
                    mm(side[:, 0, 32:64], const("ones"), gp, start=True, stop=True).then_inc(side_mm, 1)
                elif e == "s_score":
                    b = ev[1]
                    if b == 0:
                        begin(("s_score",))
                        [out_of_psum(pe, i) for i in range(45, 48)]
                    pe.wait_ge(kv_loaded[b % 4], 16 * (b // 4 + 1))
                    for h in range(MH):
                        for mt in range(2):
                            for dc in range(2):
                                kt = kv_ring[:, b % 4, :].rearrange("p (k n) -> p k n", k=KD)
                                col = mt * 32 + h * NS + b
                                last = mm(side[:, 0, col:col + 1],
                                          kt[:, 2 * h + dc, mt * 128:(mt + 1) * 128],
                                          qc[:, 2 * h + dc, SEQ + b:SEQ + b + 1], start=(dc == 0), stop=(dc == 1))
                    last.then_inc(kv_used, 1)
                elif e == "s_rows":
                    begin(ev)
                    for mt in range(2):
                        last = nc.tensor.transpose(side[0:32, 1, mt * 128:(mt + 1) * 128],
                                                   s_sc[:, mt * 32:(mt + 1) * 32], const("ident"))
                    last.then_inc(side_mm, 1)
                elif e == "s_cols":
                    begin(ev)
                    pe.wait_ge(soft_norm, 1)
                    for mt in range(2):
                        last = nc.tensor.transpose(side[:, 0, mt * 32:(mt + 1) * 32],
                                                   s_pr[:, mt * 128:(mt + 1) * 128], const("ident", 32)[:, 0:32])
                    last.then_inc(side_mm, 1)
                elif e == "s_value":
                    b = ev[1]
                    if b == 0:
                        begin(("s_value",))
                    pe.wait_ge(kv_loaded[b % 4], 16 * ((b + NS) // 4 + 1))
                    vt = kv_ring[:, b % 4, :].rearrange("p (m n) -> p m n", m=2)
                    for k in range(KD):
                        for mt in range(2):
                            col = mt * 32 + (k // 2) * NS + b
                            last = mm(side[:, 1, k * NS + b:k * NS + b + 1], vt[:, mt, k * 128:(k + 1) * 128],
                                      s_prt[:, col:col + 1], start=(mt == 0), stop=(mt == 1))
                    last.then_inc(kv_used, 1)
                elif e == "p_score":
                    begin(ev)
                    h = ev[1]
                    for c in range(NCH):
                        dst = side[:, c // 2, (c % 2) * NM:(c % 2 + 1) * NM]
                        for dc in range(2):
                            last = mm(dst, qc[:, 2 * h + dc, c * CH:(c + 1) * CH], mk[:, 2 * h + dc, :],
                                      start=(dc == 0), stop=(dc == 1))
                    last.then_inc(side_mm, 1)
                elif e == "p_turn":
                    begin(ev)
                    h = ev[1]
                    pe.wait_ge(soft_norm, h + 2)
                    for mt in range(2):
                        for c in range(NCH):
                            last = nc.tensor.transpose(side[:, mt, c * CH:(c + 1) * CH],
                                                       prob[:, c, mt * 128:(mt + 1) * 128], const("ident"))
                    last.then_inc(side_mm, 1)
                elif e == "p_value":
                    begin(ev)
                    h = ev[1]
                    for dc in range(2):
                        for mt in range(2):
                            cc = (2 * h + dc) * 128
                            last = mm(side[:, dc, :], mv[:, mt, cc:cc + 128], prob_t[:, mt, :],
                                      start=(mt == 0), stop=(mt == 1))
                    last.then_inc(side_mm, 1)
                elif e == "l2":
                    t = ev[1]
                    if t < 3:
                        pe.wait_ge(psum_free[t], WO_TILE // 3)
                    if t == 3:
                        pe.wait_ge(side_free, SIDE[("p_value", MH - 1)] + 1)
                    if t >= 4:
                        pe.wait_ge(l2_sqrt, t - 3)
                    pe.wait_ge(l2_sq, t + 1)
                    for hf in range(2):
                        last = mm(pp[t % 4][:, hf, 0:HALF], const("ones"),
                                  l2sq[t % 4][:, hf * HALF:(hf + 1) * HALF], start=True, stop=True)
                    last.then_inc(l2_mm, 1)
                elif e == "sd_bcast":
                    begin(ev)
                    pe.wait_ge(l2_sqrt, 16)
                    pe.wait_ge(sd_rhs, 2)
                    mm(side[:, 0, 0:2 * NS * NH], const("ones", NS), s_rhs[:].rearrange("b a c h -> b (a c h)"),
                       start=True, stop=True)
                    mm(side[:, 1, 0:NS * NH], const("ones"), s_qk[:].rearrange("p h b -> p (h b)"),
                       start=True, stop=True).then_inc(side_mm, 1)
                elif e == "sd_state":
                    begin(ev)
                    pe.wait_ge(s0_loaded, 16)
                    for h in range(NH):
                        for b in range(NS):
                            c0 = (h * NS + b) * 2
                            last = mm(side[:, 0, c0:c0 + 2], s0[:, h, b, :],
                                      qkv[:, h:h + NH + 1:NH, SEQ + b], start=True, stop=True)
                    last.then_inc(side_mm, 1)
                elif e in ("sd_ktok", "sd_utok"):
                    begin(ev)
                    if e == "sd_utok":
                        pe.wait_ge(sd_u, 1)
                    for h in range(NH):
                        src = s_u[:, h, :] if e == "sd_utok" else qkv[:, NH + h, SEQ:T]
                        last = nc.tensor.transpose(side[0:NS, h // 4, (h % 4) * 128:(h % 4 + 1) * 128], src,
                                                   const("ident"))
                    last.then_inc(side_mm, 1)
                elif e == "sd_outer":
                    begin(ev)
                    h = ev[1]
                    pe.wait_ge(sd_diag, h + 1)
                    pe.wait_ge(side_free, SIDE[("sd_ktok",)] + 1)
                    for i in range(2):
                        last = mm(side[:, i, :], k_tok[:, h, :], u_diag[h % 2][:, 4 * i:4 * i + 4, :],
                                  start=True, stop=True)
                    last.then_inc(side_mm, 1)
                elif e == "delta":
                    delta(ev[1])
                elif e == "o_norm":
                    h = ev[1]
                    if h < 4:
                        for hh in range(2):
                            pe.wait_ge(delta_dve[hh], dve_at(hh, NCH - 1, "s"))
                    else:
                        pe.wait_ge(on_sqrt, h - 3)
                    pe.wait_ge(on_sq, h + 1)
                    for hf in range(2):
                        last = mm(pp[h % 4][:, hf, 0:HALF], const("ones"),
                                  osq[h % 4][:, hf * HALF:(hf + 1) * HALF], start=True, stop=True)
                    last.then_inc(on_mm, 1)
                elif e == "f_sumsq":
                    pe.wait_ge(x1_ready, 8)
                    sum_rows(pp[3], h2, sq_ready, 16, T).then_inc(fin_mm, 1)
                elif e == "router":
                    pe.wait_ge(wr_split, 1)
                    pe.wait_ge(h_lo, 32)
                    for t in range(NT):
                        n = 0
                        ts = slice(t * TT, (t + 1) * TT)
                        for k in range(KD):
                            for x_, w_ in ((ht_h, w_r_h), (ht_h, w_r_l), (ht_l, w_r_h)):
                                last = mm(pp[0][0:TT, 0, t * 36:(t + 1) * 36], x_[:, k, ts], w_[:, k, :],
                                          start=(n == 0), stop=(n == 3 * KD - 1))
                                n += 1
                    last.then_inc(router_mm, 1)
                elif e == "h_turn":
                    for t in range(NT):
                        if t >= 3:
                            pe.wait_ge(ht_lo, t - 2)
                        for k in range(KD):
                            last = nc.tensor.transpose(
                                pp[1 + t % 3][0:TT, k // 4, (k % 4) * 128:(k % 4 + 1) * 128],
                                h2[:, k, t * TT:(t + 1) * TT], const("ident"))
                        last.then_inc(ht_mm, 1)
                elif e == "rank":
                    pe.wait_ge(hit_ready, 1)
                    for t in range(NT):
                        for s in range(t + 1):
                            left = const("strict", TT)[:, 0:TT] if s == t else const("ones", TT)[:, 0:TT]
                            mm(pp[0][0:TT, 1, t * NE:(t + 1) * NE], left, hit[:, s, :],
                               start=(s == 0), stop=(s == t))
                    for s in range(NT):
                        last = mm(pp[0][:, 1, 160:160 + NE], const("ones", TT), hit[:, s, :],
                                  start=(s == 0), stop=(s == NT - 1))
                    last.then_inc(rank_mm, 1)
                elif e == "moe":
                    pe.wait_ge(moe_zero, 1)
                    pe.wait_ge(ht_lo, NT)
                    pe.wait_ge(rounds_set, 1)
                    pe.sem_inc(gather_mm, 1)
                    pe.sem_inc(turn_mm, 1)
                    rounds = pe.value_load(n_rounds[0:1, 0:1], min_val=1, max_val=9)
                    with pe.Fori(0, rounds) as r:
                        with pe.Fori(0, NE // 2) as p:
                            pair = r * (NE // 2) + p
                            gather(0, pair, None)
                            gate_up(0, pair)
                            scatter(pair, 0, 4)
                            down(0, pair)
                            gather(1, pair, None)
                            gate_up(1, pair)
                            scatter(pair, 4, 8)
                            down(1, pair)
                            turns(pair)
                    scatter(rounds * (NE // 2), 0, 8)
                elif e == "final":
                    sum_rows(pp[0], fsq, fin_sq, 0, T).then_inc(fin_mm, 1)

        @block.scalar
        def _(act):
            fn = nc.scalar.activation
            chain = [0]

            def link(ins):
                chain[0] += 1
                ins.then_inc(act_chain, 1)
                act.wait_ge(act_chain, chain[0])

            def split_hi(b):
                act.wait_ge(raw_loaded[b % 2], 16 * (b // 2 + 1))
                if b >= 2:
                    act.wait_ge(tile_mm, 2 * (b - 1))
                fn(w_h[b % 2][:], raw[b % 2][:], ACT.Copy).then_inc(hi_ready, 1)

            def squares(dst, src, done):
                for k in range(KD):
                    fn(dst[:, k, :], src[:, k, :], ACT.Square).then_inc(done, 1)

            def root_mean(ps, n, w):
                dst = rstd[:, 0:w].rearrange("p (a n) -> p a n", a=2)
                return fn(dst, ps[:, :, 0:w // 2], ACT.Sqrt, bias=const("eps"), scale=1.0 / n)

            def tile(j):
                what, t = kind(j)
                b = j // 2
                if j % 2 == 0 and b + 1 < (WO_BLOCK if b < WO_BLOCK else NBLK) and b + 1 != WO_BLOCK + 1:
                    split_hi(b + 1)
                ps = pp[j % 3][:, :, 0:HALF]

                def whole(x):
                    return x.rearrange("p (a n) -> p a n", a=2)

                if what in ("av", "au"):
                    act.wait_ge(tile_mm, j + 1)
                    dst = av if what == "av" else au
                    fn(whole(dst[:, t, :]), ps, ACT.Gelu_apprx_tanh).then_inc(psum_free[j % 3], 1)
                elif what in ("ga", "gc"):
                    act.wait_ge(tile_mm, j + 1)
                    fn(ps, ps, ACT.Sigmoid, bias=param("b_gate", t + (16 if what == "gc" else 0)))\
                        .then_inc(tile_act, 1)
                elif what == "gb":
                    act.wait_ge(tile_mm, j + 1)
                    fn(whole(zg[:, t, :]), ps, ACT.Sigmoid, bias=param("b_gate", t + 8))\
                        .then_inc(psum_free[j % 3], 1)
                elif what == "z":
                    act.wait_ge(tile_mm, j + 1)
                    fn(ps, ps, ACT.Silu).then_inc(tile_act, 1)
                elif what == "qkv":
                    act.wait_ge(tile_mm, j + 1)
                    act.wait_ge(conv_zero, 1)
                    if t == 0:
                        act.wait_ge(gc_added, 8)
                    if t >= 2:
                        act.wait_ge(conv_sum, t - 1)
                        act.wait_ge(ext_ready, t - 1)
                    fn(whole(xpad[t % 2][:, 3:3 + T]), ps, ACT.Copy).then_inc(conv_copy, 1)
                    if t >= 2:
                        act.wait_ge(conv_silu, t - 1)
                    fn(whole(cacc[t % 2][:, :]), ps, ACT.Copy, scale=param("w_conv", 4 * t + 3))\
                        .then_inc(psum_free[j % 3], 1)
                    if t >= 1:
                        act.wait_ge(conv_sum, t)
                        fn(qkv[:, t - 1, 0:SEQ], cacc[(t - 1) % 2][:, 0:SEQ], ACT.Silu).then_inc(conv_silu, 1)

            act.wait_ge(const_in, 32)
            for ev in SCHEDULE:
                e = ev[0]
                if e == "tile":
                    tile(ev[1])
                elif e == "x_sumsq":
                    act.wait_ge(x_loaded, 16)
                    squares(x_sq, x_in, sq_ready)
                    split_hi(0)
                    act.wait_ge(side_mm, SIDE_MM[ev])
                    root_mean(side, D, T).then_inc(side_free, 1)
                    for k in range(KD):
                        act.wait_ge(h_norm, k + 1)
                        fn(ht_h[:, k, :], x_in[:, k, :], ACT.Copy).then_inc(h_hi, 1)
                elif e == "m_sumsq":
                    act.wait_ge(mem_loaded, 16)
                    squares(mem_sq, mem, sq_ready)
                    act.wait_ge(side_mm, SIDE_MM[ev])
                    root_mean(side, D, NM).then_inc(side_free, 1)
                    for k in range(KD):
                        act.wait_ge(h_norm, 8 + k + 1)
                        fn(mem_h[:, k, :], mem[:, k, :], ACT.Copy).then_inc(h_hi, 1)
                elif e == "a_sumsq":
                    act.wait_ge(side_mm, SIDE_MM[ev])
                    root_mean(side, D, T).then_inc(side_free, 1)
                elif e == "a_turn":
                    act.wait_ge(side_mm, SIDE_MM[ev])
                    fn(av_tok[:, ev[1], :].rearrange("p (a n) -> p a n", a=2), side[:], ACT.Copy)\
                        .then_inc(side_free, 1)
                elif e == "ba":
                    act.wait_ge(wba_loaded, 16)
                    fn(w_ba_h[:], w_ba[:], ACT.Copy).then_inc(wba_hi, 1)
                    link(fn(neg_a[:], param("a_log"), ACT.Exp))
                    act.wait_ge(g_step, 1)
                    for rows, ts in ((128, slice(0, 4)), (NS, slice(4, 5))):
                        x, y = tmp_g[0:rows, 0, ts, :], tmp_g[0:rows, 1, ts, :]
                        link(fn(y, x, ACT.Abs))
                        link(fn(y, y, ACT.Exp, scale=-1.0))
                        fn(y, y, ACT.Ln, bias=1.0).then_inc(g_act, 1)
                    for rows, ts in ((128, slice(0, 4)), (NS, slice(4, 5))):
                        fn(beta[0:rows, ts, :], ba[0:rows, ts, 0:NH], ACT.Sigmoid).then_inc(g_act, 1)
                elif e == "cumsum":
                    act.wait_ge(g_step, 5)
                    fn(dec_end[:].rearrange("p c h -> p (c h)"), side[:, 0, 32:64], ACT.Exp).then_inc(g_act, 1)
                    fn(dec_kb[:], cum_g[:], ACT.Exp).then_inc(g_act, 1)
                    fn(dec_kd[:], dec_kd[:], ACT.Exp).then_inc(g_act, 1)
                    fn(s_eg[:], gate_g[0:NS, 4, :], ACT.Exp).then_inc(g_act, 1)
                elif e == "s_rows":
                    act.wait_ge(soft_max, 1)
                    fn(s_pr[:], side[0:32, 1, 0:NM], ACT.Exp, bias=s_small[:, 1:2], scale=1.0 / 16,
                       accum_out=s_small[:, 2:3]).then_inc(soft_exp, 1)
                elif e == "p_score":
                    h = ev[1]
                    act.wait_ge(soft_max, h + 2)
                    sp_ = side[:].rearrange("p a (c m) -> p (a c) m", c=2)
                    for c in range(NCH):
                        fn(prob[:, c, :], sp_[:, c, :], ACT.Exp, bias=small[:, 1, c:c + 1], scale=1.0 / 16,
                           accum_out=small[:, 2, c:c + 1]).then_inc(soft_exp, 1)
                elif e == "p_turn":
                    act.wait_ge(side_mm, SIDE_MM[ev])
                    fn(prob_t[:], side[:], ACT.Copy).then_inc(side_free, 1)
                elif e == "conv_s":
                    act.wait_ge(conv_sum, 24)
                    fn(qkv[:, 23, 0:SEQ], cacc[1][:, 0:SEQ], ACT.Silu).then_inc(conv_silu, 1)
                    act.wait_ge(convs_sum, 1)
                    fn(qkv[:, :, SEQ:T], cvs_sum[:], ACT.Silu).then_inc(convs_silu, 1)
                elif e == "l2":
                    t = ev[1]

                    def l2_square(t):
                        if t >= 4:
                            act.wait_ge(l2_mm, t - 3)
                        fn(l2sq[t % 4][:], qkv[:, t, :], ACT.Square).then_inc(l2_sq, 1)

                    if t == 0:
                        act.wait_ge(conv_silu, 24)
                        act.wait_ge(convs_silu, 1)
                        l2_square(0)
                        l2_square(1)
                    if t + 2 < 2 * NH:
                        l2_square(t + 2)
                    act.wait_ge(l2_mm, t + 1)
                    if t >= 4:
                        act.wait_ge(l2_done, t - 3)
                    is_q = t < NH
                    fn(l2rn[t % 4][:].rearrange("p (a n) -> p a n", a=2), pp[t % 4][:, :, 0:HALF], ACT.Sqrt,
                       bias=const("eps128" if is_q else "eps"), scale=128.0 if is_q else 1.0)\
                        .then_inc(l2_sqrt, 1)
                elif e == "sd_ktok":
                    act.wait_ge(side_mm, SIDE_MM[ev])
                    fn(k_tok[:].rearrange("p h n -> p (h n)").rearrange("p (a n) -> p a n", a=2), side[0:NS],
                       ACT.Copy).then_inc(side_free, 1)
                elif e == "delta":
                    c = ev[1]

                    def wp(hh, step, cc=c):
                        act.wait_ge(delta_pe[hh], pe_at(hh, cc, step))

                    for hh in range(2):
                        act.wait_ge(delta_dve[hh], dve_at(hh, c, "arg"))
                        fn(dl[hh][8][:], bank[hh][0], ACT.Exp).then_inc(delta_act[hh], 1)
                    for hh in range(2):
                        act.wait_ge(delta_dve[hh], dve_at(hh, c, "arg"))
                        fn(dl[hh][0][:], dl[hh][0][:], ACT.Exp).then_inc(delta_act[hh], 1)
                    for hh in range(2):
                        wp(hh, "turn_k")
                        for step, w_, dst in (("kb", dec_kb, 5), ("kd", dec_kd, 6)):
                            for u in range(4):
                                last = fn(dl[hh][dst][:, u, :], bank[hh][0][:, u, :], ACT.Copy,
                                          scale=w_[:, c, 4 * hh + u:4 * hh + u + 1])
                            last.then_inc(delta_act[hh], 1)
                        wp(hh, "turn_v")
                        for u in range(4):
                            last = fn(dl[hh][7][:, u, :], bank[hh][1][:, u, :], ACT.Copy,
                                      scale=beta[:, c, 4 * hh + u:4 * hh + u + 1])
                        last.then_inc(delta_act[hh], 1)
                    for hh in range(2):
                        wp(hh, "turn_u")
                        fn(dl[hh][2][:], bank[hh][2], ACT.Copy).then_inc(delta_act[hh], 1)
                    for hh in range(2):
                        wp(hh, "wk")
                        fn(dl[hh][9][:], bank[hh][3], ACT.Copy, scale=-1.0).then_inc(delta_act[hh], 1)
                    for hh in range(2):
                        wp(hh, "uu")
                        fn(dl[hh][10][:], bank[hh][0], ACT.Copy).then_inc(delta_act[hh], 1)
                elif e == "o_norm":
                    h = ev[1]

                    def o_square(h):
                        if h >= 4:
                            act.wait_ge(on_mm, h - 3)
                        fn(osq[h % 4][:], qkv[:, h, :], ACT.Square).then_inc(on_sq, 1)

                    if h == 0:
                        for hh in range(2):
                            act.wait_ge(delta_dve[hh], dve_at(hh, NCH - 1, "s"))
                            act.wait_ge(delta_pe[hh], pe_at(hh, NCH - 1, "ss"))
                        act.wait_ge(sd_o, 1)
                        o_square(0)
                        o_square(1)
                    if h + 2 < NH:
                        o_square(h + 2)
                    act.wait_ge(on_mm, h + 1)
                    if h >= 4:
                        act.wait_ge(on_done, h - 3)
                    fn(orn[h % 4][:].rearrange("p (a n) -> p a n", a=2), pp[h % 4][:, :, 0:HALF], ACT.Sqrt,
                       bias=const("eps"), scale=1.0 / 128).then_inc(on_sqrt, 1)
                elif e == "m_split":
                    act.wait_ge(out_s0, 16)
                    split_hi(WO_BLOCK)
                    split_hi(WO_BLOCK + 1)
                    for k in range(KD):
                        act.wait_ge(on_done, k + 1)
                        fn(ht_h[:, k, :], mrg[:, k, :], ACT.Copy).then_inc(h_hi, 1)
                    act.wait_ge(wr_loaded, 16)
                    fn(w_r_h[:], w_r[:], ACT.Copy).then_inc(wr_hi, 1)
                elif e == "f_sumsq":
                    for k in range(KD):
                        act.wait_ge(x1_ready, k + 1)
                        fn(h2[:, k, :], x1[:, k, :], ACT.Square).then_inc(sq_ready, 1)
                    act.wait_ge(fin_mm, 1)
                    root_mean(pp[3], D, T).then_inc(sqrt_done, 1)
                    for k in range(KD):
                        act.wait_ge(h_norm, 16 + k + 1)
                        fn(ht_h[:, k, :], h2[:, k, :], ACT.Copy).then_inc(h_hi, 1)
                elif e == "router":
                    act.wait_ge(lg_ready, 1)
                    link(fn(r8[:, :, 4:8, 0], r8[:, :, 4:8, 1], ACT.Exp))
                    fn(r8[:, :, 0:1, 3], r8[:, :, 0:1, 2], ACT.Exp).then_inc(lg_exp, 1)
                elif e == "h_turn":
                    act.wait_ge(router_mm, 1)
                    for t in range(NT):
                        act.wait_ge(ht_mm, t + 1)
                        fn(h2t_h[:, t, :].rearrange("p (a n) -> p a n", a=2), pp[1 + t % 3][0:TT], ACT.Copy)\
                            .then_inc(ht_hi, 1)
                elif e == "moe":
                    act.wait_ge(rounds_set, 1)
                    act.sem_inc(xt_ready, 1)
                    act.sem_inc(y_ready, 1)
                    rounds = act.value_load(n_rounds[0:1, 0:1], min_val=1, max_val=9)
                    tb = pp[1][:, 1, :]
                    with act.Fori(0, rounds) as r:
                        with act.Fori(0, NE // 2) as p:
                            pair = r * (NE // 2) + p
                            for j in range(2):
                                n = pair * 2 + j
                                act.wait_ge(gather_mm, n + 2)
                                fn(xt[j][:].rearrange("p k n -> p (k n)"), pp[0][:, 0, :], ACT.Copy)\
                                    .then_inc(xt_ready, 1)
                                act.wait_ge(gu_mm, n + 1)
                                fn(sg[:].rearrange("p f n -> p (f n)"), pp[0][:, 1, 0:256], ACT.Silu)\
                                    .then_inc(silu_done, 1)
                                act.wait_ge(y_mm, n + 1)
                                fn(y_t[:, :, j * CAP:(j + 1) * CAP],
                                   pp[1][:, 0, :].rearrange("p (k n) -> p k n", k=KD), ACT.Copy)\
                                    .then_inc(y_ready, 1)
                            for i in range(2):
                                act.wait_ge(turn_mm, pair * 4 + 4 + i)
                                fn(y_tok[:, i * 512:(i + 1) * 512], tb, ACT.Copy).then_inc(turn_out, 1)
                elif e == "final":
                    for k in range(KD):
                        act.wait_ge(x1_ready, 8 + k + 1)
                        fn(fsq[:, k, :], x1[:, k, :], ACT.Square).then_inc(fin_sq, 1)
                    act.wait_ge(fin_mm, 2)
                    root_mean(pp[0], D, T).then_inc(sqrt_done, 1)

        @block.gpsimd
        def _(pool):
            tt = nc.gpsimd.tensor_tensor

            def split_lo(b):
                pool.wait_ge(hi_ready, b + 1)
                tt(w_l[b % 2][:], raw[b % 2][:], w_h[b % 2][:].bitcast(F32), ALU.subtract).then_inc(lo_ready, 1)

            pool.wait_ge(const_in, 32)
            for ev in SCHEDULE:
                e = ev[0]
                if e == "tile":
                    j = ev[1]
                    what, t = kind(j)
                    b = j // 2
                    if j % 2 == 0 and b + 1 < (WO_BLOCK if b < WO_BLOCK else NBLK) and b + 1 != WO_BLOCK + 1:
                        split_lo(b + 1)
                    if what == "av":
                        out_of_psum(pool, j)
                        tt(a_sq[:, t, :], av[:, t, :], av[:, t, :], ALU.mult).then_inc(a_sq_ready, 1)
                    elif what == "gc":
                        out_of_psum(pool, j)
                        tt(mrg[:, t, :], mrg[:, t, :], qc[:, t, :], ALU.add).then_inc(gc_added, 1)
                        if t == 7:
                            pool.wait_ge(gc_added, 8)
                            for i in range(2):
                                last = nc.gpsimd.memset(xpad[i][:, 0:3], 0.0)
                            last.then_inc(conv_zero, 1)
                            nc.gpsimd.memset(st[:], 0.0).then_inc(st_zero, 1)
                    elif what == "qkv":
                        pool.wait_ge(conv_copy, t + 1)
                        nc.gpsimd.tensor_copy(convp[:, t, :], xpad[t % 2][:, SEQ:SEQ + 3])
                        nc.gpsimd.tensor_copy(ext[:, t, 3, :], xpad[t % 2][:, 3 + SEQ:3 + T]).then_inc(ext_ready, 1)
                elif e == "x_sumsq":
                    split_lo(0)
                    pool.wait_ge(ws_loaded, 32)
                    tt(ws_t[:], ws_t[:], const("triu").rearrange("p (o n) -> p o n", o=1)
                       .to_broadcast([128, NH, CH]), ALU.mult).then_inc(ws_masked, 1)
                elif e == "ba":
                    pool.wait_ge(wba_hi, 1)
                    tt(w_ba_l[:], w_ba[:], w_ba_h[:].bitcast(F32), ALU.subtract).then_inc(wba_split, 1)
                elif e == "sd_outer":
                    h = ev[1]
                    if h == 0:
                        pool.wait_ge(side_free, SIDE[("sd_state",)] + 1)
                    tt(s0[:, h, :, :], s0[:, h, :, :], s_bc[:, 1, :, h:h + 1].to_broadcast([128, NS, 128]),
                       ALU.mult).then_inc(sd_dec, 1)
                elif e == "m_split":
                    split_lo(WO_BLOCK)
                    split_lo(WO_BLOCK + 1)
                    pool.wait_ge(wr_hi, 1)
                    tt(w_r_l[:], w_r[:], w_r_h[:].bitcast(F32), ALU.subtract).then_inc(wr_split, 1)

        @block.vector
        def _(dve):
            tt = nc.vector.tensor_tensor
            ts_ = nc.vector.tensor_scalar
            stt = nc.vector.scalar_tensor_tensor
            copy = nc.vector.tensor_copy
            chain = [0]

            def link(ins):
                chain[0] += 1
                ins.then_inc(dve_chain, 1)
                dve.wait_ge(dve_chain, chain[0])

            def normed(dst, src, gain, n, done):
                for k in range(KD):
                    stt(dst[:, k, :], src[:, k, :], param(gain, k), rstd[:, 0:n], ALU.mult, ALU.mult)\
                        .then_inc(done, 1)

            def split_lo(lo, hi, src, at):
                for k in range(KD):
                    dve.wait_ge(h_hi, at + k + 1)
                    tt(lo[:, k, :], src[:, k, :], hi[:, k, :].bitcast(F32), ALU.subtract).then_inc(h_lo, 1)

            def tile(j):
                what, t = kind(j)
                ps = pp[j % 3][:, :, 0:HALF]
                free = psum_free[j % 3]

                def whole(x):
                    return x.rearrange("p (a n) -> p a n", a=2)

                if what in ("mk", "mv", "qm", "wo"):
                    dve.wait_ge(tile_mm, j + 1)
                if what == "mk":
                    copy(mk[:, t, :], pp[j % 3][:, 0, 0:NM]).then_inc(free, 1)
                elif what == "mv":
                    copy(mv[:, t % 2, (t // 2) * BLK:(t // 2 + 1) * BLK], pp[j % 3][:, 0, 0:BLK]).then_inc(free, 1)
                elif what == "ga":
                    dve.wait_ge(tile_act, t + 1)
                    tt(whole(mrg[:, t, :]), ps, whole(au[:, t, :]), ALU.mult).then_inc(free, 1)
                elif what == "qm":
                    copy(whole(qc[:, t, :]), ps).then_inc(free, 1)
                elif what == "z":
                    dve.wait_ge(tile_act, 8 + t + 1)
                    out_of_psum(dve, j - 8)
                    stt(whole(zg[:, t, :]), ps, param("norm_gdn"), whole(zg[:, t, :]), ALU.mult, ALU.mult)\
                        .then_inc(free, 1)
                elif what == "gc":
                    dve.wait_ge(tile_act, 16 + t + 1)
                    dve.wait_ge(side_free, SIDE[("p_value", t // 2)] + 1)
                    tt(whole(qc[:, t, :]), ps, whole(qc[:, t, :]), ALU.mult).then_inc(free, 1)
                elif what == "qkv":
                    out_of_psum(dve, j)
                    c_, x_ = cacc[t % 2], xpad[t % 2]
                    for tap in range(3):
                        ins = stt(c_[:, 0:SEQ], x_[:, tap:tap + SEQ], param("w_conv", 4 * t + tap), c_[:, 0:SEQ],
                                  ALU.mult, ALU.add)
                        if tap < 2:
                            link(ins)
                        else:
                            ins.then_inc(conv_sum, 1)
                elif what == "wo":
                    dve.wait_ge(xres_loaded, 16)
                    tt(whole(x1[:, t, :]), ps, whole(x_res[:, t, :]), ALU.add).then_inc(x1_ready, 1)

            dve.wait_ge(const_in, 32)
            for ev in SCHEDULE:
                e = ev[0]
                if e == "tile":
                    tile(ev[1])
                elif e == "x_sumsq":
                    dve.wait_ge(side_free, SIDE[ev] + 1)
                    link(nc.vector.reciprocal(rstd[:], rstd[:]))
                    normed(x_in, x_in, "norm_mix", T, h_norm)
                    split_lo(ht_l, ht_h, x_in, 0)
                elif e == "m_sumsq":
                    dve.wait_ge(side_free, SIDE[ev] + 1)
                    link(nc.vector.reciprocal(rstd[:, 0:NM], rstd[:, 0:NM]))
                    normed(mem, mem, "norm_mem", NM, h_norm)
                    split_lo(mem_l, mem_h, mem, 8)
                elif e == "a_sumsq":
                    dve.wait_ge(side_free, SIDE[ev] + 1)
                    link(nc.vector.reciprocal(rstd[:], rstd[:]))
                    normed(av, av, "norm_a_v", T, a_normed)
                elif e == "a_mix":
                    g = ev[1]
                    if g == 0:
                        dve.wait_ge(a_normed, 8)
                        for i in range(13, 16):
                            out_of_psum(dve, i)
                        link(tt(s_tmp[:], av[:, :, SEQ:T],
                                param("ws00").rearrange("p (g o) -> p g o", o=1).to_broadcast([128, NH, NS]), ALU.mult))
                        link(tt(s_tmp[:], s_tmp[:],
                                param("bs0").rearrange("p (g o) -> p g o", o=1).to_broadcast([128, NH, NS]), ALU.add))
                        link(tt(au[:, :, SEQ:T], au[:, :, SEQ:T], s_tmp[:], ALU.mult))
                    dve.wait_ge(side_mm, SIDE_MM[ev])
                    tt(au[:, g:g + 2, 0:SEQ], side[:], au[:, g:g + 2, 0:SEQ], ALU.mult).then_inc(side_free, 1)
                elif e == "ba":
                    dve.wait_ge(side_mm, SIDE_MM[ev])
                    copy(ba[:, 0:4, :].rearrange("p c n -> p (c n)"), side[:, 0, 0:64])
                    copy(ba[0:NS, 4, :], side[0:NS, 0, 64:80]).then_inc(side_free, 1)
                    dve.wait_ge(side_free, SIDE[ev] + 1)
                    for rows, ts in ((128, slice(0, 4)), (NS, slice(4, 5))):
                        n = ts.stop - ts.start
                        last = tt(tmp_g[0:rows, 0, ts, :], ba[0:rows, ts, NH:2 * NH],
                                  param("dt_bias")[0:rows].rearrange("p (o h) -> p o h", o=1)
                                  .to_broadcast([rows, n, NH]), ALU.add)
                    last.then_inc(g_step, 1)
                    dve.wait_ge(g_act, 2)
                    for rows, ts in ((128, slice(0, 4)), (NS, slice(4, 5))):
                        n = ts.stop - ts.start
                        link(stt(tmp_g[0:rows, 0, ts, :], tmp_g[0:rows, 0, ts, :], 0.0, tmp_g[0:rows, 1, ts, :],
                                 ALU.max, ALU.add))
                        stt(gate_g[0:rows, ts, :], tmp_g[0:rows, 0, ts, :], -1.0,
                            neg_a[0:rows].rearrange("p (o h) -> p o h", o=1).to_broadcast([rows, n, NH]),
                            ALU.mult, ALU.mult).then_inc(g_step, 1)
                elif e == "cumsum":
                    dve.wait_ge(side_mm, SIDE_MM[ev])
                    flat = cum_g[:].rearrange("p c h -> p (c h)")
                    copy(flat, side[:, 0, 0:32]).then_inc(g_step, 1)
                    dve.wait_ge(g_step, 4)
                    tt(dec_kd[:].rearrange("p c h -> p (c h)"), side[:, 0, 32:64], flat, ALU.subtract)\
                        .then_inc(g_step, 1)
                    dve.wait_ge(g_act, 8)
                    tt(dec_kb[:], dec_kb[:], beta[:, 0:NCH, :], ALU.mult).then_inc(side_free, 1)
                elif e == "s_score":
                    if ev[1] == NS - 1:
                        dve.wait_ge(kv_used, NS)
                        copy(s_sc[:], side[:, 0, 0:64]).then_inc(side_free, 1)
                elif e == "s_rows":
                    dve.wait_ge(side_mm, SIDE_MM[ev])
                    link(nc.vector.tensor_reduce(s_small[:, 0:1], side[0:32, 1, 0:NM], AX.X, ALU.max))
                    ts_(s_small[:, 1:2], s_small[:, 0:1], -1.0 / 16, None, ALU.mult).then_inc(soft_max, 1)
                    dve.wait_ge(soft_exp, 1)
                    link(nc.vector.reciprocal(s_small[:, 3:4], s_small[:, 2:3]))
                    ts_(s_pr[:], s_pr[:], s_small[:, 3:4], None, ALU.mult).then_inc(soft_norm, 1)
                    nc.vector.memset(s_small[:, 0:1], 0.0).then_inc(side_free, 1)
                elif e == "s_cols":
                    dve.wait_ge(side_mm, SIDE_MM[ev])
                    copy(s_prt[:], side[:, 0, 0:64]).then_inc(side_free, 1)
                elif e == "s_value":
                    if ev[1] == NS - 1:
                        dve.wait_ge(kv_used, 2 * NS)
                        copy(qc[:, :, SEQ:T], side[:, 1, 0:64].rearrange("p (k b) -> p k b", k=KD))\
                            .then_inc(side_free, 1)
                elif e == "p_score":
                    h = ev[1]
                    dve.wait_ge(side_mm, SIDE_MM[ev])
                    link(nc.vector.tensor_reduce(small[:, 0, :], side[:].rearrange("p a (c m) -> p (a c) m", c=2),
                                                 AX.X, ALU.max))
                    ts_(small[:, 1, :], small[:, 0, :], -1.0 / 16, None, ALU.mult).then_inc(soft_max, 1)
                    dve.wait_ge(soft_exp, 1 + NCH * (h + 1))
                    link(nc.vector.reciprocal(small[:, 3, :], small[:, 2, :]))
                    tt(prob[:], prob[:], small[:, 3, :].rearrange("p (c o) -> p c o", o=1)
                       .to_broadcast([128, NCH, NM]), ALU.mult).then_inc(soft_norm, 1)
                    nc.vector.memset(small[:, 0, :], 0.0).then_inc(side_free, 1)
                elif e == "p_value":
                    dve.wait_ge(side_mm, SIDE_MM[ev])
                    h = ev[1]
                    copy(qc[:, 2 * h:2 * h + 2, 0:SEQ], side[:]).then_inc(side_free, 1)
                elif e == "conv_s":
                    dve.wait_ge(ext_loaded, 16)
                    dve.wait_ge(ext_ready, 24)
                    link(tt(cvs[:], ext[:], param("w_conv").rearrange("p (t j o) -> p t j o", t=24, o=1)
                            .to_broadcast([128, 24, 4, NS]), ALU.mult))
                    nc.vector.tensor_reduce(cvs_sum[:], cvs[:].rearrange("p t j b -> p t b j"), AX.X, ALU.add)\
                        .then_inc(convs_sum, 1)
                elif e == "l2":
                    t = ev[1]
                    dve.wait_ge(l2_sqrt, t + 1)
                    link(nc.vector.reciprocal(l2rn[t % 4][:], l2rn[t % 4][:]))
                    tt(qkv[:, t, :], qkv[:, t, :], l2rn[t % 4][:], ALU.mult).then_inc(l2_done, 1)
                elif e == "sd_bcast":
                    idb = const("ident", NS)[:, 0:NS].rearrange("p (c o) -> p c o", o=1).to_broadcast([NS, NS, NH])
                    for i, src in enumerate((beta[0:NS, 4, :], s_eg[:])):
                        last = tt(s_rhs[:, i, :, :], idb,
                                  src.rearrange("p (o h) -> p o h", o=1).to_broadcast([NS, NS, NH]), ALU.mult)
                    last.then_inc(sd_rhs, 1)
                    dve.wait_ge(l2_done, 16)
                    tt(s_qk[:], qkv[:, 0:NH, SEQ:T], qkv[:, NH:2 * NH, SEQ:T], ALU.mult).then_inc(sd_rhs, 1)
                    dve.wait_ge(side_mm, SIDE_MM[ev])
                    copy(s_bc[:].rearrange("p a c h -> p (a c h)"), side[:, 0, 0:2 * NS * NH])
                    copy(s_qk[:].rearrange("p h b -> p (h b)"), side[:, 1, 0:NS * NH]).then_inc(side_free, 1)
                elif e == "sd_state":
                    dve.wait_ge(side_free, SIDE[("sd_bcast",)] + 1)
                    dve.wait_ge(side_mm, SIDE_MM[ev])
                    sv = side[:, 0, 0:2 * NS * NH].rearrange("p (h b a) -> p a h b", h=NH, b=NS)
                    bb, eg = s_bc[:, 0, :, :].rearrange("p b h -> p h b"), s_bc[:, 1, :, :].rearrange("p b h -> p h b")
                    link(tt(s_u[:], sv[:, 1, :, :], eg, ALU.mult))
                    link(tt(s_u[:], qkv[:, 2 * NH:3 * NH, SEQ:T], s_u[:], ALU.subtract))
                    tt(s_u[:], s_u[:], bb, ALU.mult).then_inc(sd_u, 1)
                    link(tt(s_tmp[:], sv[:, 0, :, :], eg, ALU.mult))
                    dve.wait_ge(sd_u, 1)
                    link(tt(s_qk[:], s_qk[:], s_u[:], ALU.mult))
                    tt(qkv[:, 0:NH, SEQ:T], s_qk[:], s_tmp[:], ALU.add).then_inc(side_free, 1)
                elif e == "sd_utok":
                    dve.wait_ge(side_mm, SIDE_MM[ev])
                    copy(u_tok[:].rearrange("p h n -> p (h n)").rearrange("p (a n) -> p a n", a=2), side[0:NS])\
                        .then_inc(side_free, 1)
                elif e == "sd_outer":
                    h = ev[1]

                    def diag(h):
                        if h >= 2:
                            dve.wait_ge(side_mm, SIDE_MM[("sd_outer", h - 2)])
                        tt(u_diag[h % 2][:], u_tok[:, h:h + 1, :].to_broadcast([NS, NS, 128]),
                           const("ident", NS)[:, 0:NS].rearrange("p (c o) -> p c o", o=1)
                           .to_broadcast([NS, NS, 128]), ALU.mult).then_inc(sd_diag, 1)

                    if h == 0:
                        dve.wait_ge(side_free, SIDE[("sd_utok",)] + 1)
                        diag(0)
                    if h + 1 < NH:
                        diag(h + 1)
                    dve.wait_ge(side_mm, SIDE_MM[ev])
                    dve.wait_ge(sd_dec, h + 1)
                    tt(s0[:, h, :, :].rearrange("p (a b) n -> p a (b n)", a=2), side[:],
                       s0[:, h, :, :].rearrange("p (a b) n -> p a (b n)", a=2), ALU.add).then_inc(side_free, 1)
                    dve.wait_ge(side_free, SIDE[ev] + 1)
                    nc.vector.memset(small[:, 0, 0:1], 0.0).then_inc(sd_new, 1)
                    if h == 0:
                        nc.vector.memset(small[:, 0, 1:2], 0.0).then_inc(sd_o, 1)
                elif e == "delta":
                    c = ev[1]
                    cs = slice(c * CH, (c + 1) * CH)

                    def wp(hh, step, cc=c):
                        dve.wait_ge(delta_pe[hh], pe_at(hh, cc, step))

                    def wa(hh, step, cc=c):
                        dve.wait_ge(delta_act[hh], act_at(hh, cc, step))

                    def wide(mask):
                        return mask.rearrange("p (o n) -> p o n", o=1).to_broadcast([128, 4, 128])

                    for hh in range(2):
                        wp(hh, "grow")
                        if c:
                            wp(hh, "oo", c - 1)
                        for u in range(4):
                            h = 4 * hh + u
                            last = ts_(dl[hh][0][:, u, :], bank[hh][0][:, u, :], cum_g[:, c, h:h + 1], 0.0,
                                       ALU.subtract, ALU.min)
                        last.then_inc(delta_dve[hh], 1)
                    for hh in range(2):
                        wa(hh, "dt")
                        link(tt(dl[hh][1][:], dl[hh][0][:], wide(const("strict")), ALU.mult))
                        wp(hh, "brow")
                        tt(dl[hh][1][:], bank[hh][1], dl[hh][1][:], ALU.mult).then_inc(delta_dve[hh], 1)
                    for hh in range(2):
                        wp(hh, "kk")
                        dve.wait_ge(delta_dve[hh], dve_at(hh, c, "bs"))
                        tt(dl[hh][1][:], bank[hh][2], dl[hh][1][:], ALU.mult).then_inc(delta_dve[hh], 1)
                    for hh in range(2):
                        dve.wait_ge(delta_dve[hh], dve_at(hh, c, "mt"))
                        link(tt(dl[hh][4][:], dl[hh][1][:], wide(const("first_t")), ALU.mult))
                        tt(dl[hh][3][:], wide(const("ident")), dl[hh][4][:], ALU.subtract)\
                            .then_inc(delta_dve[hh], 1)
                    for hh in range(2):
                        link(tt(dl[hh][0][:], dl[hh][0][:], wide(const("triu")), ALU.mult))
                        wp(hh, "kq")
                        tt(dl[hh][0][:], bank[hh][3], dl[hh][0][:], ALU.mult).then_inc(delta_dve[hh], 1)
                    for hh in range(2):
                        wa(hh, "eg")
                        tt(dl[hh][8][:], qkv[:, 4 * hh:4 * hh + 4, cs], dl[hh][8][:], ALU.mult)\
                            .then_inc(delta_dve[hh], 1)
                    for l in range(6):
                        x, y = CONST["merge"]
                        mask = consts[:, x + l * 128:x + (l + 1) * 128]
                        for hh in range(2):
                            wp(hh, f"mt{l}")
                            tt(dl[hh][4][:], bank[hh][2], wide(mask), ALU.mult).then_inc(delta_dve[hh], 1)
                        for hh in range(2):
                            wp(hh, f"tx{l}")
                            tt(dl[hh][2][:], dl[hh][2][:], bank[hh][3], ALU.subtract)
                            tt(dl[hh][3][:], dl[hh][3][:], bank[hh][2], ALU.subtract).then_inc(delta_dve[hh], 1)
                    for hh in range(2):
                        wp(hh, "oo")
                        copy(qkv[:, 4 * hh:4 * hh + 4, cs], bank[hh][1]).then_inc(delta_dve[hh], 1)
                    for hh in range(2):
                        wp(hh, "ss")
                        if c == 0:
                            dve.wait_ge(st_zero, 1)
                        else:
                            dve.wait_ge(delta_dve[hh], dve_at(hh, c - 1, "s"))
                        for u in range(4):
                            h = 4 * hh + u
                            last = stt(st[:, h, :], st[:, h, :], dec_end[:, c, h:h + 1], bank[hh][2][:, u, :],
                                       ALU.mult, ALU.add)
                        last.then_inc(delta_dve[hh], 1)
                elif e == "o_norm":
                    h = ev[1]
                    dve.wait_ge(on_sqrt, h + 1)
                    link(nc.vector.reciprocal(orn[h % 4][:], orn[h % 4][:]))
                    link(tt(qkv[:, h, :], qkv[:, h, :], orn[h % 4][:], ALU.mult))
                    link(tt(qkv[:, h, :], qkv[:, h, :], zg[:, h, :], ALU.mult))
                    dve.wait_ge(gc_added, 8)
                    tt(mrg[:, h, :], mrg[:, h, :], qkv[:, h, :], ALU.add).then_inc(on_done, 1)
                elif e == "m_split":
                    split_lo(ht_l, ht_h, mrg, 16)
                elif e == "f_sumsq":
                    dve.wait_ge(sqrt_done, 1)
                    link(nc.vector.reciprocal(rstd[:], rstd[:]))
                    normed(h2, x1, "norm_ffn", T, h_norm)
                    split_lo(ht_l, ht_h, h2, 24)
                elif e == "router":
                    dve.wait_ge(router_mm, 1)
                    link(tt(lg[:], pp[0][0:TT, 0, 0:180].rearrange("p (t n) -> p t n", t=NT),
                            param("b_router")[0:TT].rearrange("p (o n) -> p o n", o=1)
                            .to_broadcast([TT, NT, NG + NE]), ALU.add))
                    gl = lg[:, :, 0:NG]
                    g_top, g_first = r8[:, :, 0:1, 0], r8[:, :, 1:2, 0]
                    one4 = r8[:, :, 0:4, 1]

                    def wide(x, n):
                        return x.to_broadcast([TT, NT, n])

                    def first_top(one, src, top, tmp, desc, n):
                        d_ = const(desc, TT).rearrange("p (o n) -> p o n", o=1).to_broadcast([TT, NT, n])
                        link(nc.vector.tensor_reduce(top, src, AX.X, ALU.max))
                        link(tt(one, src, wide(top, n), ALU.is_equal))
                        link(tt(one, one, d_, ALU.mult))
                        link(nc.vector.tensor_reduce(tmp, one, AX.X, ALU.max))
                        link(tt(one, one, wide(tmp, n), ALU.is_equal))

                    first_top(one4, gl, g_top, g_first, "desc4", 4)
                    link(tt(prod32[:], lg[:, :, NG:].rearrange("p t (g x) -> p t g x", g=NG),
                            one4.rearrange("p t (g o) -> p t g o", o=1).to_broadcast([TT, NT, NG, EPG]), ALU.mult))
                    link(nc.vector.tensor_reduce(ing[:], prod32[:].rearrange("p t g x -> p t x g"), AX.X, ALU.add))
                    m1, m2, f1 = r8[:, :, 2:3, 0], r8[:, :, 3:4, 0], r8[:, :, 0:1, 3]
                    first_top(oh1[:], ing[:], m1, f1, "desc8", 8)
                    link(stt(ing2[:], oh1[:], -3.0e38, ing[:], ALU.mult, ALU.add))
                    first_top(oh2[:], ing2[:], m2, f1, "desc8", 8)
                    link(tt(r8[:, :, 0:1, 2], m2, m1, ALU.subtract))
                    tt(r8[:, :, 4:8, 1], gl, wide(g_top, 4), ALU.subtract).then_inc(lg_ready, 1)
                    dve.wait_ge(lg_exp, 1)
                    psum_, e2, w1, w2 = r8[:, :, 1:2, 2], r8[:, :, 0:1, 3], r8[:, :, 2:3, 2], r8[:, :, 3:4, 2]
                    link(nc.vector.tensor_reduce(psum_, r8[:, :, 4:8, 0], AX.X, ALU.add))
                    link(ts_(w1, e2, 1.0, None, ALU.add))
                    link(tt(w1, w1, psum_, ALU.mult))
                    link(nc.vector.reciprocal(w1, w1))
                    link(tt(w2, w1, e2, ALU.mult))
                    link(tt(w8[:], oh1[:], wide(w1, EPG), ALU.mult))
                    link(tt(ing2[:], oh2[:], wide(w2, EPG), ALU.mult))
                    link(tt(w8[:], w8[:], ing2[:], ALU.add))
                    link(tt(ing[:], oh1[:], oh2[:], ALU.add))
                    o4 = one4.rearrange("p t (g o) -> p t g o", o=1).to_broadcast([TT, NT, NG, EPG])

                    def over_groups(x):
                        return x[:].rearrange("p t (o x) -> p t o x", o=1).to_broadcast([TT, NT, NG, EPG])

                    link(tt(comb[:].rearrange("p t (g x) -> p t g x", g=NG), over_groups(w8), o4, ALU.mult))
                    tt(hit[:].rearrange("p t (g x) -> p t g x", g=NG), over_groups(ing), o4, ALU.mult)\
                        .then_inc(hit_ready, 1)
                elif e == "h_turn":
                    for t in range(NT):
                        dve.wait_ge(ht_hi, t + 1)
                        tt(h2t_l[:, t, :].rearrange("p (a n) -> p a n", a=2), pp[1 + t % 3][0:TT],
                           h2t_h[:, t, :].bitcast(F32).rearrange("p (a n) -> p a n", a=2), ALU.subtract)\
                            .then_inc(ht_lo, 1)
                elif e == "rank":
                    dve.wait_ge(rank_mm, 1)
                    link(stt(rank[:].rearrange("p t n -> p (t n)"), pp[0][0:TT, 1, 0:160], 1.0,
                             hit[:].rearrange("p t n -> p (t n)"), ALU.add, ALU.mult))
                    link(ts_(rank[:], rank[:], -1.0, None, ALU.add))
                    link(nc.vector.tensor_reduce(cnt[:, 0:1], pp[0][:, 1, 160:160 + NE], AX.X, ALU.max))
                    link(ts_(cnt[:, 8:16], const("rounds"), cnt[:, 0:1], None, ALU.is_lt))
                    link(nc.vector.tensor_reduce(cnt[:, 1:2], cnt[:, 8:16], AX.X, ALU.add))
                    ts_(n_rounds[0:1, 0:1], cnt[0:1, 1:2], 1.0, None, ALU.add).then_inc(rounds_set, 1)
                    nc.vector.memset(y_tok[:], 0.0)
                    nc.vector.memset(sel_t[:], 0.0).then_inc(moe_zero, 1)
                    nc.vector.memset(cnt[:, 2:3], 0.0).then_inc(sc_free, 2)
                elif e == "moe":
                    dve.wait_ge(rounds_set, 1)
                    dve.sem_inc(act_ready, 1)
                    dve.sem_inc(turn_out, 1)
                    dve.wait_ge(ht_mm, NT)
                    rounds = dve.value_load(n_rounds[0:1, 0:1], min_val=1, max_val=9)
                    gb = pp[0][:, 1, 256:512].rearrange("p (f n) -> p f n", f=4)
                    slots = const("slots", TT).rearrange("p (o n) -> p o n", o=1).to_broadcast([TT, NT, CAP])

                    def add_back(pair, dc0, dc1):
                        for dc in range(dc0, dc1):
                            dve.wait_ge(sc_mm, pair * KD + dc + 1)
                            tt(x1[:, dc, :].rearrange("p (a n) -> p a n", a=2), pp[2 + dc % 2][:, :, 0:HALF],
                               x1[:, dc, :].rearrange("p (a n) -> p a n", a=2), ALU.add).then_inc(sc_free, 1)

                    with dve.Fori(0, rounds) as r:
                        with dve.Fori(0, NE // 2) as p:
                            pair = r * (NE // 2) + p
                            for j in range(2):
                                ex = p * 2 + j
                                dve.wait_ge(gather_mm, pair * 2 + j + 1)
                                tt(sel[j][:], slots, rank[:, :, bass.ds(ex, 1)].to_broadcast([TT, NT, CAP]),
                                   ALU.is_equal).then_inc(sel_ready, 1)
                            for j in range(2):
                                ex = p * 2 + j
                                dve.wait_ge(turn_mm, pair * 4 + 1)
                                dve.wait_ge(sel_ready, pair * 2 + 2)
                                tt(sel_w[:, :, j * CAP:(j + 1) * CAP], sel[j][:].bitcast(F32),
                                   comb[:, :, bass.ds(ex, 1)].to_broadcast([TT, NT, CAP]), ALU.mult)\
                                    .then_inc(selw_ready, 1)
                            for j in range(2):
                                n = pair * 2 + j
                                dve.wait_ge(silu_done, n + 1)
                                tt(act_t[j][:], gb, sg[:], ALU.mult).then_inc(act_ready, 1)
                                add_back(pair, 4 * j, 4 * j + 4)
                            dve.wait_ge(turn_mm, pair * 4 + 2)
                            copy(sel_t[:, 0:4, :].rearrange("p t n -> p (t n)"), pp[1][:, 1, 0:4 * TT])\
                                .then_inc(turn_out, 1)
                            dve.wait_ge(turn_mm, pair * 4 + 3)
                            copy(sel_t[:, 4, :], pp[1][:, 1, 0:TT]).then_inc(turn_out, 1)
                        dve.wait_ge(sel_ready, (r + 1) * NE)
                        ts_(rank[:], rank[:], -float(CAP), None, ALU.add).then_inc(rank_moved, 1)
                        dve.wait_ge(rank_moved, r + 1)
                    add_back(rounds * (NE // 2), 0, 8)
                elif e == "final":
                    dve.wait_ge(sc_free, rounds * (NE // 2) * KD + 2 + KD)
                    nc.vector.memset(cnt[:, 2:3], 0.0).then_inc(x1_ready, 8)
                    dve.wait_ge(sqrt_done, 2)
                    link(nc.vector.reciprocal(rstd[:], rstd[:]))
                    normed(x1, x1, "norm_final", T, fin_done)


def kernel(**inputs):
    import numpy as _np
    import concourse.bacc as _bacc
    from concourse.bass_utils import run_bass_kernel_spmd as _run

    f = {k: _np.asarray(v) for k, v in inputs.items()}

    def chunks(x):
        return x.reshape(x.shape[0], -1, 128).transpose(2, 1, 0)

    def cols(x):
        return x.reshape(-1, 128).T

    def everywhere(x):
        return _np.broadcast_to(x.reshape(1, -1), (128, x.size))

    w_in = f["w_in"][0]
    edge = _np.cumsum([0, D, D, 3 * D, D, NH, NH, D, D, D, D])
    part = {n: w_in[:, edge[i]:edge[i + 1]] for i, n in
            enumerate(("au", "av", "qkv", "z", "beta", "alpha", "qm", "ga", "gb", "gc"))}
    part["mk"], part["mv"] = f["w_mem_kv"][0][:, :D], f["w_mem_kv"][0][:, D:]
    part["wo"] = f["w_o"][0]
    w_blk = _np.concatenate([part[n].reshape(KD, 128, -1, BLK).transpose(2, 1, 0, 3) for n, _ in BLOCKS])
    kc = f["cache_mem_k"][0].reshape(NS, NM, MH, 2, 128).transpose(0, 4, 2, 3, 1)
    vc = f["cache_mem_v"][0].reshape(NS, 2, 128, D).transpose(0, 2, 1, 3)
    x = _np.concatenate([f["x_prompt"][0], f["x_sample"][:, 0]])
    par = _np.concatenate([
        cols(f["norm_mix"]), cols(f["norm_mem"]), cols(f["norm_ffn"]), cols(f["norm_final"]),
        cols(f["norm_a_v"]), f["norm_gdn_out"].T, cols(f["b_gate"]),
        f["w_conv"][0].reshape(4, 24, 128).transpose(2, 1, 0).reshape(128, 96),
        everywhere(f["w_s"][0, :, 0, 0]), everywhere(f["b_s"][0, :, 0]), everywhere(f["a_log"][0]),
        everywhere(f["dt_bias"][0]), everywhere(f["b_router_group"][0]), everywhere(f["b_router_expert"][0])],
        axis=1)

    def rows(w, n):
        return w.reshape(NE, n, 128, -1).transpose(0, 2, 1, 3).reshape(NE, 128, -1)

    arrays = {
        "consts": make_constants(), "params": par,
        "x_t": chunks(x).reshape(128, -1), "mem_t": chunks(f["mem_prompt"][0]).reshape(128, -1),
        "w_blk": w_blk.reshape(NBLK, 128, -1),
        "w_ba": _np.concatenate([part["beta"], part["alpha"]], 1).reshape(KD, 128, 16).transpose(1, 0, 2)
                   .reshape(128, -1),
        "ws_t": f["w_s"][0].transpose(2, 0, 1).reshape(128, -1), "bs": f["b_s"][0].reshape(1, -1),
        "cache_k": kc.reshape(NS, 128, -1), "cache_v": vc.reshape(NS, 128, -1),
        "state_conv": f["state_conv"][0].reshape(NS, 3, 24, 128).transpose(3, 2, 1, 0).reshape(128, -1),
        "state_gdn": f["state_gdn"][0].transpose(2, 1, 0, 3).reshape(128, -1),
        "w_router": _np.concatenate([f["w_router_group"][0], f["w_router_expert"][0]], 1)
                       .reshape(KD, 128, NG + NE).transpose(1, 0, 2).reshape(128, -1),
        "w_gate": rows(f["w_exp_gate"], KD), "w_up": rows(f["w_exp_up"], KD), "w_down": rows(f["w_exp_down"], 4),
    }
    arrays = {k: _np.ascontiguousarray(v) for k, v in arrays.items()}
    outs = {"y": KD * T, "av": KD * NS, "mk": KD * NM, "mv": 2 * D, "conv_s": 24 * 3 * NS, "conv_p": 24 * 3,
            "gdn_s": NH * NS * 128, "gdn_p": NH * 128}

    nc = _bacc.Bacc("TRN2", target_bir_lowering=False, num_devices=1)
    a = {k: nc.dram_tensor(f"in_{k}", v.shape, mybir.dt.from_np(v.dtype), kind="ExternalInput").ap()
         for k, v in arrays.items()}
    o = {k: nc.dram_tensor(f"out_{k}", (128, n), F32, kind="ExternalOutput").ap() for k, n in outs.items()}
    build_step(nc, a, o)
    got = _run(nc, [{f"in_{k}": v for k, v in arrays.items()}], core_ids=[0]).results[0]
    r = {k: got[f"out_{k}"] for k in outs}

    y = r["y"].reshape(128, KD, T).transpose(2, 1, 0).reshape(T, D)
    return (
        y[:SEQ].reshape(1, SEQ, D), y[SEQ:].reshape(NS, 1, D),
        r["mk"].reshape(128, KD, NM).transpose(2, 1, 0).reshape(1, 1, NM, MH, D // MH),
        r["mv"].reshape(128, 2, D).transpose(1, 0, 2).reshape(1, 1, NM, MH, D // MH),
        r["gdn_p"].reshape(128, NH, 128).transpose(1, 0, 2).reshape(1, 1, NH, 128, 128),
        r["conv_p"].reshape(128, 24, 3).transpose(2, 1, 0).reshape(1, 1, 3, 3 * D),
        r["gdn_s"].reshape(128, NH, NS, 128).transpose(2, 1, 0, 3).reshape(1, NS, NH, 128, 128),
        r["conv_s"].reshape(128, 24, 3, NS).transpose(3, 2, 1, 0).reshape(1, NS, 3, 3 * D),
        r["av"].reshape(128, KD, NS).transpose(2, 1, 0).reshape(1, NS, 1, D),
    )
```

```python
from contextlib import ExitStack

import numpy as np
import concourse.bass as bass
from concourse import mybir

F32 = mybir.dt.float32
F32R = mybir.dt.float32r
BF16 = mybir.dt.bfloat16
I32 = mybir.dt.int32
ALU = mybir.AluOpType
ACT = mybir.ActivationFunctionType
AX = mybir.AxisListType

D = 1024
SEQ = 512
NS = 8
T = SEQ + NS
HALF = T // 2
KD = D // 128
NM = 256
NH = 8
MH = 4
CH = 128
NCH = SEQ // CH
BLK = 256
NG, EPG = 4, 8
NE = NG * EPG
DE = 512
CAP = 64
TT, NT = 104, 5
EPS = 1e-6
NPAIR = NE // 2
SC = 2 * KD

BLOCKS = [("av", 4), ("au", 4), ("mk", 4), ("mv", 4), ("ga", 4), ("qm", 4), ("gb", 4), ("z", 4),
          ("gc", 4), ("qkv", 12), ("wo", 4)]
BLOCK_KIND = [name for name, n in BLOCKS for _ in range(n)]
FIRST_BLOCK = {name: BLOCK_KIND.index(name) for name, _ in BLOCKS}
NBLK = len(BLOCK_KIND)
WO_BLOCK = FIRST_BLOCK["wo"]
WO_TILE = 2 * WO_BLOCK
QKV_TILE = 2 * FIRST_BLOCK["qkv"]

CONST = {}
_at = 0
for _n, _w in [("ident", 128), ("ones", 128), ("triu", 128), ("strict", 128), ("first_t", 128),
               ("merge", 6 * 128), ("slots", CAP), ("rounds", 8), ("desc4", 4), ("desc8", 8),
               ("eps", 1), ("eps128", 1)]:
    CONST[_n] = (_at, _at + _w)
    _at += _w
NCONST = _at
PARAM = {}
_at = 0
for _n, _w in [("norm_mix", 8), ("norm_mem", 8), ("norm_ffn", 8), ("norm_final", 8), ("norm_a_v", 8),
               ("norm_gdn", 1), ("b_gate", 24), ("w_conv", 96), ("ws00", 8), ("bs0", 8),
               ("a_log", 8), ("dt_bias", 8), ("b_router", NG + NE)]:
    PARAM[_n] = (_at, _at + _w)
    _at += _w
NPARAM = _at


def make_constants():
    c = np.zeros((128, NCONST), np.float32)
    p, f = np.arange(128)[:, None], np.arange(128)[None, :]

    def put(name, value):
        a, b = CONST[name]
        c[:, a:b] = value

    put("ident", p == f)
    put("ones", 1.0)
    put("triu", p <= f)
    put("strict", p < f)

    def below(s):
        return (p // (2 * s) == f // (2 * s)) & (p // s % 2 == 1) & (f // s % 2 == 0)

    put("first_t", below(1).T)
    put("merge", np.concatenate([below(s) for s in (2, 4, 8, 16, 32, 64)], axis=1))
    put("slots", np.arange(CAP))
    put("rounds", CAP * np.arange(1, 9))
    put("desc4", np.arange(4, 0, -1))
    put("desc8", np.arange(8, 0, -1))
    put("eps", EPS)
    put("eps128", 128 * EPS)
    return c


def make_schedule():
    after = {}

    def put(j, *events):
        after.setdefault(j, []).extend(events)

    put(3, ("m_sumsq",))
    put(9, ("a_sumsq",))
    for c in range(NCH):
        put(16 + 2 * c, ("a_turn", c))
    for g in range(0, NH, 2):
        put(24 + g, ("a_mix", g))
    put(44, ("ba",))
    put(46, ("cumsum",))
    for i in range(4):
        put(49 + i, ("s_score", 2 * i), ("s_score", 2 * i + 1))
    put(53, ("s_rows",))
    put(54, ("s_cols",))
    for i in range(8):
        put(55 + i // 3, ("s_value", i))
    for h in range(MH):
        put(58 + 3 * h, ("p_score", h))
        put(59 + 3 * h, ("p_turn", h))
        put(60 + 3 * h, ("p_value", h))
    out = [("x_sumsq",)]
    for j in range(WO_TILE):
        out.append(("tile", j))
        out += after.get(j, [])
    out += [("conv_s",)] + [("l2", t) for t in range(2 * NH)]
    out += [("sd_bcast",), ("sd_state",), ("sd_ktok",), ("sd_utok",)] + [("sd_outer", h) for h in range(NH)]
    out += [("delta", c) for c in range(NCH)]
    out += [("o_norm", h) for h in range(NH)]
    out += [("m_split",)]
    out += [("tile", j) for j in range(WO_TILE, 2 * NBLK)]
    out += [("f_sumsq",), ("router",), ("h_turn",), ("rank",), ("moe",), ("final",)]
    return out


SCHEDULE = make_schedule()
SIDE = {}
for _e in SCHEDULE:
    _k = {"s_score": ("s_score",), "s_value": ("s_value",)}.get(_e[0], _e)
    if _e[0] in ("x_sumsq", "m_sumsq", "a_sumsq", "a_turn", "a_mix", "ba", "cumsum", "s_score", "s_rows",
                 "s_cols", "s_value", "p_score", "p_turn", "p_value", "sd_bcast", "sd_state", "sd_ktok",
                 "sd_utok", "sd_outer") and _k not in SIDE:
        SIDE[_k] = len(SIDE)

NO_SIDE_MM = (("s_score",), ("s_value",))
SIDE_MM = {_e: 1 + sum(SIDE[_f] < SIDE[_e] and _f not in NO_SIDE_MM for _f in SIDE) for _e in SIDE}
PE_STEPS = (["grow", "brow", "kk", "kq", "turn_k", "turn_v", "turn_u"]
            + [f"{m}{l}" for l in range(6) for m in ("mt", "tx")] + ["wk", "uu", "oo", "ss"])
DVE_STEPS = (["arg", "bs", "mt", "u1", "at", "qg"]
             + [f"{m}{l}" for l in range(6) for m in ("x", "tu")] + ["o", "s"])
ACT_STEPS = ["eg", "dt", "kb", "kd", "vb", "t1", "nw", "u"]


def build_step(nc, a, o):
    ctx = ExitStack()
    with ctx:
        def sem(name):
            return ctx.enter_context(nc.semaphore(name))

        base = (nc.sbuf_base + 63) // 64 * 64
        room = (nc.sbuf_usable_end - 64 - base) // 4
        words = {}
        at = 0
        for name, n in [("FIX", 3520), ("RA", 24 * T), ("M", 8 * T), ("ZG", 8 * T), ("HT", 16 * T),
                        ("CQ", 8 * T), ("MKV", 4096), ("RAW", 4096), ("SPL", 8192)]:
            words[name] = at
            at += n
        assert at <= room, (at, room)
        fix = [0]

        def place(name, shape, region, off=0, dt=F32):
            return nc.alloc_sbuf_tensor_at(name, shape, dt, offset=base + 4 * (words[region] + off))

        def fixed(name, shape, dt=F32):
            n = int(np.prod(shape[1:]))
            n = (n + 7) // 8 * 8
            t = place(name, shape, "FIX", fix[0], dt)
            fix[0] += n
            assert fix[0] <= 3520, fix[0]
            return t

        consts = fixed("consts", [128, NCONST])
        params = fixed("params", [128, NPARAM])
        rstd = fixed("rstd", [128, T])
        ba = fixed("ba", [128, NT, 16])
        gate_g = fixed("gate_g", [128, NT, NH])
        beta = fixed("beta", [128, NT, NH])
        tmp_g = fixed("tmp_g", [128, 2, NT, NH])
        cum_g = fixed("cum_g", [128, NCH, NH])
        dec_end = fixed("dec_end", [128, NCH, NH])
        dec_kd = fixed("dec_kd", [128, NCH, NH])
        dec_kb = fixed("dec_kb", [128, NCH, NH])
        neg_a = fixed("neg_a", [128, NH])
        small = fixed("small", [128, 4, 4])
        s_small = fixed("s_small", [32, 4])
        s_rhs = fixed("s_rhs", [NS, 2, NS, NH])
        s_bc = fixed("s_bc", [128, 2, NS, NH])
        s_qk = fixed("s_qk", [128, NH, NS])
        s_u = fixed("s_u", [128, NH, NS])
        s_tmp = fixed("s_tmp", [128, NH, NS])
        s_eg = fixed("s_eg", [NS, NH])
        n_rounds = fixed("n_rounds", [1, 8], I32)

        def const(name, rows=128):
            x, y = CONST[name]
            return consts[0:rows, x:y]

        def param(name, i=None, n=1):
            x, y = PARAM[name]
            return params[:, x:y] if i is None else params[:, x + i:x + i + n]

        x_in = place("x_in", [128, KD, T], "RA")
        x_sq = place("x_sq", [128, KD, T], "RA", 8 * T)
        av = place("av", [128, KD, T], "RA")
        au = place("au", [128, KD, T], "RA", 8 * T)
        a_sq = place("a_sq", [128, KD, T], "RA", 16 * T)
        av_tok = place("av_tok", [128, NCH, D], "RA", 16 * T)
        prob = place("prob", [128, NCH, NM], "RA")
        prob_t = place("prob_t", [128, 2, SEQ], "RA", 1024)
        kv_ring = place("kv_ring", [128, 4, 2048], "RA", 2048)
        w_ba = place("w_ba", [128, KD, 16], "RA", 10240)
        w_ba_h = place("w_ba_h", [128, KD, 16], "RA", 10368, F32R)
        w_ba_l = place("w_ba_l", [128, KD, 16], "RA", 10496, F32R)
        s_sc = place("s_sc", [128, 64], "RA", 10624)
        s_pr = place("s_pr", [32, NM], "RA", 10688)
        s_prt = place("s_prt", [128, 64], "RA", 10944)
        qkv = place("qkv", [128, 24, T], "RA")
        mem_h = place("mem_h", [128, KD, NM], "M", 0, F32R)
        mem_l = place("mem_l", [128, KD, NM], "M", 2048, F32R)
        mrg = place("mrg", [128, KD, T], "M")
        x1 = place("x1", [128, KD, T], "M")
        ws_t = place("ws_t", [128, NH, CH], "ZG")
        bs_row = place("bs_row", [1, NH, CH], "ZG", 1024)
        zg = place("zg", [128, KD, T], "ZG")
        h2 = place("h2", [128, KD, T], "ZG")
        ht_h = place("ht_h", [128, KD, T], "HT", 0, F32R)
        ht_l = place("ht_l", [128, KD, T], "HT", 8 * T, F32R)
        dl = [[place(f"dl{h}_{n}", [128, 4, 128], "HT", (11 * h + n) * 512) for n in range(11)]
              for h in range(2)]
        h2p = [place(f"h2p{i}", [TT, NT, D], "HT", i * NT * D // 2, BF16) for i in range(3)]
        h2r = [place(f"h2r{i}", [TT, D], "HT", 3 * NT * D // 2 + i * D) for i in range(2)]
        y_hi = place("y_hi", [128, D], "HT", 3 * NT * D // 2 + 2 * D, F32R)
        y_lo = place("y_lo", [128, D], "HT", 3 * NT * D // 2 + 3 * D, F32R)
        mem = place("mem", [128, KD, NM], "CQ")
        mem_sq = place("mem_sq", [128, KD, NM], "CQ", 2048)
        qc = place("qc", [128, KD, T], "CQ")
        xpad = [place(f"xpad{i}", [128, 528], "CQ", i * 528) for i in range(2)]
        cacc = [place(f"cacc{i}", [128, T], "CQ", 1056 + i * T) for i in range(2)]
        cvs = place("cvs", [128, 24, 4, NS], "CQ", 2112)
        cvs_sum = place("cvs_sum", [128, 24, NS], "CQ", 2880)
        l2sq = [place(f"l2sq{i}", [128, T], "CQ", i * T) for i in range(4)]
        l2rn = [place(f"l2rn{i}", [128, T], "CQ", (4 + i) * T) for i in range(4)]
        osq = [place(f"osq{i}", [128, T], "HT", (8 + i) * T) for i in range(4)]
        orn = [place(f"orn{i}", [128, T], "HT", (12 + i) * T) for i in range(4)]
        x_res = place("x_res", [128, KD, T], "CQ")
        mk = place("mk", [128, KD, NM], "MKV")
        mv = place("mv", [128, 2, D], "MKV", 2048)
        st = place("st", [128, NH, 128], "MKV")
        ext = place("ext", [128, 24, 4, NS], "MKV", 1024)
        convp = place("convp", [128, 24, 3], "MKV", 1792)
        w_r = place("w_r", [128, KD, NG + NE], "MKV")
        w_r_h = place("w_r_h", [128, KD, NG + NE], "MKV", 288, F32R)
        w_r_l = place("w_r_l", [128, KD, NG + NE], "MKV", 576, F32R)
        raw = [place(f"raw{i}", [128, KD, BLK], "RAW", 2048 * i) for i in range(2)]
        w_h = [place(f"w_h{i}", [128, KD, BLK], "SPL", 4096 * i, F32R) for i in range(2)]
        w_l = [place(f"w_l{i}", [128, KD, BLK], "SPL", 4096 * i + 2048, F32R) for i in range(2)]
        k_tok = place("k_tok", [NS, NH, 128], "RAW")
        u_tok = place("u_tok", [NS, NH, 128], "RAW", 1024)
        u_diag = [place(f"u_diag{i}", [NS, NS, 128], "RAW", 2048 + 1024 * i) for i in range(2)]
        s0 = place("s0", [128, NH, NS, 128], "SPL")
        fsq = place("fsq", [128, KD, T], "RA")
        e_gate = place("e_gate", [128, 2, KD, DE], "RA")
        e_up = place("e_up", [128, 2, KD, DE], "RAW")
        e_down = [place("e_down0", [128, DE // 128, D], "RA", 8192), place("e_down1", [128, DE // 128, D], "RAW", 8192)]
        moe_at = [0]

        def moe_buf(name, shape, dt=F32):
            t = place(name, shape, "MKV", 864 + moe_at[0], dt)
            moe_at[0] += (int(np.prod(shape[1:])) // (2 if dt == BF16 else 1) + 7) // 8 * 8
            assert moe_at[0] <= 4096 - 864
            return t

        lg = moe_buf("lg", [TT, NT, NG + NE])
        r8 = moe_buf("r8", [TT, NT, 8, 4])
        ing = moe_buf("ing", [TT, NT, EPG])
        ing2 = moe_buf("ing2", [TT, NT, EPG])
        oh1 = moe_buf("oh1", [TT, NT, EPG])
        oh2 = moe_buf("oh2", [TT, NT, EPG])
        w8 = moe_buf("w8", [TT, NT, EPG])
        prod32 = moe_buf("prod32", [TT, NT, NG, EPG])
        comb = moe_buf("comb", [TT, NT, NE])
        hit = moe_buf("hit", [TT, NT, NE])
        comb3 = moe_buf("comb3", [TT, NT, NE, 3], BF16)
        comb_r = moe_buf("comb_r", [TT, NT, NE])
        rank = moe_buf("rank", [TT, NT, NE + 2])
        cnt = moe_buf("cnt", [128, NE + 16])
        zoff = [0]

        def moe_z(name, shape, dt=F32):
            t = place(name, shape, "ZG", zoff[0], dt)
            zoff[0] += (int(np.prod(shape[1:])) // (2 if dt == BF16 else 1) + 7) // 8 * 8
            assert zoff[0] <= 8 * T, name
            return t

        sel = [moe_z(f"sel{i}", [TT, NT, 2, CAP], BF16) for i in range(2)]
        xt = moe_z("xt", [128, KD, 128])
        sg = moe_z("sg", [128, DE])
        act_r = moe_z("act_r", [128, DE])
        act_t = moe_z("act_t", [128, DE // 128, 128])
        slot_w = moe_z("slot_w", [128, 8])
        pair_w = moe_z("pair_w", [TT, NT, 2, 3], BF16)
        ident_b = moe_z("ident_b", [128, 128], BF16)
        sel_t = [moe_z("sel_t0", [128, T], F32R),
                 place("sel_t1", [128, T], "HT", 3 * NT * D // 2 + 4 * D, F32R)]
        fill = moe_z("fill", [1, 8])

        pp = [ctx.enter_context(nc.psum_tensor(f"pp{i}", [128, 2, 512], F32)) for i in range(4)]
        side = pp[3]
        bank = [[pp[2 * h + i // 2][:, i % 2, :].rearrange("p (u n) -> p u n", u=4) for i in range(4)]
                for h in range(2)]

        const_in = sem("const_in")
        x_loaded, mem_loaded, ws_loaded = sem("x_loaded"), sem("mem_loaded"), sem("ws_loaded")
        raw_loaded = [sem(f"raw_loaded{i}") for i in range(2)]
        hi_ready, lo_ready = sem("w_hi_ready"), sem("w_lo_ready")
        tile_mm = sem("tile_mm")
        psum_free = [sem(f"psum_free{i}") for i in range(3)]
        tile_act = sem("tile_act")
        sq_ready, sqrt_done = sem("sq_ready"), sem("sqrt_done")
        h_norm, h_hi, h_lo = sem("h_norm"), sem("h_hi"), sem("h_lo")
        side_mm, side_free = sem("side_mm"), sem("side_free")
        a_normed, a_sq_ready = sem("a_normed"), sem("a_sq_ready")
        wba_loaded, wba_hi, wba_split = sem("wba_loaded"), sem("wba_hi"), sem("wba_split")
        ws_masked = sem("ws_masked")
        g_step, g_act = sem("g_step"), sem("g_act")
        kv_loaded = [sem(f"kv_loaded{i}") for i in range(4)]
        kv_used = sem("kv_used")
        soft_max, soft_exp, soft_norm = sem("soft_max"), sem("soft_exp"), sem("soft_norm")
        out_mem, out_av, out_conv, out_st, out_y = (sem(n) for n in
                                                    ("out_mem", "out_av", "out_conv", "out_st", "out_y"))
        out_s0 = sem("out_s0")
        ext_loaded, ext_ready = sem("ext_loaded"), sem("ext_ready")
        conv_copy, conv_mul, conv_sum, conv_silu = (sem(n) for n in ("conv_copy", "conv_mul", "conv_sum",
                                                                     "conv_silu"))
        conv_zero, convs_sum, convs_silu, gc_added = (sem(n) for n in ("conv_zero", "convs_sum", "convs_silu",
                                                                       "gc_added"))
        l2_sq, l2_mm, l2_sqrt, l2_done = sem("l2_sq"), sem("l2_mm"), sem("l2_sqrt"), sem("l2_done")
        on_sq, on_mm, on_sqrt, on_done = sem("on_sq"), sem("on_mm"), sem("on_sqrt"), sem("on_done")
        s0_loaded = sem("s0_loaded")
        sd_rhs, sd_u, sd_o, sd_diag, sd_dec, sd_new = (sem(n) for n in ("sd_rhs", "sd_u", "sd_o", "sd_diag",
                                                                       "sd_dec", "sd_new"))
        delta_pe = [sem(f"delta_pe{i}") for i in range(2)]
        delta_dve = [sem(f"delta_dve{i}") for i in range(2)]
        delta_act = [sem(f"delta_act{i}") for i in range(2)]
        st_zero = sem("st_zero")
        xres_loaded, wr_loaded, wr_hi, wr_split = (sem(n) for n in
                                                   ("xres_loaded", "wr_loaded", "wr_hi", "wr_split"))
        x1_ready = sem("x1_ready")
        router_mm, ht_mm, ht_hi, ht_lo = sem("router_mm"), sem("ht_mm"), sem("ht_hi"), sem("ht_lo")
        lg_ready, lg_exp, hit_ready, rank_mm, rounds_set = (sem(n) for n in (
            "lg_ready", "lg_exp", "hit_ready", "rank_mm", "rounds_set"))
        eg_loaded, eu_loaded = sem("eg_loaded"), sem("eu_loaded")
        ed_loaded = [sem(f"ed_loaded{i}") for i in range(2)]
        sc_free = sem("sc_free")
        sel_ready, pair_w_ready, gather_mm, xt_ready = (sem(n) for n in ("sel_ready", "pair_w_ready",
                                                                         "gather_mm", "xt_ready"))
        slot_w_ready, y_hi_ready = sem("slot_w_ready"), sem("y_hi_ready")
        gate_mm, gu_mm, silu_done, act_ready = (sem(n) for n in ("gate_mm", "up_mm", "silu_done", "act_ready"))
        at_mm, at_out, y_mm, y_out = (sem(n) for n in ("act_turned_mm", "act_turned_out", "y_mm", "y_out"))
        selt_mm, selt_out, sc_mm = (sem(n) for n in ("sel_turned_mm", "sel_turned_out", "sc_mm"))
        ht_part = sem("ht_part")
        fin_mm, fin_sq, fin_done, rank_moved = (sem(n) for n in (
            "fin_mm", "fin_sq", "fin_done", "rank_moved"))
        dve_chain = sem("dve_chain")
        act_chain = sem("act_chain")

        QKV_DONE = 2 * NBLK
        block = ctx.enter_context(nc.Block())

        def pe_at(hh, c, step):
            return c * len(PE_STEPS) + PE_STEPS.index(step) + 1

        def dve_at(hh, c, step):
            return c * len(DVE_STEPS) + DVE_STEPS.index(step) + 1

        def act_at(hh, c, step):
            return c * len(ACT_STEPS) + ACT_STEPS.index(step) + 1

        def kind(j):
            return BLOCK_KIND[j // 2], j - 2 * FIRST_BLOCK[BLOCK_KIND[j // 2]]

        def out_of_psum(eng, j):
            eng.wait_ge(psum_free[j % 3], j // 3 + 1)

        @block.sync
        def _(sp):
            def load_block(b):
                if b >= 2:
                    sp.wait_ge(lo_ready, b - 1)
                sp.dma_start(raw[b % 2][:], a["w_blk"][b].rearrange("p (k n) -> p k n", k=KD))\
                    .then_inc(raw_loaded[b % 2], 16)

            def load_kv(n):
                if n >= 4:
                    sp.wait_ge(kv_used, n - 3)
                src = a["cache_k"][n] if n < NS else a["cache_v"][n - NS]
                sp.dma_start(kv_ring[:, n % 4, :], src).then_inc(kv_loaded[n % 4], 16)

            def pair(w, e, n):
                return a[w][bass.ds(e, n)].rearrange("o p (k n) -> p o k n", o=n, n=DE if w != "w_down" else D)

            def load_pair(e, used=None):
                if used is not None:
                    sp.wait_ge(gate_mm, used)
                sp.dma_start(e_gate[:], pair("w_gate", e, 2)).then_inc(eg_loaded, 16)
                if used is not None:
                    sp.wait_ge(gu_mm, used)
                else:
                    sp.wait_ge(tile_mm, 2 * NBLK)
                sp.dma_start(e_up[:], pair("w_up", e, 2)).then_inc(eu_loaded, 16)
                if used is not None:
                    sp.wait_ge(y_mm, 2 * used)
                for i in range(2):
                    sp.dma_start(e_down[i][:], pair("w_down", e + i, 1)[:, 0]).then_inc(ed_loaded[i], 16)

            sp.dma_start(consts[:], a["consts"]).then_inc(const_in, 16)
            sp.dma_start(params[:], a["params"]).then_inc(const_in, 16)
            sp.dma_start(x_in[:], a["x_t"].rearrange("p (k n) -> p k n", k=KD)).then_inc(x_loaded, 16)
            sp.dma_start(mem[:], a["mem_t"].rearrange("p (k n) -> p k n", k=KD)).then_inc(mem_loaded, 16)
            load_block(0)
            load_block(1)
            sp.dma_start(ws_t[:], a["ws_t"].rearrange("p (k n) -> p k n", k=NH)).then_inc(ws_loaded, 16)
            sp.dma_start(bs_row[:], a["bs"].rearrange("p (k n) -> p k n", k=NH)).then_inc(ws_loaded, 16)
            for ev in SCHEDULE:
                if ev[0] == "tile":
                    j = ev[1]
                    b = j // 2
                    if j % 2 == 0 and 2 <= b + 2 < WO_BLOCK:
                        load_block(b + 2)
                    if j == 15:
                        sp.wait_ge(a_normed, 8)
                        sp.dma_start(o["av"].rearrange("p (k n) -> p k n", k=KD), av[:, :, SEQ:T])\
                            .then_inc(out_av, 16)
                    if j == 31:
                        for i in range(29, 32):
                            out_of_psum(sp, i)
                        sp.dma_start(o["mk"].rearrange("p (k n) -> p k n", k=KD), mk[:]).then_inc(out_mem, 16)
                        sp.dma_start(o["mv"].rearrange("p (k n) -> p k n", k=2), mv[:]).then_inc(out_mem, 16)
                    if j == 39:
                        for i in range(37, 40):
                            out_of_psum(sp, i)
                        sp.wait_ge(out_av, 16)
                        sp.dma_start(w_ba[:], a["w_ba"].rearrange("p (k n) -> p k n", k=KD))\
                            .then_inc(wba_loaded, 16)
                        for n in range(4):
                            load_kv(n)
                    if j == QKV_TILE - 1:
                        sp.wait_ge(side_free, SIDE[("p_value", MH - 1)] + 1)
                        sp.wait_ge(out_mem, 32)
                        sp.dma_start(ext[:, :, 0:3, :],
                                     a["state_conv"].rearrange("p (t j b) -> p t j b", t=24, j=3))\
                            .then_inc(ext_loaded, 16)
                elif ev[0] in ("s_score", "s_value"):
                    n = ev[1] + (NS if ev[0] == "s_value" else 0)
                    if n + 4 < 2 * NS:
                        load_kv(n + 4)
                elif ev[0] == "conv_s":
                    sp.wait_ge(ext_ready, 24)
                    sp.dma_start(o["conv_s"].rearrange("p (t j b) -> p t j b", t=24, j=3), ext[:, :, 1:4, :])\
                        .then_inc(out_conv, 16)
                    sp.dma_start(o["conv_p"].rearrange("p (t j) -> p t j", t=24), convp[:]).then_inc(out_conv, 16)
                    sp.wait_ge(tile_mm, WO_TILE)
                    sp.dma_start(s0[:], a["state_gdn"].rearrange("p (h b n) -> p h b n", h=NH, b=NS))\
                        .then_inc(s0_loaded, 16)
                elif ev == ("sd_outer", NH - 1):
                    sp.wait_ge(sd_new, NH)
                    sp.dma_start(o["gdn_s"].rearrange("p (h b n) -> p h b n", h=NH, b=NS), s0[:])\
                        .then_inc(out_s0, 16)
                    load_block(WO_BLOCK)
                    load_block(WO_BLOCK + 1)
                elif ev[0] == "delta" and ev[1] == NCH - 1:
                    for hh in range(2):
                        sp.wait_ge(delta_dve[hh], dve_at(hh, NCH - 1, "s"))
                        sp.wait_ge(delta_pe[hh], pe_at(hh, NCH - 1, "ss"))
                    sp.dma_start(o["gdn_p"].rearrange("p (h n) -> p h n", h=NH), st[:]).then_inc(out_st, 16)
                    sp.dma_start(x_res[:], a["x_t"].rearrange("p (k n) -> p k n", k=KD))\
                        .then_inc(xres_loaded, 16)
                    sp.wait_ge(out_st, 16)
                    sp.dma_start(w_r[:], a["w_router"].rearrange("p (k n) -> p k n", k=KD))\
                        .then_inc(wr_loaded, 16)
            load_block(WO_BLOCK + 2)
            load_block(WO_BLOCK + 3)
            sp.wait_ge(on_done, 8)
            sp.wait_ge(out_conv, 16 * 2)
            load_pair(0)
            with sp.Fori(1, NPAIR) as p:
                load_pair(p * 2, p)
            sp.wait_ge(rounds_set, 1)
            rounds = sp.value_load(n_rounds[0:1, 0:1], min_val=1, max_val=9)
            with sp.If(rounds > 1):
                with sp.Fori(1, rounds) as r:
                    with sp.Fori(0, NPAIR) as p:
                        load_pair(p * 2, r * NPAIR + p)
            for k in range(KD):
                sp.wait_ge(fin_done, k + 1)
                sp.dma_start(o["y"][:, k * T:(k + 1) * T], x1[:, k, :]).then_inc(out_y, 16)
            sp.wait_ge(out_y, 16 * KD)
            sp.wait_ge(out_mem, 32)
            sp.wait_ge(out_av, 16)
            sp.wait_ge(out_st, 16)
            sp.wait_ge(out_conv, 32)
            sp.wait_ge(out_s0, 16)

        @block.tensor
        def _(pe):
            mm = nc.tensor.matmul

            def begin(ev):
                n = SIDE[ev]
                if n:
                    pe.wait_ge(side_free, n)

            def sum_rows(out, src, ready, base_count, n, start=0):
                for k in range(KD):
                    pe.wait_ge(ready, base_count + k + 1)
                    for hf in range(2):
                        w = n // 2
                        last = mm(out[:, hf, 0:w], const("ones"), src[:, k, hf * w:(hf + 1) * w],
                                  start=(k == 0), stop=(k == KD - 1))
                return last

            def tile(j):
                b, i = j // 2, j % 2
                what, _t = kind(j)
                s = b % 2
                ps = pp[j % 3]
                if i == 0:
                    pe.wait_ge(lo_ready, b + 1)
                if j >= WO_TILE + 3:
                    pe.wait_ge(x1_ready, j - WO_TILE - 2)
                elif j >= 3 and j < WO_TILE:
                    pe.wait_ge(psum_free[j % 3], j // 3)
                need = {"mk": 16, "mv": 16, "wo": 24}.get(what, 8)
                pe.wait_ge(h_lo, need)
                if what == "mv":
                    ms = slice(i * 128, (i + 1) * 128)
                    n = 0
                    for k in range(KD):
                        for m_, w_ in ((mem_h, w_h), (mem_h, w_l), (mem_l, w_h)):
                            last = mm(ps[:, 0, 0:BLK], m_[:, k, ms], w_[s][:, k, :],
                                      start=(n == 0), stop=(n == 3 * KD - 1))
                            n += 1
                    last.then_inc(tile_mm, 1)
                    return
                cs = slice(i * 128, (i + 1) * 128)
                if what == "mk":
                    moving = [(ps[:, 0, 0:NM], slice(0, NM))]
                    xh, xl = mem_h, mem_l
                else:
                    moving = [(ps[:, hf, 0:HALF], slice(hf * HALF, (hf + 1) * HALF)) for hf in range(2)]
                    xh, xl = ht_h, ht_l
                for k in range(KD):
                    for q, (w_, x_) in enumerate(((w_h, xh), (w_h, xl), (w_l, xh))):
                        for dst, ts in moving:
                            last = mm(dst, w_[s][:, k, cs], x_[:, k, ts],
                                      start=(k == 0 and q == 0), stop=(k == KD - 1 and q == 2))
                last.then_inc(tile_mm, 1)

            def delta(c):
                cs = slice(c * CH, (c + 1) * CH)

                def each(step, fn):
                    for hh in range(2):
                        last = fn(hh)
                        last.then_inc(delta_pe[hh], 1)

                def wd(hh, step, cc=c):
                    pe.wait_ge(delta_dve[hh], dve_at(hh, cc, step))

                def wa(hh, step, cc=c):
                    pe.wait_ge(delta_act[hh], act_at(hh, cc, step))

                def four(hh, out, lhs, rhs):
                    for u in range(4):
                        last = mm(out[:, u, :], lhs(4 * hh + u, u), rhs(4 * hh + u, u), start=True, stop=True)
                    return last

                def q_(h):
                    return qkv[:, h, cs]

                def k_(h):
                    return qkv[:, NH + h, cs]

                def v_(h):
                    return qkv[:, 2 * NH + h, cs]

                def turn(hh, out, src):
                    for u in range(4):
                        last = nc.tensor.transpose(out[:, u, :], src(4 * hh + u, u), const("ident"))
                    return last

                def grow(hh):
                    if c:
                        wa(hh, "u", c - 1)
                    return four(hh, bank[hh][0], lambda h, u: gate_g[:, c, h:h + 1].to_broadcast([128, 128]),
                                lambda h, u: const("triu"))

                def brow(hh):
                    if c:
                        wd(hh, "o", c - 1)
                    return four(hh, bank[hh][1], lambda h, u: beta[:, c, h:h + 1].to_broadcast([128, 128]),
                                lambda h, u: const("ident"))

                def kk(hh):
                    if c:
                        wd(hh, "s", c - 1)
                    return four(hh, bank[hh][2], lambda h, u: k_(h), lambda h, u: k_(h))

                def kq(hh):
                    if c:
                        wa(hh, "nw", c - 1)
                    return four(hh, bank[hh][3], lambda h, u: k_(h), lambda h, u: q_(h))

                def turn_k(hh):
                    wd(hh, "arg")
                    wa(hh, "eg")
                    return turn(hh, bank[hh][0], lambda h, u: k_(h))

                def turn_v(hh):
                    wd(hh, "bs")
                    return turn(hh, bank[hh][1], lambda h, u: v_(h))

                def turn_u(hh):
                    wd(hh, "u1")
                    return turn(hh, bank[hh][2], lambda h, u: dl[hh][3][:, u, :])

                if c == 0:
                    pe.wait_ge(side_free, len(SIDE))
                    pe.wait_ge(l2_sqrt, 2 * NH)
                each("grow", grow)
                each("brow", brow)
                each("kk", kk)
                each("kq", kq)
                each("turn_k", turn_k)
                each("turn_v", turn_v)
                each("turn_u", turn_u)
                for l in range(6):
                    def m_t(hh):
                        if l == 0:
                            wa(hh, "t1")
                        else:
                            wd(hh, f"tu{l - 1}")
                        return four(hh, bank[hh][2], lambda h, u: dl[hh][1][:, u, :],
                                    lambda h, u: dl[hh][2][:, u, :])

                    def t_x(hh):
                        wd(hh, f"x{l}")
                        if l == 0:
                            wd(hh, "at")
                        four(hh, bank[hh][3], lambda h, u: dl[hh][3][:, u, :],
                             lambda h, u: dl[hh][4][:, u, :])
                        return four(hh, bank[hh][2], lambda h, u: dl[hh][4][:, u, :],
                                    lambda h, u: dl[hh][3][:, u, :])

                    each(f"mt{l}", m_t)
                    each(f"tx{l}", t_x)

                def wk(hh):
                    wd(hh, "tu5")
                    wa(hh, "vb")
                    return four(hh, bank[hh][3], lambda h, u: dl[hh][5][:, u, :],
                                lambda h, u: dl[hh][3][:, u, :])

                def uu(hh):
                    wa(hh, "nw")
                    if c:
                        wd(hh, "s", c - 1)
                    else:
                        pe.wait_ge(st_zero, 1)
                    for u in range(4):
                        mm(bank[hh][0][:, u, :], dl[hh][3][:, u, :], dl[hh][7][:, u, :], start=True, stop=False)
                        last = mm(bank[hh][0][:, u, :], dl[hh][9][:, u, :], st[:, 4 * hh + u, :],
                                  start=False, stop=True)
                    return last

                def oo(hh):
                    wa(hh, "u")
                    wd(hh, "qg")
                    for u in range(4):
                        mm(bank[hh][1][:, u, :], st[:, 4 * hh + u, :], dl[hh][8][:, u, :], start=True, stop=False)
                        last = mm(bank[hh][1][:, u, :], dl[hh][10][:, u, :], dl[hh][0][:, u, :],
                                  start=False, stop=True)
                    return last

                def ss(hh):
                    return four(hh, bank[hh][2], lambda h, u: dl[hh][6][:, u, :],
                                lambda h, u: dl[hh][10][:, u, :])

                each("wk", wk)
                each("uu", uu)
                each("oo", oo)
                each("ss", ss)

            def gather(n, j):
                pe.wait_ge(sel_ready, n + 1)
                for k in range(KD):
                    i = 0
                    for t in range(NT):
                        for src in h2p:
                            last = mm(pp[0][:, k // 4, (k % 4) * 128:(k % 4 + 1) * 128],
                                      src[:, t, k * 128:(k + 1) * 128], sel[j][:, t, :, :],
                                      start=(i == 0), stop=(i == 3 * NT - 1))
                            i += 1
                last.then_inc(gather_mm, 1)

            def scatter(n, j, s0_, s1_):
                for s in range(s0_, s1_):
                    dc, hf = s // 2, s % 2
                    pe.wait_ge(sc_free, n * SC + s + 1)
                    for part in (y_hi, y_lo):
                        last = mm(pp[3][:, s % 2, 0:HALF], part[:, dc * 128:(dc + 1) * 128],
                                  sel_t[1 - j][:, hf * HALF:(hf + 1) * HALF],
                                  start=(part is y_hi), stop=(part is y_lo))
                    last.then_inc(sc_mm, 1)

            def two(out, lhs, w0, w1, start, stop):
                for i, w in enumerate((w0, w1)):
                    rows = slice(i * CAP, (i + 1) * CAP)
                    last = mm(out[rows], lhs[:, rows], w, start=start, stop=stop, skip_group_check=True)
                return last

            def experts(n, j):
                pe.wait_ge(xt_ready, n + 1)
                pe.wait_ge(eg_loaded, (n + 1) * 16)
                for k in range(KD):
                    last = two(pp[1][:, 0, :], xt[:, k, :], e_gate[:, 0, k, :], e_gate[:, 1, k, :],
                               k == 0, k == KD - 1)
                    if k == KD - 1:
                        last.then_inc(gate_mm, 1)
                    if k == 2:
                        pe.wait_ge(y_out, n + 1)
                    if k >= 3:
                        scatter(n, j, k - 3, k - 2)
                pe.wait_ge(eu_loaded, (n + 1) * 16)
                for k in range(KD):
                    last = two(pp[1][:, 1, :], xt[:, k, :], e_up[:, 0, k, :], e_up[:, 1, k, :],
                               k == 0, k == KD - 1)
                    if k == KD - 1:
                        last.then_inc(gu_mm, 1)
                    scatter(n, j, KD - 3 + k, KD - 2 + k)
                pe.wait_ge(pair_w_ready, n + 1)
                pe.wait_ge(silu_done, n + 1)
                for t in range(NT):
                    one = sel[j][:, t, :, :].rearrange("p a n -> p (a n)")
                    mm(pp[1][:, 0, 0:6], one, pair_w[:, t, :, :].rearrange("p a n -> p (a n)"),
                       start=(t == 0), stop=(t == NT - 1))
                for t in range(NT):
                    one = sel[j][:, t, :, :].rearrange("p a n -> p (a n)")
                    dst = pp[2][:, 0, t * TT:(t + 1) * TT] if t < 4 else pp[2][:, 1, 0:TT]
                    last = mm(dst, one, ident_b[0:TT, 0:TT], start=True, stop=True)
                last.then_inc(selt_mm, 1)
                gather(n + 1, 1 - j)
                pe.wait_ge(act_ready, n + 1)
                for f in range(DE // 128):
                    last = nc.tensor.transpose(pp[1][:, 0, f * 128:(f + 1) * 128], act_r[:, f * 128:(f + 1) * 128],
                                               const("ident"))
                last.then_inc(at_mm, 1)
                scatter(n, j, SC - 3, SC)
                pe.wait_ge(at_out, n + 1)
                pe.wait_ge(selt_out, n + 1)
                for i in range(2):
                    pe.wait_ge(ed_loaded[i], (n + 1) * 16)
                for hf in range(2):
                    cs = slice(hf * 512, (hf + 1) * 512)
                    for f in range(DE // 128):
                        last = two(pp[2][:, hf, :], act_t[:, f, :], e_down[0][:, f, cs], e_down[1][:, f, cs],
                                   f == 0, f == DE // 128 - 1)
                    last.then_inc(y_mm, 1)

            pe.wait_ge(const_in, 32)
            for ev in SCHEDULE:
                e = ev[0]
                if e == "tile":
                    tile(ev[1])
                elif e == "x_sumsq":
                    begin(ev)
                    sum_rows(side, x_sq, sq_ready, 0, T).then_inc(side_mm, 1)
                elif e == "m_sumsq":
                    begin(ev)
                    sum_rows(side, mem_sq, sq_ready, 8, NM).then_inc(side_mm, 1)
                elif e == "a_sumsq":
                    begin(ev)
                    sum_rows(side, a_sq, a_sq_ready, 0, T).then_inc(side_mm, 1)
                elif e == "a_turn":
                    begin(ev)
                    pe.wait_ge(a_normed, 8)
                    c = ev[1]
                    for g in range(NH):
                        last = nc.tensor.transpose(side[:, g // 4, (g % 4) * 128:(g % 4 + 1) * 128],
                                                   av[:, g, c * CH:(c + 1) * CH], const("ident"))
                    last.then_inc(side_mm, 1)
                elif e == "a_mix":
                    begin(ev)
                    pe.wait_ge(ws_masked, 1)
                    pe.wait_ge(side_free, SIDE[("a_turn", NCH - 1)] + 1)
                    for i in range(2):
                        g = ev[1] + i
                        ob = side[:, i, :].rearrange("p (c n) -> p c n", c=NCH)
                        mm(ob, const("ones", 1), bs_row[0:1, g:g + 1, :].to_broadcast([1, NCH, CH]),
                           start=True, stop=False)
                        for c in range(NCH):
                            last = mm(ob[:, c, :], av_tok[:, c, g * 128:(g + 1) * 128], ws_t[:, g, :],
                                      start=False, stop=(c == NCH - 1))
                    last.then_inc(side_mm, 1)
                elif e == "ba":
                    begin(ev)
                    pe.wait_ge(wba_split, 1)
                    for t in range(NT):
                        ts = slice(t * CH, min((t + 1) * CH, T))
                        rows = ts.stop - ts.start
                        n = 0
                        for k in range(KD):
                            for x_, w_ in ((ht_h, w_ba_h), (ht_h, w_ba_l), (ht_l, w_ba_h)):
                                last = mm(side[0:rows, 0, t * 16:(t + 1) * 16], x_[:, k, ts], w_[:, k, :],
                                          start=(n == 0), stop=(n == 3 * KD - 1))
                                n += 1
                    last.then_inc(side_mm, 1)
                elif e == "cumsum":
                    begin(ev)
                    pe.wait_ge(g_step, 3)
                    gp = gate_g[:, 0:NCH, :].rearrange("p c h -> p (c h)")
                    mm(side[:, 0, 0:32], const("triu"), gp, start=True, stop=True)
                    mm(side[:, 0, 32:64], const("ones"), gp, start=True, stop=True).then_inc(side_mm, 1)
                elif e == "s_score":
                    b = ev[1]
                    if b == 0:
                        begin(("s_score",))
                        [out_of_psum(pe, i) for i in range(45, 48)]
                    pe.wait_ge(kv_loaded[b % 4], 16 * (b // 4 + 1))
                    for h in range(MH):
                        for mt in range(2):
                            for dc in range(2):
                                kt = kv_ring[:, b % 4, :].rearrange("p (k n) -> p k n", k=KD)
                                col = mt * 32 + h * NS + b
                                last = mm(side[:, 0, col:col + 1],
                                          kt[:, 2 * h + dc, mt * 128:(mt + 1) * 128],
                                          qc[:, 2 * h + dc, SEQ + b:SEQ + b + 1], start=(dc == 0), stop=(dc == 1))
                    last.then_inc(kv_used, 1)
                elif e == "s_rows":
                    begin(ev)
                    for mt in range(2):
                        last = nc.tensor.transpose(side[0:32, 1, mt * 128:(mt + 1) * 128],
                                                   s_sc[:, mt * 32:(mt + 1) * 32], const("ident"))
                    last.then_inc(side_mm, 1)
                elif e == "s_cols":
                    begin(ev)
                    pe.wait_ge(soft_norm, 1)
                    for mt in range(2):
                        last = nc.tensor.transpose(side[:, 0, mt * 32:(mt + 1) * 32],
                                                   s_pr[:, mt * 128:(mt + 1) * 128], const("ident", 32)[:, 0:32])
                    last.then_inc(side_mm, 1)
                elif e == "s_value":
                    b = ev[1]
                    if b == 0:
                        begin(("s_value",))
                    pe.wait_ge(kv_loaded[b % 4], 16 * ((b + NS) // 4 + 1))
                    vt = kv_ring[:, b % 4, :].rearrange("p (m n) -> p m n", m=2)
                    for k in range(KD):
                        for mt in range(2):
                            col = mt * 32 + (k // 2) * NS + b
                            last = mm(side[:, 1, k * NS + b:k * NS + b + 1], vt[:, mt, k * 128:(k + 1) * 128],
                                      s_prt[:, col:col + 1], start=(mt == 0), stop=(mt == 1))
                    last.then_inc(kv_used, 1)
                elif e == "p_score":
                    begin(ev)
                    h = ev[1]
                    for c in range(NCH):
                        dst = side[:, c // 2, (c % 2) * NM:(c % 2 + 1) * NM]
                        for dc in range(2):
                            last = mm(dst, qc[:, 2 * h + dc, c * CH:(c + 1) * CH], mk[:, 2 * h + dc, :],
                                      start=(dc == 0), stop=(dc == 1))
                    last.then_inc(side_mm, 1)
                elif e == "p_turn":
                    begin(ev)
                    h = ev[1]
                    pe.wait_ge(soft_norm, h + 2)
                    for mt in range(2):
                        for c in range(NCH):
                            last = nc.tensor.transpose(side[:, mt, c * CH:(c + 1) * CH],
                                                       prob[:, c, mt * 128:(mt + 1) * 128], const("ident"))
                    last.then_inc(side_mm, 1)
                elif e == "p_value":
                    begin(ev)
                    h = ev[1]
                    for dc in range(2):
                        for mt in range(2):
                            cc = (2 * h + dc) * 128
                            last = mm(side[:, dc, :], mv[:, mt, cc:cc + 128], prob_t[:, mt, :],
                                      start=(mt == 0), stop=(mt == 1))
                    last.then_inc(side_mm, 1)
                elif e == "l2":
                    t = ev[1]
                    if t < 3:
                        pe.wait_ge(psum_free[t], WO_TILE // 3)
                    if t == 3:
                        pe.wait_ge(side_free, SIDE[("p_value", MH - 1)] + 1)
                    if t >= 4:
                        pe.wait_ge(l2_sqrt, t - 3)
                    pe.wait_ge(l2_sq, t + 1)
                    for hf in range(2):
                        last = mm(pp[t % 4][:, hf, 0:HALF], const("ones"),
                                  l2sq[t % 4][:, hf * HALF:(hf + 1) * HALF], start=True, stop=True)
                    last.then_inc(l2_mm, 1)
                elif e == "sd_bcast":
                    begin(ev)
                    pe.wait_ge(l2_sqrt, 16)
                    pe.wait_ge(sd_rhs, 2)
                    mm(side[:, 0, 0:2 * NS * NH], const("ones", NS), s_rhs[:].rearrange("b a c h -> b (a c h)"),
                       start=True, stop=True)
                    mm(side[:, 1, 0:NS * NH], const("ones"), s_qk[:].rearrange("p h b -> p (h b)"),
                       start=True, stop=True).then_inc(side_mm, 1)
                elif e == "sd_state":
                    begin(ev)
                    pe.wait_ge(s0_loaded, 16)
                    for h in range(NH):
                        for b in range(NS):
                            c0 = (h * NS + b) * 2
                            last = mm(side[:, 0, c0:c0 + 2], s0[:, h, b, :],
                                      qkv[:, h:h + NH + 1:NH, SEQ + b], start=True, stop=True)
                    last.then_inc(side_mm, 1)
                elif e in ("sd_ktok", "sd_utok"):
                    begin(ev)
                    if e == "sd_utok":
                        pe.wait_ge(sd_u, 1)
                    for h in range(NH):
                        src = s_u[:, h, :] if e == "sd_utok" else qkv[:, NH + h, SEQ:T]
                        last = nc.tensor.transpose(side[0:NS, h // 4, (h % 4) * 128:(h % 4 + 1) * 128], src,
                                                   const("ident"))
                    last.then_inc(side_mm, 1)
                elif e == "sd_outer":
                    begin(ev)
                    h = ev[1]
                    pe.wait_ge(sd_diag, h + 1)
                    pe.wait_ge(side_free, SIDE[("sd_ktok",)] + 1)
                    for i in range(2):
                        last = mm(side[:, i, :], k_tok[:, h, :], u_diag[h % 2][:, 4 * i:4 * i + 4, :],
                                  start=True, stop=True)
                    last.then_inc(side_mm, 1)
                elif e == "delta":
                    delta(ev[1])
                elif e == "o_norm":
                    h = ev[1]
                    if h < 4:
                        for hh in range(2):
                            pe.wait_ge(delta_dve[hh], dve_at(hh, NCH - 1, "s"))
                    else:
                        pe.wait_ge(on_sqrt, h - 3)
                    pe.wait_ge(on_sq, h + 1)
                    for hf in range(2):
                        last = mm(pp[h % 4][:, hf, 0:HALF], const("ones"),
                                  osq[h % 4][:, hf * HALF:(hf + 1) * HALF], start=True, stop=True)
                    last.then_inc(on_mm, 1)
                elif e == "f_sumsq":
                    pe.wait_ge(x1_ready, 8)
                    sum_rows(pp[3], h2, sq_ready, 16, T).then_inc(fin_mm, 1)
                elif e == "router":
                    pe.wait_ge(wr_split, 1)
                    pe.wait_ge(h_lo, 32)
                    for t in range(NT):
                        n = 0
                        ts = slice(t * TT, (t + 1) * TT)
                        for k in range(KD):
                            for x_, w_ in ((ht_h, w_r_h), (ht_h, w_r_l), (ht_l, w_r_h)):
                                last = mm(pp[0][0:TT, 0, t * 36:(t + 1) * 36], x_[:, k, ts], w_[:, k, :],
                                          start=(n == 0), stop=(n == 3 * KD - 1))
                                n += 1
                    last.then_inc(router_mm, 1)
                elif e == "h_turn":
                    for t in range(NT):
                        if t >= 3:
                            pe.wait_ge(ht_lo, t - 2)
                        for k in range(KD):
                            last = nc.tensor.transpose(
                                pp[1 + t % 3][0:TT, k // 4, (k % 4) * 128:(k % 4 + 1) * 128],
                                h2[:, k, t * TT:(t + 1) * TT], const("ident"))
                        last.then_inc(ht_mm, 1)
                elif e == "rank":
                    pe.wait_ge(hit_ready, 1)
                    for t in range(NT):
                        for s in range(t + 1):
                            left = const("strict", TT)[:, 0:TT] if s == t else const("ones", TT)[:, 0:TT]
                            mm(pp[0][0:TT, 1, t * NE:(t + 1) * NE], left, hit[:, s, :],
                               start=(s == 0), stop=(s == t))
                    for s in range(NT):
                        last = mm(pp[0][:, 1, 160:160 + NE], const("ones", TT), hit[:, s, :],
                                  start=(s == 0), stop=(s == NT - 1))
                    last.then_inc(rank_mm, 1)
                elif e == "moe":
                    pe.wait_ge(ht_lo, NT)
                    pe.wait_ge(rounds_set, 1)
                    rounds = pe.value_load(n_rounds[0:1, 0:1], min_val=1, max_val=9)
                    gather(0, 0)
                    with pe.Fori(0, rounds) as r:
                        with pe.Fori(0, NPAIR // 2) as p:
                            for j in range(2):
                                experts((r * (NPAIR // 2) + p) * 2 + j, j)
                    pe.wait_ge(y_out, rounds * NPAIR + 1)
                    scatter(rounds * NPAIR, 0, 0, SC)
                elif e == "final":
                    sum_rows(pp[0], fsq, fin_sq, 0, T).then_inc(fin_mm, 1)

        @block.scalar
        def _(act):
            fn = nc.scalar.activation
            chain = [0]

            def link(ins):
                chain[0] += 1
                ins.then_inc(act_chain, 1)
                act.wait_ge(act_chain, chain[0])

            def split_hi(b):
                act.wait_ge(raw_loaded[b % 2], 16 * (b // 2 + 1))
                if b >= 2:
                    act.wait_ge(tile_mm, 2 * (b - 1))
                fn(w_h[b % 2][:], raw[b % 2][:], ACT.Copy).then_inc(hi_ready, 1)

            def squares(dst, src, done):
                for k in range(KD):
                    fn(dst[:, k, :], src[:, k, :], ACT.Square).then_inc(done, 1)

            def root_mean(ps, n, w):
                dst = rstd[:, 0:w].rearrange("p (a n) -> p a n", a=2)
                return fn(dst, ps[:, :, 0:w // 2], ACT.Sqrt, bias=const("eps"), scale=1.0 / n)

            def tile(j):
                what, t = kind(j)
                b = j // 2
                if j % 2 == 0 and b + 1 < (WO_BLOCK if b < WO_BLOCK else NBLK) and b + 1 != WO_BLOCK + 1:
                    split_hi(b + 1)
                ps = pp[j % 3][:, :, 0:HALF]

                def whole(x):
                    return x.rearrange("p (a n) -> p a n", a=2)

                if what in ("av", "au"):
                    act.wait_ge(tile_mm, j + 1)
                    dst = av if what == "av" else au
                    fn(whole(dst[:, t, :]), ps, ACT.Gelu_apprx_tanh).then_inc(psum_free[j % 3], 1)
                elif what in ("ga", "gc"):
                    act.wait_ge(tile_mm, j + 1)
                    fn(ps, ps, ACT.Sigmoid, bias=param("b_gate", t + (16 if what == "gc" else 0)))\
                        .then_inc(tile_act, 1)
                elif what == "gb":
                    act.wait_ge(tile_mm, j + 1)
                    fn(whole(zg[:, t, :]), ps, ACT.Sigmoid, bias=param("b_gate", t + 8))\
                        .then_inc(psum_free[j % 3], 1)
                elif what == "z":
                    act.wait_ge(tile_mm, j + 1)
                    fn(ps, ps, ACT.Silu).then_inc(tile_act, 1)
                elif what == "qkv":
                    act.wait_ge(tile_mm, j + 1)
                    act.wait_ge(conv_zero, 1)
                    if t == 0:
                        act.wait_ge(gc_added, 8)
                    if t >= 2:
                        act.wait_ge(conv_sum, t - 1)
                        act.wait_ge(ext_ready, t - 1)
                    fn(whole(xpad[t % 2][:, 3:3 + T]), ps, ACT.Copy).then_inc(conv_copy, 1)
                    if t >= 2:
                        act.wait_ge(conv_silu, t - 1)
                    fn(whole(cacc[t % 2][:, :]), ps, ACT.Copy, scale=param("w_conv", 4 * t + 3))\
                        .then_inc(psum_free[j % 3], 1)
                    if t >= 1:
                        act.wait_ge(conv_sum, t)
                        fn(qkv[:, t - 1, 0:SEQ], cacc[(t - 1) % 2][:, 0:SEQ], ACT.Silu).then_inc(conv_silu, 1)

            act.wait_ge(const_in, 32)
            for ev in SCHEDULE:
                e = ev[0]
                if e == "tile":
                    tile(ev[1])
                elif e == "x_sumsq":
                    act.wait_ge(x_loaded, 16)
                    squares(x_sq, x_in, sq_ready)
                    split_hi(0)
                    act.wait_ge(side_mm, SIDE_MM[ev])
                    root_mean(side, D, T).then_inc(side_free, 1)
                    for k in range(KD):
                        act.wait_ge(h_norm, k + 1)
                        fn(ht_h[:, k, :], x_in[:, k, :], ACT.Copy).then_inc(h_hi, 1)
                elif e == "m_sumsq":
                    act.wait_ge(mem_loaded, 16)
                    squares(mem_sq, mem, sq_ready)
                    act.wait_ge(side_mm, SIDE_MM[ev])
                    root_mean(side, D, NM).then_inc(side_free, 1)
                    for k in range(KD):
                        act.wait_ge(h_norm, 8 + k + 1)
                        fn(mem_h[:, k, :], mem[:, k, :], ACT.Copy).then_inc(h_hi, 1)
                elif e == "a_sumsq":
                    act.wait_ge(side_mm, SIDE_MM[ev])
                    root_mean(side, D, T).then_inc(side_free, 1)
                elif e == "a_turn":
                    act.wait_ge(side_mm, SIDE_MM[ev])
                    fn(av_tok[:, ev[1], :].rearrange("p (a n) -> p a n", a=2), side[:], ACT.Copy)\
                        .then_inc(side_free, 1)
                elif e == "ba":
                    act.wait_ge(wba_loaded, 16)
                    fn(w_ba_h[:], w_ba[:], ACT.Copy).then_inc(wba_hi, 1)
                    link(fn(neg_a[:], param("a_log"), ACT.Exp))
                    act.wait_ge(g_step, 1)
                    for rows, ts in ((128, slice(0, 4)), (NS, slice(4, 5))):
                        x, y = tmp_g[0:rows, 0, ts, :], tmp_g[0:rows, 1, ts, :]
                        link(fn(y, x, ACT.Abs))
                        link(fn(y, y, ACT.Exp, scale=-1.0))
                        fn(y, y, ACT.Ln, bias=1.0).then_inc(g_act, 1)
                    for rows, ts in ((128, slice(0, 4)), (NS, slice(4, 5))):
                        fn(beta[0:rows, ts, :], ba[0:rows, ts, 0:NH], ACT.Sigmoid).then_inc(g_act, 1)
                elif e == "cumsum":
                    act.wait_ge(g_step, 5)
                    fn(dec_end[:].rearrange("p c h -> p (c h)"), side[:, 0, 32:64], ACT.Exp).then_inc(g_act, 1)
                    fn(dec_kb[:], cum_g[:], ACT.Exp).then_inc(g_act, 1)
                    fn(dec_kd[:], dec_kd[:], ACT.Exp).then_inc(g_act, 1)
                    fn(s_eg[:], gate_g[0:NS, 4, :], ACT.Exp).then_inc(g_act, 1)
                elif e == "s_rows":
                    act.wait_ge(soft_max, 1)
                    fn(s_pr[:], side[0:32, 1, 0:NM], ACT.Exp, bias=s_small[:, 1:2], scale=1.0 / 16,
                       accum_out=s_small[:, 2:3]).then_inc(soft_exp, 1)
                elif e == "p_score":
                    h = ev[1]
                    act.wait_ge(soft_max, h + 2)
                    sp_ = side[:].rearrange("p a (c m) -> p (a c) m", c=2)
                    for c in range(NCH):
                        fn(prob[:, c, :], sp_[:, c, :], ACT.Exp, bias=small[:, 1, c:c + 1], scale=1.0 / 16,
                           accum_out=small[:, 2, c:c + 1]).then_inc(soft_exp, 1)
                elif e == "p_turn":
                    act.wait_ge(side_mm, SIDE_MM[ev])
                    fn(prob_t[:], side[:], ACT.Copy).then_inc(side_free, 1)
                elif e == "conv_s":
                    act.wait_ge(conv_sum, 24)
                    fn(qkv[:, 23, 0:SEQ], cacc[1][:, 0:SEQ], ACT.Silu).then_inc(conv_silu, 1)
                    act.wait_ge(convs_sum, 1)
                    fn(qkv[:, :, SEQ:T], cvs_sum[:], ACT.Silu).then_inc(convs_silu, 1)
                elif e == "l2":
                    t = ev[1]

                    def l2_square(t):
                        if t >= 4:
                            act.wait_ge(l2_mm, t - 3)
                        fn(l2sq[t % 4][:], qkv[:, t, :], ACT.Square).then_inc(l2_sq, 1)

                    if t == 0:
                        act.wait_ge(conv_silu, 24)
                        act.wait_ge(convs_silu, 1)
                        l2_square(0)
                        l2_square(1)
                    if t + 2 < 2 * NH:
                        l2_square(t + 2)
                    act.wait_ge(l2_mm, t + 1)
                    if t >= 4:
                        act.wait_ge(l2_done, t - 3)
                    is_q = t < NH
                    fn(l2rn[t % 4][:].rearrange("p (a n) -> p a n", a=2), pp[t % 4][:, :, 0:HALF], ACT.Sqrt,
                       bias=const("eps128" if is_q else "eps"), scale=128.0 if is_q else 1.0)\
                        .then_inc(l2_sqrt, 1)
                elif e == "sd_ktok":
                    act.wait_ge(side_mm, SIDE_MM[ev])
                    fn(k_tok[:].rearrange("p h n -> p (h n)").rearrange("p (a n) -> p a n", a=2), side[0:NS],
                       ACT.Copy).then_inc(side_free, 1)
                elif e == "delta":
                    c = ev[1]

                    def wp(hh, step, cc=c):
                        act.wait_ge(delta_pe[hh], pe_at(hh, cc, step))

                    for hh in range(2):
                        act.wait_ge(delta_dve[hh], dve_at(hh, c, "arg"))
                        fn(dl[hh][8][:], bank[hh][0], ACT.Exp).then_inc(delta_act[hh], 1)
                    for hh in range(2):
                        act.wait_ge(delta_dve[hh], dve_at(hh, c, "arg"))
                        fn(dl[hh][0][:], dl[hh][0][:], ACT.Exp).then_inc(delta_act[hh], 1)
                    for hh in range(2):
                        wp(hh, "turn_k")
                        for step, w_, dst in (("kb", dec_kb, 5), ("kd", dec_kd, 6)):
                            for u in range(4):
                                last = fn(dl[hh][dst][:, u, :], bank[hh][0][:, u, :], ACT.Copy,
                                          scale=w_[:, c, 4 * hh + u:4 * hh + u + 1])
                            last.then_inc(delta_act[hh], 1)
                        wp(hh, "turn_v")
                        for u in range(4):
                            last = fn(dl[hh][7][:, u, :], bank[hh][1][:, u, :], ACT.Copy,
                                      scale=beta[:, c, 4 * hh + u:4 * hh + u + 1])
                        last.then_inc(delta_act[hh], 1)
                    for hh in range(2):
                        wp(hh, "turn_u")
                        fn(dl[hh][2][:], bank[hh][2], ACT.Copy).then_inc(delta_act[hh], 1)
                    for hh in range(2):
                        wp(hh, "wk")
                        fn(dl[hh][9][:], bank[hh][3], ACT.Copy, scale=-1.0).then_inc(delta_act[hh], 1)
                    for hh in range(2):
                        wp(hh, "uu")
                        fn(dl[hh][10][:], bank[hh][0], ACT.Copy).then_inc(delta_act[hh], 1)
                elif e == "o_norm":
                    h = ev[1]

                    def o_square(h):
                        if h >= 4:
                            act.wait_ge(on_mm, h - 3)
                        fn(osq[h % 4][:], qkv[:, h, :], ACT.Square).then_inc(on_sq, 1)

                    if h == 0:
                        for hh in range(2):
                            act.wait_ge(delta_dve[hh], dve_at(hh, NCH - 1, "s"))
                            act.wait_ge(delta_pe[hh], pe_at(hh, NCH - 1, "ss"))
                        act.wait_ge(sd_o, 1)
                        o_square(0)
                        o_square(1)
                    if h + 2 < NH:
                        o_square(h + 2)
                    act.wait_ge(on_mm, h + 1)
                    if h >= 4:
                        act.wait_ge(on_done, h - 3)
                    fn(orn[h % 4][:].rearrange("p (a n) -> p a n", a=2), pp[h % 4][:, :, 0:HALF], ACT.Sqrt,
                       bias=const("eps"), scale=1.0 / 128).then_inc(on_sqrt, 1)
                elif e == "m_split":
                    act.wait_ge(out_s0, 16)
                    split_hi(WO_BLOCK)
                    split_hi(WO_BLOCK + 1)
                    for k in range(KD):
                        act.wait_ge(on_done, k + 1)
                        fn(ht_h[:, k, :], mrg[:, k, :], ACT.Copy).then_inc(h_hi, 1)
                    act.wait_ge(wr_loaded, 16)
                    fn(w_r_h[:], w_r[:], ACT.Copy).then_inc(wr_hi, 1)
                elif e == "f_sumsq":
                    for k in range(KD):
                        act.wait_ge(x1_ready, k + 1)
                        fn(h2[:, k, :], x1[:, k, :], ACT.Square).then_inc(sq_ready, 1)
                    act.wait_ge(fin_mm, 1)
                    root_mean(pp[3], D, T).then_inc(sqrt_done, 1)
                    for k in range(KD):
                        act.wait_ge(h_norm, 16 + k + 1)
                        fn(ht_h[:, k, :], h2[:, k, :], ACT.Copy).then_inc(h_hi, 1)
                elif e == "router":
                    act.wait_ge(lg_ready, 1)
                    link(fn(r8[:, :, 4:8, 0], r8[:, :, 4:8, 1], ACT.Exp))
                    fn(r8[:, :, 0:1, 3], r8[:, :, 0:1, 2], ACT.Exp).then_inc(lg_exp, 1)
                elif e == "h_turn":
                    act.wait_ge(router_mm, 1)
                    for t in range(NT):
                        act.wait_ge(ht_mm, t + 1)
                        fn(h2p[0][:, t, :].rearrange("p (a n) -> p a n", a=2), pp[1 + t % 3][0:TT], ACT.Copy)\
                            .then_inc(ht_hi, 1)
                        act.wait_ge(ht_part, t + 1)
                        fn(h2p[1][:, t, :], h2r[t % 2][:], ACT.Copy).then_inc(ht_hi, 1)
                elif e == "moe":
                    act.wait_ge(rounds_set, 1)
                    rounds = act.value_load(n_rounds[0:1, 0:1], min_val=1, max_val=9)

                    def tokens(n):
                        act.wait_ge(gather_mm, n + 1)
                        fn(xt[:].rearrange("p (a k) n -> p a (k n)", a=2), pp[0][:], ACT.Copy).then_inc(xt_ready, 1)

                    tokens(0)
                    with act.Fori(0, rounds) as r:
                        with act.Fori(0, NPAIR // 2) as p:
                            for j in range(2):
                                n = (r * (NPAIR // 2) + p) * 2 + j
                                act.wait_ge(gate_mm, n + 1)
                                fn(sg[:], pp[1][:, 0, :], ACT.Silu).then_inc(silu_done, 1)
                                act.wait_ge(selt_mm, n + 1)
                                fn(sel_t[j][:, 0:4 * TT], pp[2][:, 0, 0:4 * TT], ACT.Copy)
                                fn(sel_t[j][:, 4 * TT:T], pp[2][:, 1, 0:TT], ACT.Copy).then_inc(selt_out, 1)
                                tokens(n + 1)
                                act.wait_ge(at_mm, n + 1)
                                fn(act_t[:].rearrange("p a n -> p (a n)"), pp[1][:, 0, :], ACT.Copy)\
                                    .then_inc(at_out, 1)
                                act.wait_ge(slot_w_ready, n + 1)
                                for hf in range(2):
                                    act.wait_ge(y_mm, n * 2 + hf + 1)
                                    fn(y_hi[:, hf * 512:(hf + 1) * 512], pp[2][:, hf, :], ACT.Copy,
                                       scale=slot_w[:, 0:1]).then_inc(y_hi_ready, 1)
                elif e == "final":
                    for k in range(KD):
                        act.wait_ge(x1_ready, 8 + k + 1)
                        fn(fsq[:, k, :], x1[:, k, :], ACT.Square).then_inc(fin_sq, 1)
                    act.wait_ge(fin_mm, 2)
                    root_mean(pp[0], D, T).then_inc(sqrt_done, 1)

        @block.gpsimd
        def _(pool):
            tt = nc.gpsimd.tensor_tensor

            pool.wait_ge(const_in, 32)
            for ev in SCHEDULE:
                e = ev[0]
                if e == "tile":
                    j = ev[1]
                    what, t = kind(j)
                    b = j // 2
                    if what == "av":
                        out_of_psum(pool, j)
                        tt(a_sq[:, t, :], av[:, t, :], av[:, t, :], ALU.mult).then_inc(a_sq_ready, 1)
                    elif what == "gc":
                        out_of_psum(pool, j)
                        tt(mrg[:, t, :], mrg[:, t, :], qc[:, t, :], ALU.add).then_inc(gc_added, 1)
                        if t == 7:
                            pool.wait_ge(gc_added, 8)
                            for i in range(2):
                                last = nc.gpsimd.memset(xpad[i][:, 0:3], 0.0)
                            last.then_inc(conv_zero, 1)
                            nc.gpsimd.memset(st[:], 0.0).then_inc(st_zero, 1)
                    elif what == "qkv":
                        pool.wait_ge(conv_copy, t + 1)
                        nc.gpsimd.tensor_copy(convp[:, t, :], xpad[t % 2][:, SEQ:SEQ + 3])
                        nc.gpsimd.tensor_copy(ext[:, t, 3, :], xpad[t % 2][:, 3 + SEQ:3 + T]).then_inc(ext_ready, 1)
                elif e == "x_sumsq":
                    pool.wait_ge(ws_loaded, 32)
                    tt(ws_t[:], ws_t[:], const("triu").rearrange("p (o n) -> p o n", o=1)
                       .to_broadcast([128, NH, CH]), ALU.mult).then_inc(ws_masked, 1)
                elif e == "ba":
                    pool.wait_ge(wba_hi, 1)
                    tt(w_ba_l[:], w_ba[:], w_ba_h[:].bitcast(F32), ALU.subtract).then_inc(wba_split, 1)
                elif e == "sd_outer":
                    h = ev[1]
                    if h == 0:
                        pool.wait_ge(side_free, SIDE[("sd_state",)] + 1)
                    tt(s0[:, h, :, :], s0[:, h, :, :], s_bc[:, 1, :, h:h + 1].to_broadcast([128, NS, 128]),
                       ALU.mult).then_inc(sd_dec, 1)
                elif e == "m_split":
                    pool.wait_ge(wr_hi, 1)
                    tt(w_r_l[:], w_r[:], w_r_h[:].bitcast(F32), ALU.subtract).then_inc(wr_split, 1)

        @block.vector
        def _(dve):
            tt = nc.vector.tensor_tensor
            ts_ = nc.vector.tensor_scalar
            stt = nc.vector.scalar_tensor_tensor
            copy = nc.vector.tensor_copy
            chain = [0]

            def link(ins):
                chain[0] += 1
                ins.then_inc(dve_chain, 1)
                dve.wait_ge(dve_chain, chain[0])

            def weights_lo(b):
                dve.wait_ge(hi_ready, b + 1)
                tt(w_l[b % 2][:], raw[b % 2][:], w_h[b % 2][:].bitcast(F32), ALU.subtract).then_inc(lo_ready, 1)

            def normed(dst, src, gain, n, done):
                for k in range(KD):
                    stt(dst[:, k, :], src[:, k, :], param(gain, k), rstd[:, 0:n], ALU.mult, ALU.mult)\
                        .then_inc(done, 1)

            def split_lo(lo, hi, src, at):
                for k in range(KD):
                    dve.wait_ge(h_hi, at + k + 1)
                    tt(lo[:, k, :], src[:, k, :], hi[:, k, :].bitcast(F32), ALU.subtract).then_inc(h_lo, 1)

            def tile(j):
                what, t = kind(j)
                b = j // 2
                if j % 2 == 0 and b + 1 < (WO_BLOCK if b < WO_BLOCK else NBLK) and b + 1 != WO_BLOCK + 1:
                    weights_lo(b + 1)
                ps = pp[j % 3][:, :, 0:HALF]
                free = psum_free[j % 3]

                def whole(x):
                    return x.rearrange("p (a n) -> p a n", a=2)

                if what in ("mk", "mv", "qm", "wo"):
                    dve.wait_ge(tile_mm, j + 1)
                if what == "mk":
                    copy(mk[:, t, :], pp[j % 3][:, 0, 0:NM]).then_inc(free, 1)
                elif what == "mv":
                    copy(mv[:, t % 2, (t // 2) * BLK:(t // 2 + 1) * BLK], pp[j % 3][:, 0, 0:BLK]).then_inc(free, 1)
                elif what == "ga":
                    dve.wait_ge(tile_act, t + 1)
                    tt(whole(mrg[:, t, :]), ps, whole(au[:, t, :]), ALU.mult).then_inc(free, 1)
                elif what == "qm":
                    copy(whole(qc[:, t, :]), ps).then_inc(free, 1)
                elif what == "z":
                    dve.wait_ge(tile_act, 8 + t + 1)
                    out_of_psum(dve, j - 8)
                    stt(whole(zg[:, t, :]), ps, param("norm_gdn"), whole(zg[:, t, :]), ALU.mult, ALU.mult)\
                        .then_inc(free, 1)
                elif what == "gc":
                    dve.wait_ge(tile_act, 16 + t + 1)
                    dve.wait_ge(side_free, SIDE[("p_value", t // 2)] + 1)
                    tt(whole(qc[:, t, :]), ps, whole(qc[:, t, :]), ALU.mult).then_inc(free, 1)
                elif what == "qkv":
                    out_of_psum(dve, j)
                    c_, x_ = cacc[t % 2], xpad[t % 2]
                    for tap in range(3):
                        ins = stt(c_[:, 0:SEQ], x_[:, tap:tap + SEQ], param("w_conv", 4 * t + tap), c_[:, 0:SEQ],
                                  ALU.mult, ALU.add)
                        if tap < 2:
                            link(ins)
                        else:
                            ins.then_inc(conv_sum, 1)
                elif what == "wo":
                    dve.wait_ge(xres_loaded, 16)
                    tt(whole(x1[:, t, :]), ps, whole(x_res[:, t, :]), ALU.add).then_inc(x1_ready, 1)

            dve.wait_ge(const_in, 32)
            for ev in SCHEDULE:
                e = ev[0]
                if e == "tile":
                    tile(ev[1])
                elif e == "x_sumsq":
                    dve.wait_ge(side_free, SIDE[ev] + 1)
                    link(nc.vector.reciprocal(rstd[:], rstd[:]))
                    weights_lo(0)
                    normed(x_in, x_in, "norm_mix", T, h_norm)
                    split_lo(ht_l, ht_h, x_in, 0)
                elif e == "m_sumsq":
                    dve.wait_ge(side_free, SIDE[ev] + 1)
                    link(nc.vector.reciprocal(rstd[:, 0:NM], rstd[:, 0:NM]))
                    normed(mem, mem, "norm_mem", NM, h_norm)
                    split_lo(mem_l, mem_h, mem, 8)
                elif e == "a_sumsq":
                    dve.wait_ge(side_free, SIDE[ev] + 1)
                    link(nc.vector.reciprocal(rstd[:], rstd[:]))
                    normed(av, av, "norm_a_v", T, a_normed)
                elif e == "a_mix":
                    g = ev[1]
                    if g == 0:
                        dve.wait_ge(a_normed, 8)
                        for i in range(13, 16):
                            out_of_psum(dve, i)
                        link(tt(s_tmp[:], av[:, :, SEQ:T],
                                param("ws00").rearrange("p (g o) -> p g o", o=1).to_broadcast([128, NH, NS]), ALU.mult))
                        link(tt(s_tmp[:], s_tmp[:],
                                param("bs0").rearrange("p (g o) -> p g o", o=1).to_broadcast([128, NH, NS]), ALU.add))
                        link(tt(au[:, :, SEQ:T], au[:, :, SEQ:T], s_tmp[:], ALU.mult))
                    dve.wait_ge(side_mm, SIDE_MM[ev])
                    tt(au[:, g:g + 2, 0:SEQ], side[:], au[:, g:g + 2, 0:SEQ], ALU.mult).then_inc(side_free, 1)
                elif e == "ba":
                    dve.wait_ge(side_mm, SIDE_MM[ev])
                    copy(ba[:, 0:4, :].rearrange("p c n -> p (c n)"), side[:, 0, 0:64])
                    copy(ba[0:NS, 4, :], side[0:NS, 0, 64:80]).then_inc(side_free, 1)
                    dve.wait_ge(side_free, SIDE[ev] + 1)
                    for rows, ts in ((128, slice(0, 4)), (NS, slice(4, 5))):
                        n = ts.stop - ts.start
                        last = tt(tmp_g[0:rows, 0, ts, :], ba[0:rows, ts, NH:2 * NH],
                                  param("dt_bias")[0:rows].rearrange("p (o h) -> p o h", o=1)
                                  .to_broadcast([rows, n, NH]), ALU.add)
                    last.then_inc(g_step, 1)
                    dve.wait_ge(g_act, 2)
                    for rows, ts in ((128, slice(0, 4)), (NS, slice(4, 5))):
                        n = ts.stop - ts.start
                        link(stt(tmp_g[0:rows, 0, ts, :], tmp_g[0:rows, 0, ts, :], 0.0, tmp_g[0:rows, 1, ts, :],
                                 ALU.max, ALU.add))
                        stt(gate_g[0:rows, ts, :], tmp_g[0:rows, 0, ts, :], -1.0,
                            neg_a[0:rows].rearrange("p (o h) -> p o h", o=1).to_broadcast([rows, n, NH]),
                            ALU.mult, ALU.mult).then_inc(g_step, 1)
                elif e == "cumsum":
                    dve.wait_ge(side_mm, SIDE_MM[ev])
                    flat = cum_g[:].rearrange("p c h -> p (c h)")
                    copy(flat, side[:, 0, 0:32]).then_inc(g_step, 1)
                    dve.wait_ge(g_step, 4)
                    tt(dec_kd[:].rearrange("p c h -> p (c h)"), side[:, 0, 32:64], flat, ALU.subtract)\
                        .then_inc(g_step, 1)
                    dve.wait_ge(g_act, 8)
                    tt(dec_kb[:], dec_kb[:], beta[:, 0:NCH, :], ALU.mult).then_inc(side_free, 1)
                elif e == "s_score":
                    if ev[1] == NS - 1:
                        dve.wait_ge(kv_used, NS)
                        copy(s_sc[:], side[:, 0, 0:64]).then_inc(side_free, 1)
                elif e == "s_rows":
                    dve.wait_ge(side_mm, SIDE_MM[ev])
                    link(nc.vector.tensor_reduce(s_small[:, 0:1], side[0:32, 1, 0:NM], AX.X, ALU.max))
                    ts_(s_small[:, 1:2], s_small[:, 0:1], -1.0 / 16, None, ALU.mult).then_inc(soft_max, 1)
                    dve.wait_ge(soft_exp, 1)
                    link(nc.vector.reciprocal(s_small[:, 3:4], s_small[:, 2:3]))
                    ts_(s_pr[:], s_pr[:], s_small[:, 3:4], None, ALU.mult).then_inc(soft_norm, 1)
                    nc.vector.memset(s_small[:, 0:1], 0.0).then_inc(side_free, 1)
                elif e == "s_cols":
                    dve.wait_ge(side_mm, SIDE_MM[ev])
                    copy(s_prt[:], side[:, 0, 0:64]).then_inc(side_free, 1)
                elif e == "s_value":
                    if ev[1] == NS - 1:
                        dve.wait_ge(kv_used, 2 * NS)
                        copy(qc[:, :, SEQ:T], side[:, 1, 0:64].rearrange("p (k b) -> p k b", k=KD))\
                            .then_inc(side_free, 1)
                elif e == "p_score":
                    h = ev[1]
                    dve.wait_ge(side_mm, SIDE_MM[ev])
                    link(nc.vector.tensor_reduce(small[:, 0, :], side[:].rearrange("p a (c m) -> p (a c) m", c=2),
                                                 AX.X, ALU.max))
                    ts_(small[:, 1, :], small[:, 0, :], -1.0 / 16, None, ALU.mult).then_inc(soft_max, 1)
                    dve.wait_ge(soft_exp, 1 + NCH * (h + 1))
                    link(nc.vector.reciprocal(small[:, 3, :], small[:, 2, :]))
                    tt(prob[:], prob[:], small[:, 3, :].rearrange("p (c o) -> p c o", o=1)
                       .to_broadcast([128, NCH, NM]), ALU.mult).then_inc(soft_norm, 1)
                    nc.vector.memset(small[:, 0, :], 0.0).then_inc(side_free, 1)
                elif e == "p_value":
                    dve.wait_ge(side_mm, SIDE_MM[ev])
                    h = ev[1]
                    copy(qc[:, 2 * h:2 * h + 2, 0:SEQ], side[:]).then_inc(side_free, 1)
                elif e == "conv_s":
                    dve.wait_ge(ext_loaded, 16)
                    dve.wait_ge(ext_ready, 24)
                    link(tt(cvs[:], ext[:], param("w_conv").rearrange("p (t j o) -> p t j o", t=24, o=1)
                            .to_broadcast([128, 24, 4, NS]), ALU.mult))
                    nc.vector.tensor_reduce(cvs_sum[:], cvs[:].rearrange("p t j b -> p t b j"), AX.X, ALU.add)\
                        .then_inc(convs_sum, 1)
                elif e == "l2":
                    t = ev[1]
                    dve.wait_ge(l2_sqrt, t + 1)
                    link(nc.vector.reciprocal(l2rn[t % 4][:], l2rn[t % 4][:]))
                    tt(qkv[:, t, :], qkv[:, t, :], l2rn[t % 4][:], ALU.mult).then_inc(l2_done, 1)
                elif e == "sd_bcast":
                    idb = const("ident", NS)[:, 0:NS].rearrange("p (c o) -> p c o", o=1).to_broadcast([NS, NS, NH])
                    for i, src in enumerate((beta[0:NS, 4, :], s_eg[:])):
                        last = tt(s_rhs[:, i, :, :], idb,
                                  src.rearrange("p (o h) -> p o h", o=1).to_broadcast([NS, NS, NH]), ALU.mult)
                    last.then_inc(sd_rhs, 1)
                    dve.wait_ge(l2_done, 16)
                    tt(s_qk[:], qkv[:, 0:NH, SEQ:T], qkv[:, NH:2 * NH, SEQ:T], ALU.mult).then_inc(sd_rhs, 1)
                    dve.wait_ge(side_mm, SIDE_MM[ev])
                    copy(s_bc[:].rearrange("p a c h -> p (a c h)"), side[:, 0, 0:2 * NS * NH])
                    copy(s_qk[:].rearrange("p h b -> p (h b)"), side[:, 1, 0:NS * NH]).then_inc(side_free, 1)
                elif e == "sd_state":
                    dve.wait_ge(side_free, SIDE[("sd_bcast",)] + 1)
                    dve.wait_ge(side_mm, SIDE_MM[ev])
                    sv = side[:, 0, 0:2 * NS * NH].rearrange("p (h b a) -> p a h b", h=NH, b=NS)
                    bb, eg = s_bc[:, 0, :, :].rearrange("p b h -> p h b"), s_bc[:, 1, :, :].rearrange("p b h -> p h b")
                    link(tt(s_u[:], sv[:, 1, :, :], eg, ALU.mult))
                    link(tt(s_u[:], qkv[:, 2 * NH:3 * NH, SEQ:T], s_u[:], ALU.subtract))
                    tt(s_u[:], s_u[:], bb, ALU.mult).then_inc(sd_u, 1)
                    link(tt(s_tmp[:], sv[:, 0, :, :], eg, ALU.mult))
                    dve.wait_ge(sd_u, 1)
                    link(tt(s_qk[:], s_qk[:], s_u[:], ALU.mult))
                    tt(qkv[:, 0:NH, SEQ:T], s_qk[:], s_tmp[:], ALU.add).then_inc(side_free, 1)
                elif e == "sd_utok":
                    dve.wait_ge(side_mm, SIDE_MM[ev])
                    copy(u_tok[:].rearrange("p h n -> p (h n)").rearrange("p (a n) -> p a n", a=2), side[0:NS])\
                        .then_inc(side_free, 1)
                elif e == "sd_outer":
                    h = ev[1]

                    def diag(h):
                        if h >= 2:
                            dve.wait_ge(side_mm, SIDE_MM[("sd_outer", h - 2)])
                        tt(u_diag[h % 2][:], u_tok[:, h:h + 1, :].to_broadcast([NS, NS, 128]),
                           const("ident", NS)[:, 0:NS].rearrange("p (c o) -> p c o", o=1)
                           .to_broadcast([NS, NS, 128]), ALU.mult).then_inc(sd_diag, 1)

                    if h == 0:
                        dve.wait_ge(side_free, SIDE[("sd_utok",)] + 1)
                        diag(0)
                    if h + 1 < NH:
                        diag(h + 1)
                    dve.wait_ge(side_mm, SIDE_MM[ev])
                    dve.wait_ge(sd_dec, h + 1)
                    tt(s0[:, h, :, :].rearrange("p (a b) n -> p a (b n)", a=2), side[:],
                       s0[:, h, :, :].rearrange("p (a b) n -> p a (b n)", a=2), ALU.add).then_inc(side_free, 1)
                    dve.wait_ge(side_free, SIDE[ev] + 1)
                    nc.vector.memset(small[:, 0, 0:1], 0.0).then_inc(sd_new, 1)
                    if h == 0:
                        nc.vector.memset(small[:, 0, 1:2], 0.0).then_inc(sd_o, 1)
                elif e == "delta":
                    c = ev[1]
                    cs = slice(c * CH, (c + 1) * CH)

                    def wp(hh, step, cc=c):
                        dve.wait_ge(delta_pe[hh], pe_at(hh, cc, step))

                    def wa(hh, step, cc=c):
                        dve.wait_ge(delta_act[hh], act_at(hh, cc, step))

                    def wide(mask):
                        return mask.rearrange("p (o n) -> p o n", o=1).to_broadcast([128, 4, 128])

                    for hh in range(2):
                        wp(hh, "grow")
                        if c:
                            wp(hh, "oo", c - 1)
                        for u in range(4):
                            h = 4 * hh + u
                            last = ts_(dl[hh][0][:, u, :], bank[hh][0][:, u, :], cum_g[:, c, h:h + 1], 0.0,
                                       ALU.subtract, ALU.min)
                        last.then_inc(delta_dve[hh], 1)
                    for hh in range(2):
                        wa(hh, "dt")
                        link(tt(dl[hh][1][:], dl[hh][0][:], wide(const("strict")), ALU.mult))
                        wp(hh, "brow")
                        tt(dl[hh][1][:], bank[hh][1], dl[hh][1][:], ALU.mult).then_inc(delta_dve[hh], 1)
                    for hh in range(2):
                        wp(hh, "kk")
                        dve.wait_ge(delta_dve[hh], dve_at(hh, c, "bs"))
                        tt(dl[hh][1][:], bank[hh][2], dl[hh][1][:], ALU.mult).then_inc(delta_dve[hh], 1)
                    for hh in range(2):
                        dve.wait_ge(delta_dve[hh], dve_at(hh, c, "mt"))
                        link(tt(dl[hh][4][:], dl[hh][1][:], wide(const("first_t")), ALU.mult))
                        tt(dl[hh][3][:], wide(const("ident")), dl[hh][4][:], ALU.subtract)\
                            .then_inc(delta_dve[hh], 1)
                    for hh in range(2):
                        link(tt(dl[hh][0][:], dl[hh][0][:], wide(const("triu")), ALU.mult))
                        wp(hh, "kq")
                        tt(dl[hh][0][:], bank[hh][3], dl[hh][0][:], ALU.mult).then_inc(delta_dve[hh], 1)
                    for hh in range(2):
                        wa(hh, "eg")
                        tt(dl[hh][8][:], qkv[:, 4 * hh:4 * hh + 4, cs], dl[hh][8][:], ALU.mult)\
                            .then_inc(delta_dve[hh], 1)
                    for l in range(6):
                        x, y = CONST["merge"]
                        mask = consts[:, x + l * 128:x + (l + 1) * 128]
                        for hh in range(2):
                            wp(hh, f"mt{l}")
                            tt(dl[hh][4][:], bank[hh][2], wide(mask), ALU.mult).then_inc(delta_dve[hh], 1)
                        for hh in range(2):
                            wp(hh, f"tx{l}")
                            tt(dl[hh][2][:], dl[hh][2][:], bank[hh][3], ALU.subtract)
                            tt(dl[hh][3][:], dl[hh][3][:], bank[hh][2], ALU.subtract).then_inc(delta_dve[hh], 1)
                    for hh in range(2):
                        wp(hh, "oo")
                        copy(qkv[:, 4 * hh:4 * hh + 4, cs], bank[hh][1]).then_inc(delta_dve[hh], 1)
                    for hh in range(2):
                        wp(hh, "ss")
                        if c == 0:
                            dve.wait_ge(st_zero, 1)
                        else:
                            dve.wait_ge(delta_dve[hh], dve_at(hh, c - 1, "s"))
                        for u in range(4):
                            h = 4 * hh + u
                            last = stt(st[:, h, :], st[:, h, :], dec_end[:, c, h:h + 1], bank[hh][2][:, u, :],
                                       ALU.mult, ALU.add)
                        last.then_inc(delta_dve[hh], 1)
                elif e == "o_norm":
                    h = ev[1]
                    dve.wait_ge(on_sqrt, h + 1)
                    link(nc.vector.reciprocal(orn[h % 4][:], orn[h % 4][:]))
                    link(tt(qkv[:, h, :], qkv[:, h, :], orn[h % 4][:], ALU.mult))
                    link(tt(qkv[:, h, :], qkv[:, h, :], zg[:, h, :], ALU.mult))
                    dve.wait_ge(gc_added, 8)
                    tt(mrg[:, h, :], mrg[:, h, :], qkv[:, h, :], ALU.add).then_inc(on_done, 1)
                elif e == "m_split":
                    weights_lo(WO_BLOCK)
                    weights_lo(WO_BLOCK + 1)
                    split_lo(ht_l, ht_h, mrg, 16)
                elif e == "f_sumsq":
                    dve.wait_ge(sqrt_done, 1)
                    link(nc.vector.reciprocal(rstd[:], rstd[:]))
                    normed(h2, x1, "norm_ffn", T, h_norm)
                    split_lo(ht_l, ht_h, h2, 24)
                elif e == "router":
                    dve.wait_ge(router_mm, 1)
                    link(tt(lg[:], pp[0][0:TT, 0, 0:180].rearrange("p (t n) -> p t n", t=NT),
                            param("b_router")[0:TT].rearrange("p (o n) -> p o n", o=1)
                            .to_broadcast([TT, NT, NG + NE]), ALU.add))
                    gl = lg[:, :, 0:NG]
                    g_top, g_first = r8[:, :, 0:1, 0], r8[:, :, 1:2, 0]
                    one4 = r8[:, :, 0:4, 1]

                    def wide(x, n):
                        return x.to_broadcast([TT, NT, n])

                    def first_top(one, src, top, tmp, desc, n):
                        d_ = const(desc, TT).rearrange("p (o n) -> p o n", o=1).to_broadcast([TT, NT, n])
                        link(nc.vector.tensor_reduce(top, src, AX.X, ALU.max))
                        link(tt(one, src, wide(top, n), ALU.is_equal))
                        link(tt(one, one, d_, ALU.mult))
                        link(nc.vector.tensor_reduce(tmp, one, AX.X, ALU.max))
                        link(tt(one, one, wide(tmp, n), ALU.is_equal))

                    first_top(one4, gl, g_top, g_first, "desc4", 4)
                    link(tt(prod32[:], lg[:, :, NG:].rearrange("p t (g x) -> p t g x", g=NG),
                            one4.rearrange("p t (g o) -> p t g o", o=1).to_broadcast([TT, NT, NG, EPG]), ALU.mult))
                    link(nc.vector.tensor_reduce(ing[:], prod32[:].rearrange("p t g x -> p t x g"), AX.X, ALU.add))
                    m1, m2, f1 = r8[:, :, 2:3, 0], r8[:, :, 3:4, 0], r8[:, :, 0:1, 3]
                    first_top(oh1[:], ing[:], m1, f1, "desc8", 8)
                    link(stt(ing2[:], oh1[:], -3.0e38, ing[:], ALU.mult, ALU.add))
                    first_top(oh2[:], ing2[:], m2, f1, "desc8", 8)
                    link(tt(r8[:, :, 0:1, 2], m2, m1, ALU.subtract))
                    tt(r8[:, :, 4:8, 1], gl, wide(g_top, 4), ALU.subtract).then_inc(lg_ready, 1)
                    dve.wait_ge(lg_exp, 1)
                    psum_, e2, w1, w2 = r8[:, :, 1:2, 2], r8[:, :, 0:1, 3], r8[:, :, 2:3, 2], r8[:, :, 3:4, 2]
                    link(nc.vector.tensor_reduce(psum_, r8[:, :, 4:8, 0], AX.X, ALU.add))
                    link(ts_(w1, e2, 1.0, None, ALU.add))
                    link(tt(w1, w1, psum_, ALU.mult))
                    link(nc.vector.reciprocal(w1, w1))
                    link(tt(w2, w1, e2, ALU.mult))
                    link(tt(w8[:], oh1[:], wide(w1, EPG), ALU.mult))
                    link(tt(ing2[:], oh2[:], wide(w2, EPG), ALU.mult))
                    link(tt(w8[:], w8[:], ing2[:], ALU.add))
                    link(tt(ing[:], oh1[:], oh2[:], ALU.add))
                    o4 = one4.rearrange("p t (g o) -> p t g o", o=1).to_broadcast([TT, NT, NG, EPG])

                    def over_groups(x):
                        return x[:].rearrange("p t (o x) -> p t o x", o=1).to_broadcast([TT, NT, NG, EPG])

                    link(tt(comb[:].rearrange("p t (g x) -> p t g x", g=NG), over_groups(w8), o4, ALU.mult))
                    tt(hit[:].rearrange("p t (g x) -> p t g x", g=NG), over_groups(ing), o4, ALU.mult)\
                        .then_inc(hit_ready, 1)
                elif e == "h_turn":
                    for t in range(NT):
                        dve.wait_ge(ht_hi, 2 * t + 1)
                        tt(h2r[t % 2][:].rearrange("p (a n) -> p a n", a=2), pp[1 + t % 3][0:TT],
                           h2p[0][:, t, :].rearrange("p (a n) -> p a n", a=2), ALU.subtract).then_inc(ht_part, 1)
                        dve.wait_ge(ht_hi, 2 * t + 2)
                        tt(h2p[2][:, t, :], h2r[t % 2][:], h2p[1][:, t, :], ALU.subtract).then_inc(ht_lo, 1)
                elif e == "rank":
                    dve.wait_ge(rank_mm, 1)
                    link(stt(rank[:, :, 0:NE], pp[0][0:TT, 1, 0:NT * NE].rearrange("p (t n) -> p t n", t=NT), 1.0,
                             hit[:], ALU.add, ALU.mult))
                    link(ts_(rank[:, :, 0:NE], rank[:, :, 0:NE], -1.0, None, ALU.add))
                    link(ts_(rank[:, :, NE:NE + 2], rank[:, :, 0:2], -float(CAP), None, ALU.add))
                    link(nc.vector.tensor_reduce(cnt[:, 0:1], pp[0][:, 1, 160:160 + NE], AX.X, ALU.max))
                    link(ts_(cnt[:, 8:16], const("rounds"), cnt[:, 0:1], None, ALU.is_lt))
                    link(nc.vector.tensor_reduce(cnt[:, 1:2], cnt[:, 8:16], AX.X, ALU.add))
                    ts_(n_rounds[0:1, 0:1], cnt[0:1, 1:2], 1.0, None, ALU.add).then_inc(rounds_set, 1)
                    copy(ident_b[:], const("ident"))
                    c3 = [comb3[:, :, :, i:i + 1].rearrange("p t e o -> p t (e o)") for i in range(3)]
                    link(copy(c3[0], comb[:]))
                    link(tt(comb_r[:], comb[:], c3[0], ALU.subtract))
                    link(copy(c3[1], comb_r[:]))
                    link(tt(c3[2], comb_r[:], c3[1], ALU.subtract))
                    nc.vector.memset(fill[:, 0:1], 0.0).then_inc(sc_free, 2)
                elif e == "moe":
                    dve.wait_ge(rounds_set, 1)
                    dve.wait_ge(ht_mm, NT)
                    rounds = dve.value_load(n_rounds[0:1, 0:1], min_val=1, max_val=9)
                    slots = const("slots", TT).rearrange("p (o a n) -> p o a n", o=1, a=1)\
                        .to_broadcast([TT, NT, 2, CAP])
                    for dst in (y_hi[:], y_lo[:], sel_t[1][:]):
                        last = ts_(dst, consts[:, 0:dst.shape[1]], 0.0, None, ALU.mult)
                    last.then_inc(y_out, 1)

                    def one_hot(n, j, ex):
                        at_ = rank[:, :, bass.ds(ex, 2)].rearrange("p t (e o) -> p t e o", o=1)
                        tt(sel[j][:], slots, at_.to_broadcast([TT, NT, 2, CAP]), ALU.is_equal).then_inc(sel_ready, 1)

                    def add_back(n, s0_, s1_):
                        for s in range(s0_, s1_):
                            dc, hf = s // 2, s % 2
                            dve.wait_ge(sc_mm, n * SC + s + 1)
                            xs = x1[:, dc, hf * HALF:(hf + 1) * HALF]
                            tt(xs, pp[3][:, s % 2, 0:HALF], xs, ALU.add).then_inc(sc_free, 1)

                    one_hot(0, 0, 0)
                    with dve.Fori(0, rounds) as r:
                        with dve.Fori(0, NPAIR // 2) as p:
                            for j in range(2):
                                n = (r * (NPAIR // 2) + p) * 2 + j
                                ex = p * 4 + j * 2
                                dve.wait_ge(gather_mm, n + 1)
                                one_hot(n + 1, 1 - j, ex + 2)
                                copy(pair_w[:], comb3[:, :, bass.ds(ex, 2), :]).then_inc(pair_w_ready, 1)
                                add_back(n, 0, SC - 3)
                                dve.wait_ge(selt_mm, n + 1)
                                for i in range(2):
                                    rows = slice(i * CAP, (i + 1) * CAP)
                                    last = nc.vector.tensor_reduce(slot_w[rows, 0:1], pp[1][rows, 0, 3 * i:3 * i + 3],
                                                                   AX.X, ALU.add)
                                last.then_inc(slot_w_ready, 1)
                                dve.wait_ge(silu_done, n + 1)
                                dve.wait_ge(gu_mm, n + 1)
                                tt(act_r[:], pp[1][:, 1, :], sg[:], ALU.mult).then_inc(act_ready, 1)
                                add_back(n, SC - 3, SC)
                                dve.wait_ge(slot_w_ready, n + 1)
                                for hf in range(2):
                                    dve.wait_ge(y_hi_ready, n * 2 + hf + 1)
                                    cs = slice(hf * 512, (hf + 1) * 512)
                                    last = stt(y_lo[:, cs], pp[2][:, hf, :], slot_w[:, 0:1], y_hi[:, cs].bitcast(F32),
                                               ALU.mult, ALU.subtract)
                                last.then_inc(y_out, 1)
                        dve.wait_ge(sel_ready, (r + 1) * NPAIR + 1)
                        ts_(rank[:], rank[:], -float(CAP), None, ALU.add).then_inc(rank_moved, 1)
                        dve.wait_ge(rank_moved, r + 1)
                    add_back(rounds * NPAIR, 0, SC)
                elif e == "final":
                    dve.wait_ge(sc_free, rounds * (NPAIR * SC) + 2 + SC)
                    nc.vector.memset(fill[:, 0:1], 0.0).then_inc(x1_ready, 8)
                    dve.wait_ge(sqrt_done, 2)
                    link(nc.vector.reciprocal(rstd[:], rstd[:]))
                    normed(x1, x1, "norm_final", T, fin_done)


def kernel(**inputs):
    import numpy as _np
    import concourse.bacc as _bacc
    from concourse.bass_utils import run_bass_kernel_spmd as _run

    f = {k: _np.asarray(v) for k, v in inputs.items()}

    def chunks(x):
        return x.reshape(x.shape[0], -1, 128).transpose(2, 1, 0)

    def cols(x):
        return x.reshape(-1, 128).T

    def everywhere(x):
        return _np.broadcast_to(x.reshape(1, -1), (128, x.size))

    w_in = f["w_in"][0]
    edge = _np.cumsum([0, D, D, 3 * D, D, NH, NH, D, D, D, D])
    part = {n: w_in[:, edge[i]:edge[i + 1]] for i, n in
            enumerate(("au", "av", "qkv", "z", "beta", "alpha", "qm", "ga", "gb", "gc"))}
    part["mk"], part["mv"] = f["w_mem_kv"][0][:, :D], f["w_mem_kv"][0][:, D:]
    part["wo"] = f["w_o"][0]
    w_blk = _np.concatenate([part[n].reshape(KD, 128, -1, BLK).transpose(2, 1, 0, 3) for n, _ in BLOCKS])
    kc = f["cache_mem_k"][0].reshape(NS, NM, MH, 2, 128).transpose(0, 4, 2, 3, 1)
    vc = f["cache_mem_v"][0].reshape(NS, 2, 128, D).transpose(0, 2, 1, 3)
    x = _np.concatenate([f["x_prompt"][0], f["x_sample"][:, 0]])
    par = _np.concatenate([
        cols(f["norm_mix"]), cols(f["norm_mem"]), cols(f["norm_ffn"]), cols(f["norm_final"]),
        cols(f["norm_a_v"]), f["norm_gdn_out"].T, cols(f["b_gate"]),
        f["w_conv"][0].reshape(4, 24, 128).transpose(2, 1, 0).reshape(128, 96),
        everywhere(f["w_s"][0, :, 0, 0]), everywhere(f["b_s"][0, :, 0]), everywhere(f["a_log"][0]),
        everywhere(f["dt_bias"][0]), everywhere(f["b_router_group"][0]), everywhere(f["b_router_expert"][0])],
        axis=1)

    def rows(w, n):
        return w.reshape(NE, n, 128, -1).transpose(0, 2, 1, 3).reshape(NE, 128, -1)

    arrays = {
        "consts": make_constants(), "params": par,
        "x_t": chunks(x).reshape(128, -1), "mem_t": chunks(f["mem_prompt"][0]).reshape(128, -1),
        "w_blk": w_blk.reshape(NBLK, 128, -1),
        "w_ba": _np.concatenate([part["beta"], part["alpha"]], 1).reshape(KD, 128, 16).transpose(1, 0, 2)
                   .reshape(128, -1),
        "ws_t": f["w_s"][0].transpose(2, 0, 1).reshape(128, -1), "bs": f["b_s"][0].reshape(1, -1),
        "cache_k": kc.reshape(NS, 128, -1), "cache_v": vc.reshape(NS, 128, -1),
        "state_conv": f["state_conv"][0].reshape(NS, 3, 24, 128).transpose(3, 2, 1, 0).reshape(128, -1),
        "state_gdn": f["state_gdn"][0].transpose(2, 1, 0, 3).reshape(128, -1),
        "w_router": _np.concatenate([f["w_router_group"][0], f["w_router_expert"][0]], 1)
                       .reshape(KD, 128, NG + NE).transpose(1, 0, 2).reshape(128, -1),
        "w_gate": rows(f["w_exp_gate"], KD), "w_up": rows(f["w_exp_up"], KD), "w_down": rows(f["w_exp_down"], 4),
    }
    arrays = {k: _np.ascontiguousarray(v) for k, v in arrays.items()}
    outs = {"y": KD * T, "av": KD * NS, "mk": KD * NM, "mv": 2 * D, "conv_s": 24 * 3 * NS, "conv_p": 24 * 3,
            "gdn_s": NH * NS * 128, "gdn_p": NH * 128}

    nc = _bacc.Bacc("TRN2", target_bir_lowering=False, num_devices=1)
    a = {k: nc.dram_tensor(f"in_{k}", v.shape, mybir.dt.from_np(v.dtype), kind="ExternalInput").ap()
         for k, v in arrays.items()}
    o = {k: nc.dram_tensor(f"out_{k}", (128, n), F32, kind="ExternalOutput").ap() for k, n in outs.items()}
    build_step(nc, a, o)
    got = _run(nc, [{f"in_{k}": v for k, v in arrays.items()}], core_ids=[0]).results[0]
    r = {k: got[f"out_{k}"] for k in outs}

    y = r["y"].reshape(128, KD, T).transpose(2, 1, 0).reshape(T, D)
    return (
        y[:SEQ].reshape(1, SEQ, D), y[SEQ:].reshape(NS, 1, D),
        r["mk"].reshape(128, KD, NM).transpose(2, 1, 0).reshape(1, 1, NM, MH, D // MH),
        r["mv"].reshape(128, 2, D).transpose(1, 0, 2).reshape(1, 1, NM, MH, D // MH),
        r["gdn_p"].reshape(128, NH, 128).transpose(1, 0, 2).reshape(1, 1, NH, 128, 128),
        r["conv_p"].reshape(128, 24, 3).transpose(2, 1, 0).reshape(1, 1, 3, 3 * D),
        r["gdn_s"].reshape(128, NH, NS, 128).transpose(2, 1, 0, 3).reshape(1, NS, NH, 128, 128),
        r["conv_s"].reshape(128, 24, 3, NS).transpose(3, 2, 1, 0).reshape(1, NS, 3, 3 * D),
        r["av"].reshape(128, KD, NS).transpose(2, 1, 0).reshape(1, NS, 1, D),
    )
```

```python
from contextlib import ExitStack

import numpy as np
import concourse.bass as bass
from concourse import mybir

F32 = mybir.dt.float32
F32R = mybir.dt.float32r
BF16 = mybir.dt.bfloat16
I32 = mybir.dt.int32
ALU = mybir.AluOpType
ACT = mybir.ActivationFunctionType
AX = mybir.AxisListType

D = 1024
SEQ = 512
NS = 8
T = SEQ + NS
HALF = T // 2
KD = D // 128
NM = 256
NH = 8
MH = 4
CH = 128
NCH = SEQ // CH
BLK = 256
NG, EPG = 4, 8
NE = NG * EPG
DE = 512
CAP = 64
TT, NT = 104, 5
EPS = 1e-6
NPAIR = NE // 2
SC = 2 * KD

BLOCKS = [("av", 4), ("au", 4), ("mk", 4), ("mv", 4), ("ga", 4), ("qm", 4), ("gb", 4), ("z", 4),
          ("gc", 4), ("qkv", 12), ("wo", 4)]
BLOCK_KIND = [name for name, n in BLOCKS for _ in range(n)]
FIRST_BLOCK = {name: BLOCK_KIND.index(name) for name, _ in BLOCKS}
NBLK = len(BLOCK_KIND)
WO_BLOCK = FIRST_BLOCK["wo"]
WO_TILE = 2 * WO_BLOCK
QKV_TILE = 2 * FIRST_BLOCK["qkv"]

CONST = {}
_at = 0
for _n, _w in [("ident", 128), ("ones", 128), ("triu", 128), ("strict", 128), ("first_t", 128),
               ("merge", 6 * 128), ("slots", CAP), ("rounds", 8), ("desc4", 4), ("desc8", 8),
               ("eps", 1),
               ("pick", 31), ("q_scale", 1), ("q_scale_all", 1)]:
    CONST[_n] = (_at, _at + _w)
    _at += _w
NCONST = _at
PARAM = {}
_at = 0
for _n, _w in [("norm_mix", 8), ("norm_mem", 8), ("norm_ffn", 8), ("norm_final", 8), ("norm_a_v", 8),
               ("norm_gdn", 1), ("b_gate", 24), ("w_conv", 96), ("ws00", 8), ("bs0", 8),
               ("a_log", 8), ("dt_bias", 8), ("b_router", NG + NE)]:
    PARAM[_n] = (_at, _at + _w)
    _at += _w
NPARAM = _at


def make_constants():
    c = np.zeros((128, NCONST), np.float32)
    p, f = np.arange(128)[:, None], np.arange(128)[None, :]

    def put(name, value):
        a, b = CONST[name]
        c[:, a:b] = value

    put("ident", p == f)
    put("ones", 1.0)
    put("triu", p <= f)
    put("strict", p < f)

    def below(s):
        return (p // (2 * s) == f // (2 * s)) & (p // s % 2 == 1) & (f // s % 2 == 0)

    put("first_t", below(1).T)
    put("merge", np.concatenate([below(s) for s in (2, 4, 8, 16, 32, 64)], axis=1))
    put("slots", np.arange(CAP))
    put("rounds", CAP * np.arange(1, 9))
    put("desc4", np.arange(4, 0, -1))
    put("desc8", np.arange(8, 0, -1))
    put("eps", EPS)
    put("pick", np.arange(31) == 15)
    put("q_scale", np.where(p < NH, -0.5 * np.log(128.0), 0.0))
    put("q_scale_all", -0.5 * np.log(128.0))
    return c


def make_schedule():
    after = {}

    def put(j, *events):
        after.setdefault(j, []).extend(events)

    put(3, ("m_sumsq",))
    put(9, ("a_sumsq",))
    for c in range(NCH):
        put(16 + 2 * c, ("a_turn", c))
    for g in range(0, NH, 2):
        put(24 + g, ("a_mix", g))
    put(44, ("ba",))
    put(45, ("ba_turn",))
    put(46, ("cumsum",))
    put(48, ("s_query",))
    for i in range(4):
        put(49 + i, ("s_score", 2 * i), ("s_score", 2 * i + 1))
    put(54, ("s_cols",))
    for i in range(8):
        put(55 + i // 3, ("s_value", i))
    put(57, ("s_back",))
    for t in range(2 * NH):
        put(QKV_TILE + t + 2, ("l2_sum", t))
    for i in range(6):
        put(QKV_TILE + 18 + i, ("l2_spread", i))
    for h in range(MH):
        put(58 + 3 * h, ("p_score", h))
        put(59 + 3 * h, ("p_turn", h))
        put(60 + 3 * h, ("p_value", h))
    out = [("x_sumsq",)]
    for j in range(WO_TILE):
        out.append(("tile", j))
        out += after.get(j, [])
    out += [("conv_s",), ("l2_spread", 6), ("l2_s",), ("l2_spread", 7)]
    out += [("sd_bcast",), ("sd_state",), ("sd_ktok",), ("sd_utok",)] + [("sd_outer", h) for h in range(NH)]
    out += [("delta", 0), ("wo_split",)] + [("delta", c) for c in range(1, NCH)]
    out += [("o_sum",)] + [("o_spread", h) for h in range(NH)]
    out += [("m_split",)]
    for k in range(KD):
        out += [("tile", WO_TILE + k)] + ([("f_sum", k - 2)] if k >= 2 else [])
    out += [("f_sum", KD - 2), ("f_sum", KD - 1)]
    out += [("f_sumsq",), ("h_turn", 0, 3), ("router",), ("h_turn", 3, NT), ("rank",), ("moe",), ("final",)]
    return out


SCHEDULE = make_schedule()
SIDE = {}
for _e in SCHEDULE:
    _k = {"s_score": ("s_score",), "s_value": ("s_value",), "l2_sum": ("l2_sum",)}.get(_e[0], _e)
    if _e[0] in ("x_sumsq", "m_sumsq", "a_sumsq", "a_turn", "a_mix", "ba", "ba_turn", "cumsum", "s_score", "s_cols",
                 "s_value", "s_back", "l2_sum", "l2_spread", "l2_s", "p_score", "p_turn", "p_value", "sd_bcast", "sd_state", "sd_ktok",
                 "sd_utok", "sd_outer") and _k not in SIDE:
        SIDE[_k] = len(SIDE)

NO_SIDE_MM = (("s_score",), ("s_value",), ("l2_sum",))
SIDE_MM = {_e: 1 + sum(SIDE[_f] < SIDE[_e] and _f not in NO_SIDE_MM for _f in SIDE) for _e in SIDE}
PE_STEPS = (["grow", "brow", "kk", "kq", "turn_k", "turn_v", "turn_u"]
            + [f"{m}{l}" for l in range(6) for m in ("mt", "tx")] + ["wk", "uu", "oo", "ss"])
DVE_STEPS = (["arg", "bs", "mt", "u1", "at", "qg"]
             + [f"{m}{l}" for l in range(6) for m in ("x", "tu")] + ["o", "s"])
ACT_STEPS = ["eg", "dt", "kb", "kd", "vb", "t1", "nw", "u"]


def build_step(nc, a, o):
    ctx = ExitStack()
    with ctx:
        def sem(name):
            return ctx.enter_context(nc.semaphore(name))

        base = (nc.sbuf_base + 63) // 64 * 64
        room = (nc.sbuf_usable_end - 64 - base) // 4
        words = {}
        at = 0
        for name, n in [("FIX", 3200), ("RA", 24 * T), ("M", 8 * T), ("ZG", 8 * T), ("HT", 16 * T),
                        ("CQ", 8 * T), ("MKV", 4096), ("RAW", 4096), ("SPL", 8192)]:
            words[name] = at
            at += n
        assert at <= room, (at, room)
        fix = [0]

        def place(name, shape, region, off=0, dt=F32):
            return nc.alloc_sbuf_tensor_at(name, shape, dt, offset=base + 4 * (words[region] + off))

        def fixed(name, shape, dt=F32):
            n = int(np.prod(shape[1:]))
            n = (n + 7) // 8 * 8
            t = place(name, shape, "FIX", fix[0], dt)
            fix[0] += n
            assert fix[0] <= 3200, fix[0]
            return t

        consts = fixed("consts", [128, NCONST])
        params = fixed("params", [128, NPARAM])
        rstd = fixed("rstd", [128, T])
        ba = fixed("ba", [128, NT, 16])
        gate_g = fixed("gate_g", [128, NT, NH])
        beta = fixed("beta", [128, NT, NH])
        tmp_g = fixed("tmp_g", [128, 2, NT, NH])
        cum_g = fixed("cum_g", [128, NCH, NH])
        dec_end = fixed("dec_end", [128, NCH, NH])
        dec_kd = fixed("dec_kd", [128, NCH, NH])
        dec_kb = fixed("dec_kb", [128, NCH, NH])
        neg_a = fixed("neg_a", [128, NH])
        small = fixed("small", [128, 4, 4])
        s_small = fixed("s_small", [128, 4])
        s_rhs = fixed("s_rhs", [NS, 2, NS, NH])
        s_bc = fixed("s_bc", [128, 2, NS, NH])
        s_qk = fixed("s_qk", [128, NH, NS])
        s_u = fixed("s_u", [128, NH, NS])
        s_tmp = fixed("s_tmp", [128, NH, NS])
        s_eg = fixed("s_eg", [NS, NH])
        n_rounds = fixed("n_rounds", [1, 8], I32)

        def const(name, rows=128):
            x, y = CONST[name]
            return consts[0:rows, x:y]

        def param(name, i=None, n=1):
            x, y = PARAM[name]
            return params[:, x:y] if i is None else params[:, x + i:x + i + n]

        x_in = place("x_in", [128, KD, T], "RA")
        x_sq = place("x_sq", [128, KD, T], "RA", 8 * T)
        av = place("av", [128, KD, T], "RA")
        au = place("au", [128, KD, T], "RA", 8 * T)
        a_sq = place("a_sq", [128, KD, T], "RA", 16 * T)
        av_tok = place("av_tok", [128, NCH, D], "RA", 16 * T)
        prob = place("prob", [128, NCH, NM], "RA")
        prob_t = place("prob_t", [128, 2, SEQ], "RA", 1024)
        kv_ring = place("kv_ring", [128, 4, 2048], "RA", 2048)
        w_ba = place("w_ba", [128, KD, 16], "RA", 10240)
        w_ba_h = place("w_ba_h", [128, KD, 16], "RA", 10368, F32R)
        w_ba_l = place("w_ba_l", [128, KD, 16], "RA", 10496, F32R)
        s_q = place("s_q", [128, KD, NS * 32], "RA")
        s_p = place("s_p", [128, 2 * MH, NS * 32], "RA")
        s_pr = place("s_pr", [128, NM], "RA", 10624)
        ba_t = place("ba_t", [16, T], "RA", 10624)
        s_o = place("s_o", [128, NM], "RA", 10880)
        qkv = place("qkv", [128, 24, T], "RA")
        mem_h = place("mem_h", [128, KD, NM], "M", 0, F32R)
        mem_l = place("mem_l", [128, KD, NM], "M", 2048, F32R)
        mrg = place("mrg", [128, KD, T], "M")
        x1 = place("x1", [128, KD, T], "M")
        ws_t = place("ws_t", [128, NH, CH], "ZG")
        bs_row = place("bs_row", [1, NH, CH], "ZG", 1024)
        zg = place("zg", [128, KD, T], "ZG")
        h2 = place("h2", [128, KD, T], "ZG")
        ht_h = place("ht_h", [128, KD, T], "HT", 0, F32R)
        ht_l = place("ht_l", [128, KD, T], "HT", 8 * T, F32R)
        dl = [[place(f"dl{h}_{n}", [128, 4, 128], "HT", (11 * h + n) * 512) for n in range(11)]
              for h in range(2)]
        h2p = [place(f"h2p{i}", [TT, NT, D], "HT", i * NT * D // 2, BF16) for i in range(3)]
        h2r = [place(f"h2r{i}", [TT, D], "HT", 3 * NT * D // 2 + i * D) for i in range(2)]
        lg_t = place("lg_t", [NG + NE, T], "HT", 3 * NT * D // 2 + 2 * D)
        y_hi = place("y_hi", [128, D], "HT", 3 * NT * D // 2 + 2 * D, F32R)
        y_lo = place("y_lo", [128, D], "HT", 3 * NT * D // 2 + 3 * D, F32R)
        mem = place("mem", [128, KD, NM], "CQ")
        mem_sq = place("mem_sq", [128, KD, NM], "CQ", 2048)
        qc = place("qc", [128, KD, T], "CQ")
        xpad = [place(f"xpad{i}", [128, 528], "CQ", i * 528) for i in range(2)]
        cacc = [place(f"cacc{i}", [128, T], "CQ", 1056 + i * T) for i in range(2)]
        cvs = place("cvs", [128, 24, 4, NS], "CQ", 2112)
        cvs_sum = place("cvs_sum", [128, 24, NS], "CQ", 2880)
        s_rows = place("s_rows", [128, 2, 1024], "CQ", 0)
        s_kq = place("s_kq", [128, NS, 32], "MKV", 3336)
        s_sv = place("s_sv", [128, 2, NH, NS], "CQ", 2048)
        l2sq = [place(f"l2sq{i}", [128, SEQ], "CQ", 3072 + i * SEQ) for i in range(2)]
        osq = [place(f"osq{i}", [128, T], "HT", (8 + i) * T) for i in range(4)]
        x_res = place("x_res", [128, KD, T], "CQ")
        mk = place("mk", [128, KD, NM], "MKV")
        mv = place("mv", [128, 2, D], "MKV", 2048)
        st = place("st", [128, NH, 128], "MKV")
        ext = place("ext", [128, 24, 4, NS], "MKV", 1024)
        convp = place("convp", [128, 24, 3], "MKV", 1792)
        l2rn = place("l2rn", [16, SEQ], "MKV", 2048)
        s_sq = place("s_sq", [128, 2 * NH, NS], "MKV", 2560)
        s_rn = place("s_rn", [128, 2 * NH, NS], "MKV", 2688)
        orn = place("orn", [16, T], "MKV", 2816)
        w_r = place("w_r", [128, KD, NG + NE], "MKV")
        w_r_h = place("w_r_h", [128, KD, NG + NE], "MKV", 288, F32R)
        w_r_l = place("w_r_l", [128, KD, NG + NE], "MKV", 576, F32R)
        raw = [place(f"raw{i}", [128, KD, BLK], "RAW", 2048 * i) for i in range(2)]
        w_h = [place(f"w_h{i}", [128, KD, BLK], "SPL", 4096 * i, F32R) for i in range(2)]
        w_l = [place(f"w_l{i}", [128, KD, BLK], "SPL", 4096 * i + 2048, F32R) for i in range(2)]
        k_tok = place("k_tok", [NS, NH, 128], "RAW")
        u_tok = place("u_tok", [NS, NH, 128], "RAW", 1024)
        u_diag = [place(f"u_diag{i}", [NS, NS, 128], "RAW", 2048 + 1024 * i) for i in range(2)]
        s0 = place("s0", [128, NH, NS, 128], "SPL")
        hr_h = place("hr_h", [128, KD, T], "RAW", 0, F32R)
        hr_l = place("hr_l", [128, KD, T], "RAW", KD * T, F32R)
        fsq = place("fsq", [128, KD, T], "RA")
        e_gate = place("e_gate", [128, 2, KD, DE], "RA")
        e_up = place("e_up", [128, 2, KD, DE], "RAW")
        e_down = [place("e_down0", [128, DE // 128, D], "RA", 8192), place("e_down1", [128, DE // 128, D], "RAW", 8192)]
        moe_at = [0]

        def moe_buf(name, shape, dt=F32):
            t = place(name, shape, "MKV", 864 + moe_at[0], dt)
            moe_at[0] += (int(np.prod(shape[1:])) // (2 if dt == BF16 else 1) + 7) // 8 * 8
            assert moe_at[0] <= 4096 - 864
            return t

        lg = moe_buf("lg", [TT, NT, NG + NE])
        r8 = moe_buf("r8", [TT, NT, 8, 4])
        ing = moe_buf("ing", [TT, NT, EPG])
        ing2 = moe_buf("ing2", [TT, NT, EPG])
        oh1 = moe_buf("oh1", [TT, NT, EPG])
        oh2 = moe_buf("oh2", [TT, NT, EPG])
        w8 = moe_buf("w8", [TT, NT, EPG])
        prod32 = moe_buf("prod32", [TT, NT, NG, EPG])
        comb = moe_buf("comb", [TT, NT, NE])
        strict_b = moe_buf("strict_b", [TT, TT], BF16)
        ones_b = moe_buf("ones_b", [TT, 128], BF16)
        hit = moe_buf("hit", [TT, NT, NE], BF16)
        comb3 = moe_buf("comb3", [TT, NT, NE, 3], BF16)
        comb_r = moe_buf("comb_r", [TT, NT, NE])
        rank = moe_buf("rank", [TT, NT, NE + 2])
        cnt = moe_buf("cnt", [128, NE + 16])
        zoff = [0]

        def moe_z(name, shape, dt=F32):
            t = place(name, shape, "ZG", zoff[0], dt)
            zoff[0] += (int(np.prod(shape[1:])) // (2 if dt == BF16 else 1) + 7) // 8 * 8
            assert zoff[0] <= 8 * T, name
            return t

        sel = [moe_z(f"sel{i}", [TT, NT, 2, CAP], BF16) for i in range(2)]
        xt = moe_z("xt", [128, KD, 128])
        sg = moe_z("sg", [128, DE])
        act_r = moe_z("act_r", [128, DE])
        act_t = moe_z("act_t", [128, DE // 128, 128])
        slot_w = moe_z("slot_w", [128, 8])
        pair_w = moe_z("pair_w", [TT, NT, 2, 3], BF16)
        ident_b = moe_z("ident_b", [128, 128], BF16)
        sel_t = [moe_z("sel_t0", [128, T], F32R),
                 place("sel_t1", [128, T], "HT", 3 * NT * D // 2 + 4 * D, F32R)]
        fill = moe_z("fill", [1, 8])

        pp = [ctx.enter_context(nc.psum_tensor(f"pp{i}", [128, 2, 512], F32)) for i in range(4)]
        side = pp[3]
        bank = [[pp[2 * h + i // 2][:, i % 2, :].rearrange("p (u n) -> p u n", u=4) for i in range(4)]
                for h in range(2)]

        const_in = sem("const_in")
        x_loaded = [sem(f"x_loaded{i}") for i in range(2)]
        mem_loaded, ws_loaded = sem("mem_loaded"), sem("ws_loaded")
        raw_loaded = [sem(f"raw_loaded{i}") for i in range(2)]
        hi_ready, lo_ready = sem("w_hi_ready"), sem("w_lo_ready")
        tile_mm = sem("tile_mm")
        psum_free = [sem(f"psum_free{i}") for i in range(3)]
        tile_act = sem("tile_act")
        sq_ready, rstd_ready = sem("sq_ready"), sem("rstd_ready")
        h_norm, h_hi, h_lo = sem("h_norm"), sem("h_hi"), sem("h_lo")
        side_mm, side_free = sem("side_mm"), sem("side_free")
        a_normed, a_sq_ready = sem("a_normed"), sem("a_sq_ready")
        wba_loaded, wba_hi, wba_split = sem("wba_loaded"), sem("wba_hi"), sem("wba_split")
        ws_masked = sem("ws_masked")
        g_step, g_act = sem("g_step"), sem("g_act")
        kv_loaded = [sem(f"kv_loaded{i}") for i in range(4)]
        kv_used = sem("kv_used")
        soft_max, soft_exp, soft_norm = sem("soft_max"), sem("soft_exp"), sem("soft_norm")
        out_mem, out_av, out_conv, out_st, out_y = (sem(n) for n in
                                                    ("out_mem", "out_av", "out_conv", "out_st", "out_y"))
        out_s0 = sem("out_s0")
        ext_loaded, ext_ready = sem("ext_loaded"), sem("ext_ready")
        conv_copy, conv_sum, conv_silu = (sem(n) for n in ("conv_copy", "conv_sum", "conv_silu"))
        conv_zero, convs_sum, convs_silu, gc_added = (sem(n) for n in ("conv_zero", "convs_sum", "convs_silu",
                                                                       "gc_added"))
        l2_sq, l2_mm, l2_rows, l2_done = sem("l2_sq"), sem("l2_mm"), sem("l2_rows"), sem("l2_done")
        on_sq, on_mm, on_rows, on_done = sem("on_sq"), sem("on_mm"), sem("on_rows"), sem("on_done")
        on_spread, on_mul, on_z = sem("on_spread"), sem("on_mul"), sem("on_z")
        s_q_ready = sem("s_q_ready")
        s0_loaded = sem("s0_loaded")
        sd_rhs, sd_u, sd_o, sd_diag, sd_dec, sd_new = (sem(n) for n in ("sd_rhs", "sd_u", "sd_o", "sd_diag",
                                                                       "sd_dec", "sd_new"))
        delta_pe = [sem(f"delta_pe{i}") for i in range(2)]
        delta_dve = [sem(f"delta_dve{i}") for i in range(2)]
        delta_act = [sem(f"delta_act{i}") for i in range(2)]
        st_zero = sem("st_zero")
        xres_loaded, wr_loaded, wr_hi, wr_split = (sem(n) for n in
                                                   ("xres_loaded", "wr_loaded", "wr_hi", "wr_split"))
        x1_ready = sem("x1_ready")
        router_mm, ht_mm, ht_hi, ht_lo = sem("router_mm"), sem("ht_mm"), sem("ht_hi"), sem("ht_lo")
        lg_ready, lg_exp, hit_ready, rank_mm, rounds_set = (sem(n) for n in (
            "lg_ready", "lg_exp", "hit_ready", "rank_mm", "rounds_set"))
        eg_loaded, eu_loaded = sem("eg_loaded"), sem("eu_loaded")
        ed_loaded = [sem(f"ed_loaded{i}") for i in range(2)]
        sc_free = sem("sc_free")
        sel_ready, pair_w_ready, gather_mm, xt_ready = (sem(n) for n in ("sel_ready", "pair_w_ready",
                                                                         "gather_mm", "xt_ready"))
        slot_w_ready, y_hi_ready = sem("slot_w_ready"), sem("y_hi_ready")
        gate_mm, gu_mm, silu_done, act_ready = (sem(n) for n in ("gate_mm", "up_mm", "silu_done", "act_ready"))
        at_mm, at_out, y_mm, y_out = (sem(n) for n in ("act_turned_mm", "act_turned_out", "y_mm", "y_out"))
        selt_mm, selt_out, sc_mm = (sem(n) for n in ("sel_turned_mm", "sel_turned_out", "sc_mm"))
        lg_t_ready, logits_mm = sem("lg_t_ready"), sem("logits_mm")
        sd_rows, sd_rows_out = sem("sd_rows"), sem("sd_rows_out")
        ht_part, ht_mid = sem("ht_part"), sem("ht_mid")
        fin_mm, fin_sq, fin_done, rank_moved = (sem(n) for n in (
            "fin_mm", "fin_sq", "fin_done", "rank_moved"))
        dve_chain = sem("dve_chain")
        act_chain = sem("act_chain")

        block = ctx.enter_context(nc.Block())

        def pe_at(hh, c, step):
            return c * len(PE_STEPS) + PE_STEPS.index(step) + 1

        def dve_at(hh, c, step):
            return c * len(DVE_STEPS) + DVE_STEPS.index(step) + 1

        def act_at(hh, c, step):
            return c * len(ACT_STEPS) + ACT_STEPS.index(step) + 1

        def kind(j):
            return BLOCK_KIND[j // 2], j - 2 * FIRST_BLOCK[BLOCK_KIND[j // 2]]

        def out_of_psum(eng, j):
            eng.wait_ge(psum_free[j % 3], j // 3 + 1)

        @block.sync
        def _(sp):
            def load_block(b):
                if b >= 2:
                    sp.wait_ge(lo_ready, b - 1)
                sp.dma_start(raw[b % 2][:], a["w_blk"][b].rearrange("p (k n) -> p k n", k=KD))\
                    .then_inc(raw_loaded[b % 2], 16)

            def load_kv(n):
                if n >= 4:
                    sp.wait_ge(kv_used, n - 3)
                src = a["cache_k"][n] if n < NS else a["cache_v"][n - NS]
                sp.dma_start(kv_ring[:, n % 4, :], src).then_inc(kv_loaded[n % 4], 16)

            def pair(w, e, n):
                return a[w][bass.ds(e, n)].rearrange("o p (k n) -> p o k n", o=n, n=DE if w != "w_down" else D)

            def load_pair(e, used=None):
                if used is not None:
                    sp.wait_ge(gate_mm, used)
                sp.dma_start(e_gate[:], pair("w_gate", e, 2)).then_inc(eg_loaded, 16)
                if used is None:
                    sp.dma_start(e_down[0][:], pair("w_down", e, 1)[:, 0]).then_inc(ed_loaded[0], 16)
                    sp.wait_ge(router_mm, 1)
                else:
                    sp.wait_ge(gu_mm, used)
                sp.dma_start(e_up[:], pair("w_up", e, 2)).then_inc(eu_loaded, 16)
                if used is not None:
                    sp.wait_ge(y_mm, 2 * used)
                    sp.dma_start(e_down[0][:], pair("w_down", e, 1)[:, 0]).then_inc(ed_loaded[0], 16)
                sp.dma_start(e_down[1][:], pair("w_down", e + 1, 1)[:, 0]).then_inc(ed_loaded[1], 16)

            xk = a["x_t"].rearrange("p (k n) -> p k n", k=KD)
            for i in range(2):
                sp.dma_start(x_in[:, 4 * i:4 * i + 4, :], xk[:, 4 * i:4 * i + 4, :]).then_inc(x_loaded[i], 16)
            sp.dma_start(consts[:], a["consts"]).then_inc(const_in, 16)
            sp.dma_start(params[:], a["params"]).then_inc(const_in, 16)
            sp.dma_start(mem[:], a["mem_t"].rearrange("p (k n) -> p k n", k=KD)).then_inc(mem_loaded, 16)
            load_block(0)
            load_block(1)
            sp.dma_start(ws_t[:], a["ws_t"].rearrange("p (k n) -> p k n", k=NH)).then_inc(ws_loaded, 16)
            sp.dma_start(bs_row[:], a["bs"].rearrange("p (k n) -> p k n", k=NH)).then_inc(ws_loaded, 16)
            for ev in SCHEDULE:
                if ev[0] == "tile":
                    j = ev[1]
                    b = j // 2
                    if j % 2 == 0 and 2 <= b + 2 < WO_BLOCK:
                        load_block(b + 2)
                    if j == 15:
                        sp.wait_ge(a_normed, 8)
                        sp.dma_start(o["av"].rearrange("p (k n) -> p k n", k=KD), av[:, :, SEQ:T])\
                            .then_inc(out_av, 16)
                    if j == 31:
                        for i in range(29, 32):
                            out_of_psum(sp, i)
                        sp.dma_start(o["mk"].rearrange("p (k n) -> p k n", k=KD), mk[:]).then_inc(out_mem, 16)
                        sp.dma_start(o["mv"].rearrange("p (k n) -> p k n", k=2), mv[:]).then_inc(out_mem, 16)
                    if j == 39:
                        for i in range(37, 40):
                            out_of_psum(sp, i)
                        sp.wait_ge(out_av, 16)
                        sp.dma_start(w_ba[:], a["w_ba"].rearrange("p (k n) -> p k n", k=KD))\
                            .then_inc(wba_loaded, 16)
                        for n in range(4):
                            load_kv(n)
                    if j == QKV_TILE - 1:
                        sp.wait_ge(side_free, SIDE[("p_value", MH - 1)] + 1)
                        sp.wait_ge(out_mem, 32)
                        sp.dma_start(ext[:, :, 0:3, :],
                                     a["state_conv"].rearrange("p (t j b) -> p t j b", t=24, j=3))\
                            .then_inc(ext_loaded, 16)
                elif ev[0] in ("s_score", "s_value"):
                    n = ev[1] + (NS if ev[0] == "s_value" else 0)
                    if n + 4 < 2 * NS:
                        load_kv(n + 4)
                elif ev[0] == "conv_s":
                    sp.wait_ge(ext_ready, 24)
                    sp.dma_start(o["conv_s"].rearrange("p (t j b) -> p t j b", t=24, j=3), ext[:, :, 1:4, :])\
                        .then_inc(out_conv, 16)
                    sp.dma_start(o["conv_p"].rearrange("p (t j) -> p t j", t=24), convp[:]).then_inc(out_conv, 16)
                    sp.wait_ge(tile_mm, WO_TILE)
                    sp.dma_start(s0[:], a["state_gdn"].rearrange("p (h b n) -> p h b n", h=NH, b=NS))\
                        .then_inc(s0_loaded, 16)
                elif ev == ("sd_outer", NH - 1):
                    sp.wait_ge(sd_new, NH)
                    sp.dma_start(o["gdn_s"].rearrange("p (h b n) -> p h b n", h=NH, b=NS), s0[:])\
                        .then_inc(out_s0, 16)
                    load_block(WO_BLOCK)
                    load_block(WO_BLOCK + 1)
                elif ev[0] == "delta" and ev[1] == NCH - 1:
                    for hh in range(2):
                        sp.wait_ge(delta_dve[hh], dve_at(hh, NCH - 1, "s"))
                        sp.wait_ge(delta_pe[hh], pe_at(hh, NCH - 1, "ss"))
                    sp.dma_start(o["gdn_p"].rearrange("p (h n) -> p h n", h=NH), st[:]).then_inc(out_st, 16)
                    sp.dma_start(x_res[:], a["x_t"].rearrange("p (k n) -> p k n", k=KD))\
                        .then_inc(xres_loaded, 16)
                    sp.wait_ge(out_st, 16)
                    sp.dma_start(w_r[:], a["w_router"].rearrange("p (k n) -> p k n", k=KD))\
                        .then_inc(wr_loaded, 16)
            load_block(WO_BLOCK + 2)
            load_block(WO_BLOCK + 3)
            sp.wait_ge(on_done, 8)
            sp.wait_ge(out_conv, 16 * 2)
            load_pair(0)
            with sp.Fori(1, NPAIR) as p:
                load_pair(p * 2, p)
            sp.wait_ge(rounds_set, 1)
            rounds = sp.value_load(n_rounds[0:1, 0:1], min_val=1, max_val=9)
            with sp.If(rounds > 1):
                with sp.Fori(1, rounds) as r:
                    with sp.Fori(0, NPAIR) as p:
                        load_pair(p * 2, r * NPAIR + p)
            for k in range(KD):
                sp.wait_ge(fin_done, k + 1)
                sp.dma_start(o["y"][:, k * T:(k + 1) * T], x1[:, k, :]).then_inc(out_y, 16)
            sp.wait_ge(out_y, 16 * KD)
            sp.wait_ge(out_mem, 32)
            sp.wait_ge(out_av, 16)
            sp.wait_ge(out_st, 16)
            sp.wait_ge(out_conv, 32)
            sp.wait_ge(out_s0, 16)

        @block.tensor
        def _(pe):
            mm = nc.tensor.matmul

            def begin(ev):
                n = SIDE[ev]
                if n:
                    pe.wait_ge(side_free, n)

            def sum_rows(out, src, ready, base_count, n, start=0):
                for k in range(KD):
                    pe.wait_ge(ready, base_count + k + 1)
                    for hf in range(2):
                        w = n // 2
                        last = mm(out[:, hf, 0:w], const("ones"), src[:, k, hf * w:(hf + 1) * w],
                                  start=(k == 0), stop=(k == KD - 1))
                return last

            def tile(j):
                b, i = j // 2, j % 2
                what, _t = kind(j)
                s = b % 2
                ps = pp[j % 3]
                if i == 0:
                    pe.wait_ge(lo_ready, b + 1)
                if j >= WO_TILE + 3:
                    pe.wait_ge(x1_ready, j - WO_TILE - 2)
                elif j >= 3 and j < WO_TILE:
                    pe.wait_ge(psum_free[j % 3], j // 3)
                need = {"mk": 16, "mv": 16, "wo": 24}.get(what, 8)
                first = j in (0, 2 * FIRST_BLOCK["mk"], WO_TILE)
                if not first:
                    pe.wait_ge(h_lo, need)
                if what == "mv":
                    ms = slice(i * 128, (i + 1) * 128)
                    n = 0
                    for k in range(KD):
                        for m_, w_ in ((mem_h, w_h), (mem_h, w_l), (mem_l, w_h)):
                            last = mm(ps[:, 0, 0:BLK], m_[:, k, ms], w_[s][:, k, :],
                                      start=(n == 0), stop=(n == 3 * KD - 1))
                            n += 1
                    last.then_inc(tile_mm, 1)
                    return
                cs = slice(i * 128, (i + 1) * 128)
                if what == "mk":
                    moving = [(ps[:, 0, 0:NM], slice(0, NM))]
                    xh, xl = mem_h, mem_l
                else:
                    moving = [(ps[:, hf, 0:HALF], slice(hf * HALF, (hf + 1) * HALF)) for hf in range(2)]
                    xh, xl = ht_h, ht_l
                for k in range(KD):
                    if first:
                        pe.wait_ge(h_lo, need - KD + k + 1)
                    for q, (w_, x_) in enumerate(((w_h, xh), (w_h, xl), (w_l, xh))):
                        for dst, ts in moving:
                            last = mm(dst, w_[s][:, k, cs], x_[:, k, ts],
                                      start=(k == 0 and q == 0), stop=(k == KD - 1 and q == 2))
                last.then_inc(tile_mm, 1)

            def narrow(out, wh, wl, xh, xl):
                for k in range(KD):
                    for q, (w_, x_) in enumerate(((wh, xh), (wh, xl), (wl, xh))):
                        for hf in range(2):
                            last = mm(out[:, hf, 0:HALF], w_[:, k, :], x_[:, k, hf * HALF:(hf + 1) * HALF],
                                      start=(k == 0 and q == 0), stop=(k == KD - 1 and q == 2))
                return last

            def delta(c):
                cs = slice(c * CH, (c + 1) * CH)

                def each(step, fn):
                    for hh in range(2):
                        last = fn(hh)
                        last.then_inc(delta_pe[hh], 1)

                def wd(hh, step, cc=c):
                    pe.wait_ge(delta_dve[hh], dve_at(hh, cc, step))

                def wa(hh, step, cc=c):
                    pe.wait_ge(delta_act[hh], act_at(hh, cc, step))

                def four(hh, out, lhs, rhs):
                    for u in range(4):
                        last = mm(out[:, u, :], lhs(4 * hh + u, u), rhs(4 * hh + u, u), start=True, stop=True)
                    return last

                def q_(h):
                    return qkv[:, h, cs]

                def k_(h):
                    return qkv[:, NH + h, cs]

                def v_(h):
                    return qkv[:, 2 * NH + h, cs]

                def turn(hh, out, src):
                    for u in range(4):
                        last = nc.tensor.transpose(out[:, u, :], src(4 * hh + u, u), const("ident"))
                    return last

                def grow(hh):
                    if c:
                        wa(hh, "u", c - 1)
                    return four(hh, bank[hh][0], lambda h, u: gate_g[:, c, h:h + 1].to_broadcast([128, 128]),
                                lambda h, u: const("triu"))

                def brow(hh):
                    if c:
                        wd(hh, "o", c - 1)
                    return four(hh, bank[hh][1], lambda h, u: beta[:, c, h:h + 1].to_broadcast([128, 128]),
                                lambda h, u: const("ident"))

                def kk(hh):
                    if c:
                        wd(hh, "s", c - 1)
                    return four(hh, bank[hh][2], lambda h, u: k_(h), lambda h, u: k_(h))

                def kq(hh):
                    if c:
                        wa(hh, "nw", c - 1)
                    return four(hh, bank[hh][3], lambda h, u: k_(h), lambda h, u: q_(h))

                def turn_k(hh):
                    wd(hh, "arg")
                    wa(hh, "eg")
                    return turn(hh, bank[hh][0], lambda h, u: k_(h))

                def turn_v(hh):
                    wd(hh, "bs")
                    return turn(hh, bank[hh][1], lambda h, u: v_(h))

                def turn_u(hh):
                    wd(hh, "u1")
                    return turn(hh, bank[hh][2], lambda h, u: dl[hh][3][:, u, :])

                if c == 0:
                    pe.wait_ge(side_free, len(SIDE))
                    for i in range(3):
                        pe.wait_ge(psum_free[i], WO_TILE // 3)
                    pe.wait_ge(l2_done, NH + 1)
                each("grow", grow)
                each("brow", brow)
                each("kk", kk)
                each("kq", kq)
                each("turn_k", turn_k)
                each("turn_v", turn_v)
                each("turn_u", turn_u)
                for l in range(6):
                    def m_t(hh):
                        if l == 0:
                            wa(hh, "t1")
                        else:
                            wd(hh, f"tu{l - 1}")
                        return four(hh, bank[hh][2], lambda h, u: dl[hh][1][:, u, :],
                                    lambda h, u: dl[hh][2][:, u, :])

                    def t_x(hh):
                        wd(hh, f"x{l}")
                        if l == 0:
                            wd(hh, "at")
                        if l < 5:
                            four(hh, bank[hh][3], lambda h, u: dl[hh][3][:, u, :],
                                 lambda h, u: dl[hh][4][:, u, :])
                        return four(hh, bank[hh][2], lambda h, u: dl[hh][4][:, u, :],
                                    lambda h, u: dl[hh][3][:, u, :])

                    each(f"mt{l}", m_t)
                    each(f"tx{l}", t_x)

                def wk(hh):
                    wd(hh, "tu5")
                    wa(hh, "vb")
                    return four(hh, bank[hh][3], lambda h, u: dl[hh][5][:, u, :],
                                lambda h, u: dl[hh][3][:, u, :])

                def uu(hh):
                    wa(hh, "nw")
                    if c:
                        wd(hh, "s", c - 1)
                    else:
                        pe.wait_ge(st_zero, 1)
                    for u in range(4):
                        mm(bank[hh][0][:, u, :], dl[hh][3][:, u, :], dl[hh][7][:, u, :], start=True, stop=False)
                        last = mm(bank[hh][0][:, u, :], dl[hh][9][:, u, :], st[:, 4 * hh + u, :],
                                  start=False, stop=True)
                    return last

                def oo(hh):
                    wa(hh, "u")
                    wd(hh, "qg")
                    for u in range(4):
                        mm(bank[hh][1][:, u, :], st[:, 4 * hh + u, :], dl[hh][8][:, u, :], start=True, stop=False)
                        last = mm(bank[hh][1][:, u, :], dl[hh][10][:, u, :], dl[hh][0][:, u, :],
                                  start=False, stop=True)
                    return last

                def ss(hh):
                    return four(hh, bank[hh][2], lambda h, u: dl[hh][6][:, u, :],
                                lambda h, u: dl[hh][10][:, u, :])

                each("wk", wk)
                each("uu", uu)
                each("oo", oo)
                each("ss", ss)

            def gather(n, j):
                pe.wait_ge(sel_ready, n + 1)
                for k in range(KD):
                    i = 0
                    for t in range(NT):
                        for src in h2p:
                            last = mm(pp[0][:, k // 4, (k % 4) * 128:(k % 4 + 1) * 128],
                                      src[:, t, k * 128:(k + 1) * 128], sel[j][:, t, :, :],
                                      start=(i == 0), stop=(i == 3 * NT - 1))
                            i += 1
                last.then_inc(gather_mm, 1)

            def scatter(n, j, s0_, s1_):
                for s in range(s0_, s1_):
                    dc, hf = s // 2, s % 2
                    pe.wait_ge(sc_free, n * SC + s + 1)
                    for part in (y_hi, y_lo):
                        last = mm(pp[3][:, s % 2, 0:HALF], part[:, dc * 128:(dc + 1) * 128],
                                  sel_t[1 - j][:, hf * HALF:(hf + 1) * HALF],
                                  start=(part is y_hi), stop=(part is y_lo))
                    last.then_inc(sc_mm, 1)

            def two(out, lhs, w0, w1, start, stop):
                for i, w in enumerate((w0, w1)):
                    rows = slice(i * CAP, (i + 1) * CAP)
                    last = mm(out[rows], lhs[:, rows], w, start=start, stop=stop, skip_group_check=True)
                return last

            def experts(n, j):
                pe.wait_ge(xt_ready, n + 1)
                pe.wait_ge(eg_loaded, (n + 1) * 16)
                for k in range(KD):
                    last = two(pp[1][:, 0, :], xt[:, k, :], e_gate[:, 0, k, :], e_gate[:, 1, k, :],
                               k == 0, k == KD - 1)
                    if k == KD - 1:
                        last.then_inc(gate_mm, 1)
                    if k == 2:
                        pe.wait_ge(y_out, n + 1)
                    if k >= 3:
                        scatter(n, j, k - 3, k - 2)
                pe.wait_ge(eu_loaded, (n + 1) * 16)
                for k in range(KD):
                    last = two(pp[1][:, 1, :], xt[:, k, :], e_up[:, 0, k, :], e_up[:, 1, k, :],
                               k == 0, k == KD - 1)
                    if k == KD - 1:
                        last.then_inc(gu_mm, 1)
                    scatter(n, j, KD - 3 + k, KD - 2 + k)
                pe.wait_ge(pair_w_ready, n + 1)
                pe.wait_ge(silu_done, n + 1)
                for t in range(NT):
                    one = sel[j][:, t, :, :].rearrange("p a n -> p (a n)")
                    mm(pp[1][:, 0, 0:6], one, pair_w[:, t, :, :].rearrange("p a n -> p (a n)"),
                       start=(t == 0), stop=(t == NT - 1))
                for t in range(NT):
                    one = sel[j][:, t, :, :].rearrange("p a n -> p (a n)")
                    dst = pp[2][:, 0, t * TT:(t + 1) * TT] if t < 4 else pp[2][:, 1, 0:TT]
                    last = mm(dst, one, ident_b[0:TT, 0:TT], start=True, stop=True)
                last.then_inc(selt_mm, 1)
                gather(n + 1, 1 - j)
                pe.wait_ge(act_ready, n + 1)
                for f in range(DE // 128):
                    last = nc.tensor.transpose(pp[1][:, 0, f * 128:(f + 1) * 128], act_r[:, f * 128:(f + 1) * 128],
                                               const("ident"))
                last.then_inc(at_mm, 1)
                scatter(n, j, SC - 3, SC)
                pe.wait_ge(at_out, n + 1)
                pe.wait_ge(selt_out, n + 1)
                for i in range(2):
                    pe.wait_ge(ed_loaded[i], (n + 1) * 16)
                for hf in range(2):
                    cs = slice(hf * 512, (hf + 1) * 512)
                    for f in range(DE // 128):
                        last = two(pp[2][:, hf, :], act_t[:, f, :], e_down[0][:, f, cs], e_down[1][:, f, cs],
                                   f == 0, f == DE // 128 - 1)
                    last.then_inc(y_mm, 1)

            pe.wait_ge(const_in, 32)
            for ev in SCHEDULE:
                e = ev[0]
                if e == "tile":
                    tile(ev[1])
                elif e == "x_sumsq":
                    begin(ev)
                    sum_rows(side, x_sq, sq_ready, 0, T).then_inc(side_mm, 1)
                elif e == "m_sumsq":
                    begin(ev)
                    sum_rows(side, mem_sq, sq_ready, 8, NM).then_inc(side_mm, 1)
                elif e == "a_sumsq":
                    begin(ev)
                    sum_rows(side, a_sq, a_sq_ready, 0, T).then_inc(side_mm, 1)
                elif e == "a_turn":
                    begin(ev)
                    pe.wait_ge(a_normed, 8)
                    c = ev[1]
                    for g in range(NH):
                        last = nc.tensor.transpose(side[:, g // 4, (g % 4) * 128:(g % 4 + 1) * 128],
                                                   av[:, g, c * CH:(c + 1) * CH], const("ident"))
                    last.then_inc(side_mm, 1)
                elif e == "a_mix":
                    begin(ev)
                    pe.wait_ge(ws_masked, 1)
                    pe.wait_ge(side_free, SIDE[("a_turn", NCH - 1)] + 1)
                    for i in range(2):
                        g = ev[1] + i
                        ob = side[:, i, :].rearrange("p (c n) -> p c n", c=NCH)
                        mm(ob, const("ones", 1), bs_row[0:1, g:g + 1, :].to_broadcast([1, NCH, CH]),
                           start=True, stop=False)
                        for c in range(NCH):
                            last = mm(ob[:, c, :], av_tok[:, c, g * 128:(g + 1) * 128], ws_t[:, g, :],
                                      start=False, stop=(c == NCH - 1))
                    last.then_inc(side_mm, 1)
                elif e == "ba":
                    begin(ev)
                    pe.wait_ge(wba_split, 1)
                    narrow(side[0:16], w_ba_h, w_ba_l, ht_h, ht_l).then_inc(side_mm, 1)
                elif e == "ba_turn":
                    begin(ev)
                    for t in range(NT):
                        ts = slice(t * CH, min((t + 1) * CH, T))
                        last = nc.tensor.transpose(side[0:ts.stop - ts.start, 0, t * 16:(t + 1) * 16], ba_t[:, ts],
                                                   const("ident", 16)[:, 0:16])
                    last.then_inc(side_mm, 1)
                elif e == "cumsum":
                    begin(ev)
                    pe.wait_ge(g_step, 3)
                    gp = gate_g[:, 0:NCH, :].rearrange("p c h -> p (c h)")
                    mm(side[:, 0, 0:32], const("triu"), gp, start=True, stop=True)
                    mm(side[:, 0, 32:64], const("ones"), gp, start=True, stop=True).then_inc(side_mm, 1)
                elif e == "s_score":
                    b = ev[1]
                    if b == 0:
                        begin(("s_score",))
                        pe.wait_ge(s_q_ready, 1)
                    pe.wait_ge(kv_loaded[b % 4], 16 * (b // 4 + 1))
                    kt = kv_ring[:, b % 4, :].rearrange("p (k n) -> p k n", k=KD)
                    for dc in range(2):
                        for h in range(MH):
                            last = mm(side[32 * h:32 * h + 32, 0, 0:NM], s_q[:, 2 * h + dc, b * 32:(b + 1) * 32],
                                      kt[:, 2 * h + dc, :], start=(b == 0 and dc == 0),
                                      stop=(b == NS - 1 and dc == 1), skip_group_check=True)
                    last.then_inc(kv_used, 1)
                elif e == "s_cols":
                    begin(ev)
                    pe.wait_ge(soft_norm, 1)
                    for mt in range(2):
                        last = nc.tensor.transpose(side[:, 0, mt * 128:(mt + 1) * 128],
                                                   s_pr[:, mt * 128:(mt + 1) * 128], const("ident"))
                    last.then_inc(side_mm, 1)
                elif e == "s_value":
                    b = ev[1]
                    if b == 0:
                        begin(("s_value",))
                    pe.wait_ge(kv_loaded[b % 4], 16 * ((b + NS) // 4 + 1))
                    vt = kv_ring[:, b % 4, :].rearrange("p (m n) -> p m n", m=2)
                    for mt in range(2):
                        for h in range(MH):
                            last = mm(side[32 * h:32 * h + 32, 1, 0:NM], s_p[:, mt * MH + h, b * 32:(b + 1) * 32],
                                      vt[:, mt, h * NM:(h + 1) * NM], start=(b == 0 and mt == 0),
                                      stop=(b == NS - 1 and mt == 1), skip_group_check=True)
                    last.then_inc(kv_used, 1)
                elif e == "s_back":
                    begin(ev)
                    for dc in range(2):
                        last = nc.tensor.transpose(side[:, 0, dc * 128:(dc + 1) * 128],
                                                   s_o[:, dc * 128:(dc + 1) * 128], const("ident"))
                    last.then_inc(side_mm, 1)
                elif e == "p_score":
                    begin(ev)
                    h = ev[1]
                    for c in range(NCH):
                        dst = side[:, c // 2, (c % 2) * NM:(c % 2 + 1) * NM]
                        for dc in range(2):
                            last = mm(dst, qc[:, 2 * h + dc, c * CH:(c + 1) * CH], mk[:, 2 * h + dc, :],
                                      start=(dc == 0), stop=(dc == 1))
                    last.then_inc(side_mm, 1)
                elif e == "p_turn":
                    begin(ev)
                    h = ev[1]
                    pe.wait_ge(soft_norm, h + 2)
                    for mt in range(2):
                        for c in range(NCH):
                            last = nc.tensor.transpose(side[:, mt, c * CH:(c + 1) * CH],
                                                       prob[:, c, mt * 128:(mt + 1) * 128], const("ident"))
                    last.then_inc(side_mm, 1)
                elif e == "p_value":
                    begin(ev)
                    h = ev[1]
                    for dc in range(2):
                        for mt in range(2):
                            cc = (2 * h + dc) * 128
                            last = mm(side[:, dc, :], mv[:, mt, cc:cc + 128], prob_t[:, mt, :],
                                      start=(mt == 0), stop=(mt == 1))
                    last.then_inc(side_mm, 1)
                elif e == "l2_sum":
                    t = ev[1]
                    if t == 0:
                        begin(("l2_sum",))
                    pe.wait_ge(l2_sq, t + 1)
                    mm(side[0:16, 0, :], const("pick")[:, 15 - t:31 - t], l2sq[t % 2][:],
                       start=(t == 0), stop=(t == 2 * NH - 1)).then_inc(l2_mm, 1)
                elif e == "l2_spread":
                    begin(ev)
                    pe.wait_ge(l2_rows, 1)
                    for i in range(2):
                        t = 2 * ev[1] + i
                        last = mm(side[:, i, :], const("ident", 16)[:, t:t + 1].to_broadcast([16, 128]), l2rn[:],
                                  start=True, stop=True)
                    last.then_inc(side_mm, 1)
                elif e == "l2_s":
                    begin(ev)
                    pe.wait_ge(l2_sq, 2 * NH + 1)
                    mm(side[:, 0, 0:2 * NH * NS], const("ones"), s_sq[:].rearrange("p h b -> p (h b)"),
                       start=True, stop=True).then_inc(side_mm, 1)
                elif e == "sd_bcast":
                    begin(ev)
                    pe.wait_ge(sd_rhs, 3)
                    mm(side[:, 0, 0:2 * NS * NH], const("ones", NS), s_rhs[:].rearrange("b a c h -> b (a c h)"),
                       start=True, stop=True)
                    mm(side[:, 1, 0:NS * NH], const("ones"), s_qk[:].rearrange("p h b -> p (h b)"),
                       start=True, stop=True).then_inc(side_mm, 1)
                elif e == "sd_state":
                    begin(ev)
                    pe.wait_ge(s0_loaded, 16)
                    pe.wait_ge(l2_done, NH + 1)
                    for i in range(2):
                        pe.wait_ge(psum_free[i], WO_TILE // 3)
                    for h in range(NH):
                        for i in range(2):
                            for g in range(4):
                                b = 4 * i + g
                                col = (h % 2) * 256 + i * 128
                                last = mm(pp[h // 4][32 * g:32 * g + 32, h % 4 // 2, col:col + 128],
                                          s_kq[:, b, :], s0[:, h, b, :],
                                          start=True, stop=True, skip_group_check=True)
                        if h % 4 == 3:
                            last.then_inc(sd_rows, 1)
                    for q in range(2):
                        pe.wait_ge(sd_rows_out, q + 1)
                        for m in range(8):
                            last = nc.tensor.transpose(pp[q][:, m // 4, (m % 4) * 128:(m % 4 + 1) * 128],
                                                       s_rows[:, q, m * 128:(m + 1) * 128], const("ident"))
                    last.then_inc(side_mm, 1)
                elif e in ("sd_ktok", "sd_utok"):
                    begin(ev)
                    if e == "sd_utok":
                        pe.wait_ge(sd_u, 1)
                    for h in range(NH):
                        src = s_u[:, h, :] if e == "sd_utok" else qkv[:, NH + h, SEQ:T]
                        last = nc.tensor.transpose(side[0:NS, h // 4, (h % 4) * 128:(h % 4 + 1) * 128], src,
                                                   const("ident"))
                    last.then_inc(side_mm, 1)
                elif e == "sd_outer":
                    h = ev[1]
                    if h == 0:
                        begin(ev)
                    elif h == 1:
                        pe.wait_ge(psum_free[2], WO_TILE // 3)
                    else:
                        pe.wait_ge(side_free, SIDE[ev] - 1)
                    pe.wait_ge(sd_diag, h + 1)
                    pe.wait_ge(side_free, SIDE[("sd_ktok",)] + 1)
                    for i in range(2):
                        last = mm(pp[3 - h % 2][:, i, :], k_tok[:, h, :], u_diag[h % 2][:, 4 * i:4 * i + 4, :],
                                  start=True, stop=True)
                    last.then_inc(side_mm, 1)
                elif e == "delta":
                    delta(ev[1])
                elif e == "o_sum":
                    for hh in range(2):
                        pe.wait_ge(delta_dve[hh], dve_at(hh, NCH - 1, "s"))
                    for h in range(NH):
                        pe.wait_ge(on_sq, h + 1)
                        for hf in range(2):
                            last = mm(pp[0][0:16, hf, 0:HALF], const("pick")[:, 15 - h:31 - h],
                                      osq[h % 4][:, hf * HALF:(hf + 1) * HALF], start=(h == 0), stop=(h == NH - 1))
                        last.then_inc(on_mm, 1)
                elif e == "o_spread":
                    h = ev[1]
                    pe.wait_ge(on_rows, 1)
                    if h >= 3:
                        pe.wait_ge(on_mul, h - 2)
                    for hf in range(2):
                        last = mm(pp[1 + h % 3][:, hf, 0:HALF], const("ident", 16)[:, h:h + 1].to_broadcast([16, 128]),
                                  orn[:, hf * HALF:(hf + 1) * HALF], start=True, stop=True)
                    last.then_inc(on_spread, 1)
                elif e == "f_sum":
                    k = ev[1]
                    pe.wait_ge(on_mul, NH)
                    pe.wait_ge(sq_ready, 16 + k + 1)
                    for hf in range(2):
                        last = mm(pp[3][:, hf, 0:HALF], const("ones"), h2[:, k, hf * HALF:(hf + 1) * HALF],
                                  start=(k == 0), stop=(k == KD - 1))
                    if k == KD - 1:
                        last.then_inc(fin_mm, 1)
                elif e == "router":
                    pe.wait_ge(wr_split, 1)
                    pe.wait_ge(h_lo, 32)
                    narrow(pp[0][0:NG + NE], w_r_h, w_r_l, hr_h, hr_l).then_inc(router_mm, 1)
                    pe.wait_ge(lg_t_ready, 1)
                    for t in range(NT):
                        last = nc.tensor.transpose(pp[0][0:TT, 0, t * (NG + NE):(t + 1) * (NG + NE)],
                                                   lg_t[:, t * TT:(t + 1) * TT],
                                                   const("ident", NG + NE)[:, 0:NG + NE])
                    last.then_inc(logits_mm, 1)
                elif e == "h_turn":
                    for t in range(ev[1], ev[2]):
                        if t >= 3:
                            pe.wait_ge(ht_lo, t - 2)
                        for k in range(KD):
                            if t == 0:
                                pe.wait_ge(h_norm, 16 + k + 1)
                            last = nc.tensor.transpose(
                                pp[1 + t % 3][0:TT, k // 4, (k % 4) * 128:(k % 4 + 1) * 128],
                                h2[:, k, t * TT:(t + 1) * TT], const("ident"))
                        last.then_inc(ht_mm, 1)
                elif e == "rank":
                    pe.wait_ge(hit_ready, 1)
                    for t in range(NT):
                        for s in range(t + 1):
                            left = strict_b[:] if s == t else ones_b[:, 0:TT]
                            mm(pp[0][0:TT, 1, t * NE:(t + 1) * NE], left, hit[:, s, :],
                               start=(s == 0), stop=(s == t))
                    for s in range(NT):
                        last = mm(pp[0][:, 1, 160:160 + NE], ones_b[:], hit[:, s, :],
                                  start=(s == 0), stop=(s == NT - 1))
                    last.then_inc(rank_mm, 1)
                elif e == "moe":
                    pe.wait_ge(ht_lo, NT)
                    pe.wait_ge(rounds_set, 1)
                    rounds = pe.value_load(n_rounds[0:1, 0:1], min_val=1, max_val=9)
                    gather(0, 0)
                    with pe.Fori(0, rounds) as r:
                        with pe.Fori(0, NPAIR // 2) as p:
                            for j in range(2):
                                experts((r * (NPAIR // 2) + p) * 2 + j, j)
                    pe.wait_ge(y_out, rounds * NPAIR + 1)
                    scatter(rounds * NPAIR, 0, 0, SC)
                elif e == "final":
                    sum_rows(pp[0], fsq, fin_sq, 0, T).then_inc(fin_mm, 1)

        @block.scalar
        def _(act):
            fn = nc.scalar.activation
            chain = [0]

            def link(ins):
                chain[0] += 1
                ins.then_inc(act_chain, 1)
                act.wait_ge(act_chain, chain[0])

            def split_hi(b):
                act.wait_ge(raw_loaded[b % 2], 16 * (b // 2 + 1))
                if b >= 2:
                    act.wait_ge(tile_mm, 2 * (b - 1))
                fn(w_h[b % 2][:], raw[b % 2][:], ACT.Copy).then_inc(hi_ready, 1)

            def squares(dst, src, done):
                for k in range(KD):
                    fn(dst[:, k, :], src[:, k, :], ACT.Square).then_inc(done, 1)

            def root_mean(ps, n, w):
                dst = rstd[:, 0:w].rearrange("p (a n) -> p a n", a=2)
                link(fn(dst, ps[:, :, 0:w // 2], ACT.Ln, bias=const("eps"), scale=1.0 / n))
                return fn(rstd[:, 0:w], rstd[:, 0:w], ACT.Exp, scale=-0.5)

            def tile(j):
                what, t = kind(j)
                b = j // 2
                if j % 2 == 0 and b + 1 < (WO_BLOCK if b < WO_BLOCK else NBLK) and b + 1 != WO_BLOCK + 1:
                    split_hi(b + 1)
                ps = pp[j % 3][:, :, 0:HALF]

                def whole(x):
                    return x.rearrange("p (a n) -> p a n", a=2)

                if what in ("av", "au"):
                    act.wait_ge(tile_mm, j + 1)
                    dst = av if what == "av" else au
                    fn(whole(dst[:, t, :]), ps, ACT.Gelu_apprx_tanh).then_inc(psum_free[j % 3], 1)
                elif what in ("ga", "gc"):
                    act.wait_ge(tile_mm, j + 1)
                    fn(ps, ps, ACT.Sigmoid, bias=param("b_gate", t + (16 if what == "gc" else 0)))\
                        .then_inc(tile_act, 1)
                elif what == "gb":
                    act.wait_ge(tile_mm, j + 1)
                    fn(whole(zg[:, t, :]), ps, ACT.Sigmoid, bias=param("b_gate", t + 8))\
                        .then_inc(psum_free[j % 3], 1)
                elif what == "z":
                    act.wait_ge(tile_mm, j + 1)
                    fn(ps, ps, ACT.Silu).then_inc(tile_act, 1)
                elif what == "qkv":
                    act.wait_ge(tile_mm, j + 1)
                    act.wait_ge(conv_zero, 1)
                    if t == 0:
                        act.wait_ge(gc_added, 8)
                    if t >= 2:
                        act.wait_ge(conv_sum, t - 1)
                        act.wait_ge(ext_ready, t - 1)
                    fn(whole(xpad[t % 2][:, 3:3 + T]), ps, ACT.Copy).then_inc(conv_copy, 1)
                    if t >= 2:
                        act.wait_ge(conv_silu, t - 1)
                    fn(whole(cacc[t % 2][:, :]), ps, ACT.Copy, scale=param("w_conv", 4 * t + 3))\
                        .then_inc(psum_free[j % 3], 1)
                    if t >= 1:
                        act.wait_ge(conv_sum, t)
                        fn(qkv[:, t - 1, 0:SEQ], cacc[(t - 1) % 2][:, 0:SEQ], ACT.Silu).then_inc(conv_silu, 1)

            for ev in SCHEDULE:
                e = ev[0]
                if e == "tile":
                    tile(ev[1])
                elif e == "x_sumsq":
                    for k in range(KD):
                        if k % 4 == 0:
                            act.wait_ge(x_loaded[k // 4], 16)
                        fn(x_sq[:, k, :], x_in[:, k, :], ACT.Square).then_inc(sq_ready, 1)
                    act.wait_ge(const_in, 32)
                    split_hi(0)
                    nc.scalar.preload_act_table_set("natural_log_exp_and_others")
                    act.wait_ge(side_mm, SIDE_MM[ev])
                    root_mean(side, D, T).then_inc(side_free, 1)
                    for k in range(KD):
                        act.wait_ge(h_norm, k + 1)
                        fn(ht_h[:, k, :], x_in[:, k, :], ACT.Copy).then_inc(h_hi, 1)
                elif e == "m_sumsq":
                    act.wait_ge(mem_loaded, 16)
                    squares(mem_sq, mem, sq_ready)
                    nc.scalar.preload_act_table_set("natural_log_exp_and_others")
                    act.wait_ge(side_mm, SIDE_MM[ev])
                    root_mean(side, D, NM).then_inc(side_free, 1)
                    for k in range(KD):
                        act.wait_ge(h_norm, 8 + k + 1)
                        fn(mem_h[:, k, :], mem[:, k, :], ACT.Copy).then_inc(h_hi, 1)
                elif e == "a_sumsq":
                    nc.scalar.preload_act_table_set("natural_log_exp_and_others")
                    act.wait_ge(side_mm, SIDE_MM[ev])
                    root_mean(side, D, T).then_inc(side_free, 1)
                elif e == "a_turn":
                    act.wait_ge(side_mm, SIDE_MM[ev])
                    fn(av_tok[:, ev[1], :].rearrange("p (a n) -> p a n", a=2), side[:], ACT.Copy)\
                        .then_inc(side_free, 1)
                elif e == "ba":
                    act.wait_ge(wba_loaded, 16)
                    fn(w_ba_h[:], w_ba[:], ACT.Copy).then_inc(wba_hi, 1)
                    act.wait_ge(side_mm, SIDE_MM[ev])
                    fn(ba_t[:].rearrange("p (a n) -> p a n", a=2), side[0:16, :, 0:HALF], ACT.Copy)\
                        .then_inc(side_free, 1)
                elif e == "ba_turn":
                    link(fn(neg_a[:], param("a_log"), ACT.Exp))
                    act.wait_ge(g_step, 1)
                    for rows, ts in ((128, slice(0, 4)), (NS, slice(4, 5))):
                        x, y = tmp_g[0:rows, 0, ts, :], tmp_g[0:rows, 1, ts, :]
                        link(fn(y, x, ACT.Abs))
                        link(fn(y, y, ACT.Exp, scale=-1.0))
                        fn(y, y, ACT.Ln, bias=1.0).then_inc(g_act, 1)
                    for rows, ts in ((128, slice(0, 4)), (NS, slice(4, 5))):
                        fn(beta[0:rows, ts, :], ba[0:rows, ts, 0:NH], ACT.Sigmoid).then_inc(g_act, 1)
                elif e == "cumsum":
                    act.wait_ge(g_step, 5)
                    fn(dec_end[:].rearrange("p c h -> p (c h)"), side[:, 0, 32:64], ACT.Exp).then_inc(g_act, 1)
                    fn(dec_kb[:], cum_g[:], ACT.Exp).then_inc(g_act, 1)
                    fn(dec_kd[:], dec_kd[:], ACT.Exp).then_inc(g_act, 1)
                    fn(s_eg[:], gate_g[0:NS, 4, :], ACT.Exp).then_inc(g_act, 1)
                elif ev == ("s_score", NS - 1):
                    act.wait_ge(soft_max, 1)
                    fn(s_pr[:], side[:, 0, 0:NM], ACT.Exp, bias=s_small[:, 1:2], scale=1.0 / 16,
                       accum_out=s_small[:, 2:3]).then_inc(soft_exp, 1)
                elif e == "p_score":
                    h = ev[1]
                    act.wait_ge(soft_max, h + 2)
                    sp_ = side[:].rearrange("p a (c m) -> p (a c) m", c=2)
                    for c in range(NCH):
                        fn(prob[:, c, :], sp_[:, c, :], ACT.Exp, bias=small[:, 1, c:c + 1], scale=1.0 / 16,
                           accum_out=small[:, 2, c:c + 1]).then_inc(soft_exp, 1)
                elif e == "p_turn":
                    act.wait_ge(side_mm, SIDE_MM[ev])
                    fn(prob_t[:], side[:], ACT.Copy).then_inc(side_free, 1)
                elif e == "conv_s":
                    act.wait_ge(conv_sum, 24)
                    fn(qkv[:, 23, 0:SEQ], cacc[1][:, 0:SEQ], ACT.Silu).then_inc(conv_silu, 1)
                    act.wait_ge(convs_sum, 1)
                    fn(qkv[:, :, SEQ:T], cvs_sum[:], ACT.Silu).then_inc(convs_silu, 1)
                elif ev == ("l2_sum", 2 * NH - 1):
                    act.wait_ge(l2_mm, 2 * NH)
                    act.wait_ge(out_mem, 32)
                    nc.scalar.preload_act_table_set("natural_log_exp_and_others")
                    fn(l2rn[:], side[0:16, 0, :], ACT.Ln, bias=const("eps", 16)).then_inc(side_free, 1)
                    act.wait_ge(side_free, SIDE[("l2_sum",)] + 1)
                    fn(l2rn[:], l2rn[:], ACT.Exp, scale=-0.5, bias=const("q_scale", 16)).then_inc(l2_rows, 1)
                elif e == "l2_s":
                    act.wait_ge(conv_silu, 24)
                    act.wait_ge(convs_silu, 1)
                    fn(s_sq[:], qkv[:, 0:2 * NH, SEQ:T], ACT.Square).then_inc(l2_sq, 1)
                    act.wait_ge(side_mm, SIDE_MM[ev])
                    nc.scalar.preload_act_table_set("natural_log_exp_and_others")
                    fn(s_rn[:].rearrange("p h b -> p (h b)"), side[:, 0, 0:2 * NH * NS], ACT.Ln, bias=const("eps"))\
                        .then_inc(side_free, 1)
                    act.wait_ge(side_free, SIDE[ev] + 1)
                    fn(s_rn[:, 0:NH], s_rn[:, 0:NH], ACT.Exp, scale=-0.5, bias=const("q_scale_all"))
                    fn(s_rn[:, NH:], s_rn[:, NH:], ACT.Exp, scale=-0.5).then_inc(l2_rows, 1)
                elif e == "sd_state":
                    for q in range(2):
                        act.wait_ge(sd_rows, q + 1)
                        fn(s_rows[:, q, :].rearrange("p (a n) -> p a n", a=2), pp[q][:], ACT.Copy)\
                            .then_inc(sd_rows_out, 1)
                elif e == "sd_ktok":
                    act.wait_ge(side_mm, SIDE_MM[ev])
                    fn(k_tok[:].rearrange("p h n -> p (h n)").rearrange("p (a n) -> p a n", a=2), side[0:NS],
                       ACT.Copy).then_inc(side_free, 1)
                elif e == "delta":
                    c = ev[1]

                    def wp(hh, step, cc=c):
                        act.wait_ge(delta_pe[hh], pe_at(hh, cc, step))

                    for hh in range(2):
                        act.wait_ge(delta_dve[hh], dve_at(hh, c, "arg"))
                        fn(dl[hh][8][:], bank[hh][0], ACT.Exp).then_inc(delta_act[hh], 1)
                    for hh in range(2):
                        act.wait_ge(delta_dve[hh], dve_at(hh, c, "arg"))
                        fn(dl[hh][0][:], dl[hh][0][:], ACT.Exp).then_inc(delta_act[hh], 1)
                    for hh in range(2):
                        wp(hh, "turn_k")
                        for step, w_, dst in (("kb", dec_kb, 5), ("kd", dec_kd, 6)):
                            for u in range(4):
                                last = fn(dl[hh][dst][:, u, :], bank[hh][0][:, u, :], ACT.Copy,
                                          scale=w_[:, c, 4 * hh + u:4 * hh + u + 1])
                            last.then_inc(delta_act[hh], 1)
                        wp(hh, "turn_v")
                        for u in range(4):
                            last = fn(dl[hh][7][:, u, :], bank[hh][1][:, u, :], ACT.Copy,
                                      scale=beta[:, c, 4 * hh + u:4 * hh + u + 1])
                        last.then_inc(delta_act[hh], 1)
                    for hh in range(2):
                        wp(hh, "turn_u")
                        fn(dl[hh][2][:], bank[hh][2], ACT.Copy).then_inc(delta_act[hh], 1)
                    for hh in range(2):
                        wp(hh, "wk")
                        fn(dl[hh][9][:], bank[hh][3], ACT.Copy, scale=-1.0).then_inc(delta_act[hh], 1)
                    for hh in range(2):
                        wp(hh, "uu")
                        fn(dl[hh][10][:], bank[hh][0], ACT.Copy).then_inc(delta_act[hh], 1)
                elif e == "o_sum":
                    for hh in range(2):
                        act.wait_ge(delta_dve[hh], dve_at(hh, NCH - 1, "s"))
                        act.wait_ge(delta_pe[hh], pe_at(hh, NCH - 1, "ss"))
                    act.wait_ge(sd_o, 1)
                    for h in range(NH):
                        if h >= 4:
                            act.wait_ge(on_mm, h - 3)
                        fn(osq[h % 4][:], qkv[:, h, :], ACT.Square).then_inc(on_sq, 1)
                    nc.scalar.preload_act_table_set("natural_log_exp_and_others")
                    act.wait_ge(on_mm, NH)
                    link(fn(orn[:].rearrange("p (a n) -> p a n", a=2), pp[0][0:16, :, 0:HALF], ACT.Ln,
                            bias=const("eps", 16), scale=1.0 / 128))
                    fn(orn[:], orn[:], ACT.Exp, scale=-0.5).then_inc(on_rows, 1)
                elif e == "wo_split":
                    act.wait_ge(out_s0, 16)
                    split_hi(WO_BLOCK)
                    split_hi(WO_BLOCK + 1)
                elif e == "m_split":
                    for k in range(KD):
                        act.wait_ge(on_done, k + 1)
                        fn(ht_h[:, k, :], mrg[:, k, :], ACT.Copy).then_inc(h_hi, 1)
                    act.wait_ge(wr_loaded, 16)
                    fn(w_r_h[:], w_r[:], ACT.Copy).then_inc(wr_hi, 1)
                elif e == "f_sum":
                    k = ev[1]
                    act.wait_ge(x1_ready, k + 1)
                    fn(h2[:, k, :], x1[:, k, :], ACT.Square).then_inc(sq_ready, 1)
                elif e == "f_sumsq":
                    nc.scalar.preload_act_table_set("natural_log_exp_and_others")
                    act.wait_ge(fin_mm, 1)
                    root_mean(pp[3], D, T).then_inc(rstd_ready, 1)
                    for k in range(KD):
                        act.wait_ge(h_norm, 16 + k + 1)
                        fn(hr_h[:, k, :], h2[:, k, :], ACT.Copy).then_inc(h_hi, 1)
                elif e == "router":
                    act.wait_ge(router_mm, 1)
                    fn(lg_t[:].rearrange("p (a n) -> p a n", a=2), pp[0][0:NG + NE, :, 0:HALF], ACT.Copy)\
                        .then_inc(lg_t_ready, 1)
                    act.wait_ge(lg_ready, 1)
                    link(fn(r8[:, :, 4:8, 0], r8[:, :, 4:8, 1], ACT.Exp))
                    fn(r8[:, :, 0:1, 3], r8[:, :, 0:1, 2], ACT.Exp).then_inc(lg_exp, 1)
                elif e == "h_turn":
                    def middle(t):
                        act.wait_ge(ht_part, t + 1)
                        fn(h2p[1][:, t, :], h2r[t % 2][:], ACT.Copy).then_inc(ht_mid, 1)

                    for t in range(ev[1], ev[2]):
                        act.wait_ge(ht_mm, t + 1)
                        fn(h2p[0][:, t, :].rearrange("p (a n) -> p a n", a=2), pp[1 + t % 3][0:TT], ACT.Copy)\
                            .then_inc(ht_hi, 1)
                        if t > ev[1]:
                            middle(t - 1)
                    middle(ev[2] - 1)
                elif e == "moe":
                    act.wait_ge(rounds_set, 1)
                    rounds = act.value_load(n_rounds[0:1, 0:1], min_val=1, max_val=9)

                    def tokens(n):
                        act.wait_ge(gather_mm, n + 1)
                        fn(xt[:].rearrange("p (a k) n -> p a (k n)", a=2), pp[0][:], ACT.Copy).then_inc(xt_ready, 1)

                    tokens(0)
                    with act.Fori(0, rounds) as r:
                        with act.Fori(0, NPAIR // 2) as p:
                            for j in range(2):
                                n = (r * (NPAIR // 2) + p) * 2 + j
                                act.wait_ge(gate_mm, n + 1)
                                fn(sg[:], pp[1][:, 0, :], ACT.Silu).then_inc(silu_done, 1)
                                act.wait_ge(selt_mm, n + 1)
                                fn(sel_t[j][:, 0:4 * TT], pp[2][:, 0, 0:4 * TT], ACT.Copy)
                                fn(sel_t[j][:, 4 * TT:T], pp[2][:, 1, 0:TT], ACT.Copy).then_inc(selt_out, 1)
                                tokens(n + 1)
                                act.wait_ge(at_mm, n + 1)
                                fn(act_t[:].rearrange("p a n -> p (a n)"), pp[1][:, 0, :], ACT.Copy)\
                                    .then_inc(at_out, 1)
                                act.wait_ge(slot_w_ready, n + 1)
                                for hf in range(2):
                                    act.wait_ge(y_mm, n * 2 + hf + 1)
                                    fn(y_hi[:, hf * 512:(hf + 1) * 512], pp[2][:, hf, :], ACT.Copy,
                                       scale=slot_w[:, 0:1]).then_inc(y_hi_ready, 1)
                elif e == "final":
                    for k in range(KD):
                        act.wait_ge(sc_free, rounds * (NPAIR * SC) + 2 + 2 * (k + 1))
                        fn(fsq[:, k, :], x1[:, k, :], ACT.Square).then_inc(fin_sq, 1)
                    nc.scalar.preload_act_table_set("natural_log_exp_and_others")
                    act.wait_ge(fin_mm, 2)
                    root_mean(pp[0], D, T).then_inc(rstd_ready, 1)

        @block.gpsimd
        def _(pool):
            tt = nc.gpsimd.tensor_tensor

            pool.wait_ge(const_in, 32)
            for ev in SCHEDULE:
                e = ev[0]
                if e == "tile":
                    j = ev[1]
                    what, t = kind(j)
                    b = j // 2
                    if what == "av":
                        out_of_psum(pool, j)
                        tt(a_sq[:, t, :], av[:, t, :], av[:, t, :], ALU.mult).then_inc(a_sq_ready, 1)
                    elif what == "gc":
                        out_of_psum(pool, j)
                        tt(mrg[:, t, :], mrg[:, t, :], qc[:, t, :], ALU.add).then_inc(gc_added, 1)
                        if t == 7:
                            pool.wait_ge(gc_added, 8)
                            for i in range(2):
                                last = nc.gpsimd.memset(xpad[i][:, 0:3], 0.0)
                            last.then_inc(conv_zero, 1)
                            nc.gpsimd.memset(st[:], 0.0).then_inc(st_zero, 1)
                    elif what == "qkv":
                        pool.wait_ge(conv_copy, t + 1)
                        nc.gpsimd.tensor_copy(convp[:, t, :], xpad[t % 2][:, SEQ:SEQ + 3])
                        nc.gpsimd.tensor_copy(ext[:, t, 3, :], xpad[t % 2][:, 3 + SEQ:3 + T]).then_inc(ext_ready, 1)
                        if 1 <= t <= 2 * NH:
                            pool.wait_ge(conv_silu, t)
                            if t >= 3:
                                pool.wait_ge(l2_mm, t - 2)
                            tt(l2sq[(t - 1) % 2][:], qkv[:, t - 1, 0:SEQ], qkv[:, t - 1, 0:SEQ], ALU.mult)\
                                .then_inc(l2_sq, 1)
                elif e == "x_sumsq":
                    pool.wait_ge(ws_loaded, 32)
                    tt(ws_t[:], ws_t[:], const("triu").rearrange("p (o n) -> p o n", o=1)
                       .to_broadcast([128, NH, CH]), ALU.mult).then_inc(ws_masked, 1)
                elif e == "ba":
                    pool.wait_ge(wba_hi, 1)
                    tt(w_ba_l[:], w_ba[:], w_ba_h[:].bitcast(F32), ALU.subtract).then_inc(wba_split, 1)
                elif e == "sd_outer":
                    h = ev[1]
                    if h == 0:
                        pool.wait_ge(side_free, SIDE[("sd_state",)] + 1)
                    tt(s0[:, h, :, :], s0[:, h, :, :], s_bc[:, 1, :, h:h + 1].to_broadcast([128, NS, 128]),
                       ALU.mult).then_inc(sd_dec, 1)
                elif e == "m_split":
                    pool.wait_ge(wr_hi, 1)
                    tt(w_r_l[:], w_r[:], w_r_h[:].bitcast(F32), ALU.subtract).then_inc(wr_split, 1)

        @block.vector
        def _(dve):
            tt = nc.vector.tensor_tensor
            ts_ = nc.vector.tensor_scalar
            stt = nc.vector.scalar_tensor_tensor
            copy = nc.vector.tensor_copy
            chain = [0]

            def link(ins):
                chain[0] += 1
                ins.then_inc(dve_chain, 1)
                dve.wait_ge(dve_chain, chain[0])

            def weights_lo(b):
                dve.wait_ge(hi_ready, b + 1)
                tt(w_l[b % 2][:], raw[b % 2][:], w_h[b % 2][:].bitcast(F32), ALU.subtract).then_inc(lo_ready, 1)

            def normed(dst, src, gain, n, done):
                for k in range(KD):
                    stt(dst[:, k, :], src[:, k, :], param(gain, k), rstd[:, 0:n], ALU.mult, ALU.mult)\
                        .then_inc(done, 1)

            def normed_split(dst, src, gain, n, done, lo, hi, at):
                for k in range(KD + 1):
                    if k < KD:
                        stt(dst[:, k, :], src[:, k, :], param(gain, k), rstd[:, 0:n], ALU.mult, ALU.mult)\
                            .then_inc(done, 1)
                    if k:
                        dve.wait_ge(h_hi, at + k)
                        tt(lo[:, k - 1, :], dst[:, k - 1, :], hi[:, k - 1, :].bitcast(F32), ALU.subtract)\
                            .then_inc(h_lo, 1)

            def split_lo(lo, hi, src, at):
                for k in range(KD):
                    dve.wait_ge(h_hi, at + k + 1)
                    tt(lo[:, k, :], src[:, k, :], hi[:, k, :].bitcast(F32), ALU.subtract).then_inc(h_lo, 1)

            def tile(j):
                what, t = kind(j)
                b = j // 2
                if j % 2 == 0 and b + 1 < (WO_BLOCK if b < WO_BLOCK else NBLK) and b + 1 != WO_BLOCK + 1:
                    weights_lo(b + 1)
                ps = pp[j % 3][:, :, 0:HALF]
                free = psum_free[j % 3]

                def whole(x):
                    return x.rearrange("p (a n) -> p a n", a=2)

                if what in ("mk", "mv", "qm", "wo"):
                    dve.wait_ge(tile_mm, j + 1)
                if what == "mk":
                    copy(mk[:, t, :], pp[j % 3][:, 0, 0:NM]).then_inc(free, 1)
                elif what == "mv":
                    copy(mv[:, t % 2, (t // 2) * BLK:(t // 2 + 1) * BLK], pp[j % 3][:, 0, 0:BLK]).then_inc(free, 1)
                elif what == "ga":
                    dve.wait_ge(tile_act, t + 1)
                    tt(whole(mrg[:, t, :]), ps, whole(au[:, t, :]), ALU.mult).then_inc(free, 1)
                elif what == "qm":
                    copy(whole(qc[:, t, :]), ps).then_inc(free, 1)
                elif what == "z":
                    dve.wait_ge(tile_act, 8 + t + 1)
                    out_of_psum(dve, j - 8)
                    stt(whole(zg[:, t, :]), ps, param("norm_gdn"), whole(zg[:, t, :]), ALU.mult, ALU.mult)\
                        .then_inc(free, 1)
                elif what == "gc":
                    dve.wait_ge(tile_act, 16 + t + 1)
                    dve.wait_ge(side_free, SIDE[("p_value", t // 2)] + 1)
                    tt(whole(qc[:, t, :]), ps, whole(qc[:, t, :]), ALU.mult).then_inc(free, 1)
                elif what == "qkv":
                    out_of_psum(dve, j)
                    c_, x_ = cacc[t % 2], xpad[t % 2]
                    for tap in range(3):
                        ins = stt(c_[:, 0:SEQ], x_[:, tap:tap + SEQ], param("w_conv", 4 * t + tap), c_[:, 0:SEQ],
                                  ALU.mult, ALU.add)
                        if tap < 2:
                            link(ins)
                        else:
                            ins.then_inc(conv_sum, 1)
                elif what == "wo":
                    dve.wait_ge(xres_loaded, 16)
                    tt(whole(x1[:, t, :]), ps, whole(x_res[:, t, :]), ALU.add).then_inc(x1_ready, 1)

            dve.wait_ge(const_in, 32)
            for ev in SCHEDULE:
                e = ev[0]
                if e == "tile":
                    tile(ev[1])
                elif e == "x_sumsq":
                    weights_lo(0)
                    dve.wait_ge(side_free, SIDE[ev] + 1)
                    normed_split(x_in, x_in, "norm_mix", T, h_norm, ht_l, ht_h, 0)
                elif e == "m_sumsq":
                    dve.wait_ge(side_free, SIDE[ev] + 1)
                    normed_split(mem, mem, "norm_mem", NM, h_norm, mem_l, mem_h, 8)
                elif e == "a_sumsq":
                    dve.wait_ge(side_free, SIDE[ev] + 1)
                    normed(av, av, "norm_a_v", T, a_normed)
                elif e == "a_mix":
                    g = ev[1]
                    if g == 0:
                        dve.wait_ge(a_normed, 8)
                        for i in range(13, 16):
                            out_of_psum(dve, i)
                        link(tt(s_tmp[:], av[:, :, SEQ:T],
                                param("ws00").rearrange("p (g o) -> p g o", o=1).to_broadcast([128, NH, NS]), ALU.mult))
                        link(tt(s_tmp[:], s_tmp[:],
                                param("bs0").rearrange("p (g o) -> p g o", o=1).to_broadcast([128, NH, NS]), ALU.add))
                        link(tt(au[:, :, SEQ:T], au[:, :, SEQ:T], s_tmp[:], ALU.mult))
                    dve.wait_ge(side_mm, SIDE_MM[ev])
                    tt(au[:, g:g + 2, 0:SEQ], side[:], au[:, g:g + 2, 0:SEQ], ALU.mult).then_inc(side_free, 1)
                elif e == "ba_turn":
                    dve.wait_ge(side_mm, SIDE_MM[ev])
                    copy(ba[:, 0:4, :].rearrange("p c n -> p (c n)"), side[:, 0, 0:64])
                    copy(ba[0:NS, 4, :], side[0:NS, 0, 64:80]).then_inc(side_free, 1)
                    dve.wait_ge(side_free, SIDE[ev] + 1)
                    for rows, ts in ((128, slice(0, 4)), (NS, slice(4, 5))):
                        n = ts.stop - ts.start
                        last = tt(tmp_g[0:rows, 0, ts, :], ba[0:rows, ts, NH:2 * NH],
                                  param("dt_bias")[0:rows].rearrange("p (o h) -> p o h", o=1)
                                  .to_broadcast([rows, n, NH]), ALU.add)
                    last.then_inc(g_step, 1)
                    dve.wait_ge(g_act, 2)
                    for rows, ts in ((128, slice(0, 4)), (NS, slice(4, 5))):
                        n = ts.stop - ts.start
                        link(stt(tmp_g[0:rows, 0, ts, :], tmp_g[0:rows, 0, ts, :], 0.0, tmp_g[0:rows, 1, ts, :],
                                 ALU.max, ALU.add))
                        stt(gate_g[0:rows, ts, :], tmp_g[0:rows, 0, ts, :], -1.0,
                            neg_a[0:rows].rearrange("p (o h) -> p o h", o=1).to_broadcast([rows, n, NH]),
                            ALU.mult, ALU.mult).then_inc(g_step, 1)
                elif e == "cumsum":
                    dve.wait_ge(side_mm, SIDE_MM[ev])
                    flat = cum_g[:].rearrange("p c h -> p (c h)")
                    copy(flat, side[:, 0, 0:32]).then_inc(g_step, 1)
                    dve.wait_ge(g_step, 4)
                    tt(dec_kd[:].rearrange("p c h -> p (c h)"), side[:, 0, 32:64], flat, ALU.subtract)\
                        .then_inc(g_step, 1)
                    dve.wait_ge(g_act, 8)
                    tt(dec_kb[:], dec_kb[:], beta[:, 0:NCH, :], ALU.mult).then_inc(side_free, 1)
                elif e == "s_query":
                    dve.wait_ge(out_av, 16)
                    for i in range(45, 48):
                        out_of_psum(dve, i)
                    link(nc.vector.memset(s_q[:], 0.0))
                    copy(s_q[:, :, 0:NS * 32:33], qc[:, :, SEQ:T]).then_inc(s_q_ready, 1)
                elif ev == ("s_score", NS - 1):
                    dve.wait_ge(kv_used, NS)
                    link(nc.vector.memset(s_p[:], 0.0))
                    link(nc.vector.tensor_reduce(s_small[:, 0:1], side[:, 0, 0:NM], AX.X, ALU.max))
                    ts_(s_small[:, 1:2], s_small[:, 0:1], -1.0 / 16, None, ALU.mult).then_inc(soft_max, 1)
                    dve.wait_ge(soft_exp, 1)
                    link(nc.vector.reciprocal(s_small[:, 3:4], s_small[:, 2:3]))
                    ts_(s_pr[:], s_pr[:], s_small[:, 3:4], None, ALU.mult).then_inc(soft_norm, 1)
                    nc.vector.memset(s_small[:, 0:1], 0.0).then_inc(side_free, 1)
                elif e == "s_cols":
                    dve.wait_ge(side_mm, SIDE_MM[ev])
                    copy(s_p[:, :, 0:NS * 32:33], side[:, 0, 0:NM].rearrange("p (g b) -> p g b", b=32)[:, :, 0:NS])\
                        .then_inc(side_free, 1)
                elif ev == ("s_value", NS - 1):
                    dve.wait_ge(kv_used, 2 * NS)
                    copy(s_o[:], side[:, 1, 0:NM]).then_inc(side_free, 1)
                elif e == "s_back":
                    dve.wait_ge(side_mm, SIDE_MM[ev])
                    copy(qc[:, :, SEQ:T].rearrange("p (h d) b -> p d h b", d=2),
                         side[:, 0, 0:NM].rearrange("p (d h b) -> p d h b", d=2, b=32)[:, :, :, 0:NS])\
                        .then_inc(side_free, 1)
                elif e == "p_score":
                    h = ev[1]
                    dve.wait_ge(side_mm, SIDE_MM[ev])
                    link(nc.vector.tensor_reduce(small[:, 0, :], side[:].rearrange("p a (c m) -> p (a c) m", c=2),
                                                 AX.X, ALU.max))
                    ts_(small[:, 1, :], small[:, 0, :], -1.0 / 16, None, ALU.mult).then_inc(soft_max, 1)
                    dve.wait_ge(soft_exp, 1 + NCH * (h + 1))
                    link(nc.vector.reciprocal(small[:, 3, :], small[:, 2, :]))
                    tt(prob[:], prob[:], small[:, 3, :].rearrange("p (c o) -> p c o", o=1)
                       .to_broadcast([128, NCH, NM]), ALU.mult).then_inc(soft_norm, 1)
                    nc.vector.memset(small[:, 0, :], 0.0).then_inc(side_free, 1)
                elif e == "p_value":
                    dve.wait_ge(side_mm, SIDE_MM[ev])
                    h = ev[1]
                    copy(qc[:, 2 * h:2 * h + 2, 0:SEQ], side[:]).then_inc(side_free, 1)
                elif e == "conv_s":
                    dve.wait_ge(ext_loaded, 16)
                    dve.wait_ge(ext_ready, 24)
                    link(tt(cvs[:], ext[:], param("w_conv").rearrange("p (t j o) -> p t j o", t=24, o=1)
                            .to_broadcast([128, 24, 4, NS]), ALU.mult))
                    nc.vector.tensor_reduce(cvs_sum[:], cvs[:].rearrange("p t j b -> p t b j"), AX.X, ALU.add)\
                        .then_inc(convs_sum, 1)
                elif e == "l2_spread":
                    t = 2 * ev[1]
                    dve.wait_ge(side_mm, SIDE_MM[ev])
                    tt(qkv[:, t:t + 2, 0:SEQ], side[:], qkv[:, t:t + 2, 0:SEQ], ALU.mult).then_inc(side_free, 1)
                    dve.wait_ge(side_free, SIDE[ev] + 1)
                    nc.vector.memset(small[:, 0, 2:3], 0.0).then_inc(l2_done, 1)
                elif e == "sd_bcast":
                    dve.wait_ge(l2_rows, 2)
                    tt(qkv[:, 0:2 * NH, SEQ:T], qkv[:, 0:2 * NH, SEQ:T], s_rn[:], ALU.mult).then_inc(l2_done, 1)
                    dve.wait_ge(l2_done, NH + 1)
                    for i in range(2):
                        last = copy(s_kq[:, :, 16 * i:16 * i + 16].rearrange("p b h -> p h b"),
                                    qkv[:, 0:2 * NH, SEQ:T])
                    last.then_inc(sd_rhs, 1)
                    idb = const("ident", NS)[:, 0:NS].rearrange("p (c o) -> p c o", o=1).to_broadcast([NS, NS, NH])
                    for i, src in enumerate((beta[0:NS, 4, :], s_eg[:])):
                        last = tt(s_rhs[:, i, :, :], idb,
                                  src.rearrange("p (o h) -> p o h", o=1).to_broadcast([NS, NS, NH]), ALU.mult)
                    last.then_inc(sd_rhs, 1)
                    dve.wait_ge(l2_done, NH + 1)
                    tt(s_qk[:], qkv[:, 0:NH, SEQ:T], qkv[:, NH:2 * NH, SEQ:T], ALU.mult).then_inc(sd_rhs, 1)
                    dve.wait_ge(side_mm, SIDE_MM[ev])
                    copy(s_bc[:].rearrange("p a c h -> p (a c h)"), side[:, 0, 0:2 * NS * NH])
                    copy(s_qk[:].rearrange("p h b -> p (h b)"), side[:, 1, 0:NS * NH]).then_inc(side_free, 1)
                elif e == "sd_state":
                    dve.wait_ge(side_free, SIDE[("sd_bcast",)] + 1)
                    dve.wait_ge(side_mm, SIDE_MM[ev])
                    for a in range(2):
                        for q in range(2):
                            flat = pp[q][:].rearrange("p a n -> p (a n)")
                            for hh in range(4):
                                at_ = 256 * hh + 4 * q + hh + 8 * a
                                last = copy(s_sv[:, a, 4 * q + hh, :], flat[:, at_:at_ + 225:32])
                    link(last)
                    sv = s_sv
                    bb, eg = s_bc[:, 0, :, :].rearrange("p b h -> p h b"), s_bc[:, 1, :, :].rearrange("p b h -> p h b")
                    link(tt(s_u[:], sv[:, 1, :, :], eg, ALU.mult))
                    link(tt(s_u[:], qkv[:, 2 * NH:3 * NH, SEQ:T], s_u[:], ALU.subtract))
                    tt(s_u[:], s_u[:], bb, ALU.mult).then_inc(sd_u, 1)
                    link(tt(s_tmp[:], sv[:, 0, :, :], eg, ALU.mult))
                    dve.wait_ge(sd_u, 1)
                    link(tt(s_qk[:], s_qk[:], s_u[:], ALU.mult))
                    tt(qkv[:, 0:NH, SEQ:T], s_qk[:], s_tmp[:], ALU.add).then_inc(side_free, 1)
                elif e == "sd_utok":
                    dve.wait_ge(side_mm, SIDE_MM[ev])
                    copy(u_tok[:].rearrange("p h n -> p (h n)").rearrange("p (a n) -> p a n", a=2), side[0:NS])\
                        .then_inc(side_free, 1)
                elif e == "sd_outer":
                    h = ev[1]

                    def diag(h):
                        if h >= 2:
                            dve.wait_ge(side_mm, SIDE_MM[("sd_outer", h - 2)])
                        tt(u_diag[h % 2][:], u_tok[:, h:h + 1, :].to_broadcast([NS, NS, 128]),
                           const("ident", NS)[:, 0:NS].rearrange("p (c o) -> p c o", o=1)
                           .to_broadcast([NS, NS, 128]), ALU.mult).then_inc(sd_diag, 1)

                    if h == 0:
                        dve.wait_ge(side_free, SIDE[("sd_utok",)] + 1)
                        diag(0)
                    if h + 1 < NH:
                        diag(h + 1)
                    dve.wait_ge(side_mm, SIDE_MM[ev])
                    dve.wait_ge(sd_dec, h + 1)
                    tt(s0[:, h, :, :].rearrange("p (a b) n -> p a (b n)", a=2), pp[3 - h % 2][:],
                       s0[:, h, :, :].rearrange("p (a b) n -> p a (b n)", a=2), ALU.add).then_inc(side_free, 1)
                    dve.wait_ge(side_free, SIDE[ev] + 1)
                    nc.vector.memset(small[:, 0, 0:1], 0.0).then_inc(sd_new, 1)
                    if h == 0:
                        nc.vector.memset(small[:, 0, 1:2], 0.0).then_inc(sd_o, 1)
                elif e == "delta":
                    c = ev[1]
                    cs = slice(c * CH, (c + 1) * CH)

                    def wp(hh, step, cc=c):
                        dve.wait_ge(delta_pe[hh], pe_at(hh, cc, step))

                    def wa(hh, step, cc=c):
                        dve.wait_ge(delta_act[hh], act_at(hh, cc, step))

                    def wide(mask):
                        return mask.rearrange("p (o n) -> p o n", o=1).to_broadcast([128, 4, 128])

                    for hh in range(2):
                        wp(hh, "grow")
                        if c:
                            wp(hh, "oo", c - 1)
                        for u in range(4):
                            h = 4 * hh + u
                            last = ts_(dl[hh][0][:, u, :], bank[hh][0][:, u, :], cum_g[:, c, h:h + 1], 0.0,
                                       ALU.subtract, ALU.min)
                        last.then_inc(delta_dve[hh], 1)
                    for hh in range(2):
                        wa(hh, "dt")
                        link(tt(dl[hh][1][:], dl[hh][0][:], wide(const("strict")), ALU.mult))
                        wp(hh, "brow")
                        tt(dl[hh][1][:], bank[hh][1], dl[hh][1][:], ALU.mult).then_inc(delta_dve[hh], 1)
                    for hh in range(2):
                        wp(hh, "kk")
                        dve.wait_ge(delta_dve[hh], dve_at(hh, c, "bs"))
                        tt(dl[hh][1][:], bank[hh][2], dl[hh][1][:], ALU.mult).then_inc(delta_dve[hh], 1)
                    for hh in range(2):
                        dve.wait_ge(delta_dve[hh], dve_at(hh, c, "mt"))
                        link(tt(dl[hh][4][:], dl[hh][1][:], wide(const("first_t")), ALU.mult))
                        tt(dl[hh][3][:], wide(const("ident")), dl[hh][4][:], ALU.subtract)\
                            .then_inc(delta_dve[hh], 1)
                    for hh in range(2):
                        link(tt(dl[hh][0][:], dl[hh][0][:], wide(const("triu")), ALU.mult))
                        wp(hh, "kq")
                        tt(dl[hh][0][:], bank[hh][3], dl[hh][0][:], ALU.mult).then_inc(delta_dve[hh], 1)
                    for hh in range(2):
                        wa(hh, "eg")
                        tt(dl[hh][8][:], qkv[:, 4 * hh:4 * hh + 4, cs], dl[hh][8][:], ALU.mult)\
                            .then_inc(delta_dve[hh], 1)
                    for l in range(6):
                        x, y = CONST["merge"]
                        mask = consts[:, x + l * 128:x + (l + 1) * 128]
                        for hh in range(2):
                            wp(hh, f"mt{l}")
                            tt(dl[hh][4][:], bank[hh][2], wide(mask), ALU.mult).then_inc(delta_dve[hh], 1)
                        for hh in range(2):
                            wp(hh, f"tx{l}")
                            if l < 5:
                                tt(dl[hh][2][:], dl[hh][2][:], bank[hh][3], ALU.subtract)
                            tt(dl[hh][3][:], dl[hh][3][:], bank[hh][2], ALU.subtract).then_inc(delta_dve[hh], 1)
                    for hh in range(2):
                        wp(hh, "oo")
                        copy(qkv[:, 4 * hh:4 * hh + 4, cs], bank[hh][1]).then_inc(delta_dve[hh], 1)
                    for hh in range(2):
                        wp(hh, "ss")
                        if c == 0:
                            dve.wait_ge(st_zero, 1)
                        else:
                            dve.wait_ge(delta_dve[hh], dve_at(hh, c - 1, "s"))
                        for u in range(4):
                            h = 4 * hh + u
                            last = stt(st[:, h, :], st[:, h, :], dec_end[:, c, h:h + 1], bank[hh][2][:, u, :],
                                       ALU.mult, ALU.add)
                        last.then_inc(delta_dve[hh], 1)
                elif e == "o_sum":
                    for hh in range(2):
                        dve.wait_ge(delta_dve[hh], dve_at(hh, NCH - 1, "s"))
                    for h in range(NH):
                        tt(zg[:, h, :], qkv[:, h, :], zg[:, h, :], ALU.mult).then_inc(on_z, 1)
                elif e == "o_spread":
                    h = ev[1]

                    def merge(h):
                        dve.wait_ge(on_mul, h + 1)
                        tt(mrg[:, h, :], mrg[:, h, :], zg[:, h, :], ALU.add).then_inc(on_done, 1)

                    if h == 0:
                        dve.wait_ge(gc_added, 8)
                        dve.wait_ge(on_z, NH)
                    dve.wait_ge(on_spread, h + 1)
                    z = zg[:, h, :].rearrange("p (a n) -> p a n", a=2)
                    tt(z, pp[1 + h % 3][:, :, 0:HALF], z, ALU.mult).then_inc(on_mul, 1)
                    if h:
                        merge(h - 1)
                    if h == NH - 1:
                        merge(h)
                elif e == "wo_split":
                    weights_lo(WO_BLOCK)
                    weights_lo(WO_BLOCK + 1)
                elif e == "m_split":
                    split_lo(ht_l, ht_h, mrg, 16)
                elif e == "f_sumsq":
                    dve.wait_ge(rstd_ready, 1)
                    normed(h2, x1, "norm_ffn", T, h_norm)
                    split_lo(hr_l, hr_h, h2, 24)
                elif e == "router":
                    dve.wait_ge(logits_mm, 1)
                    copy(strict_b[:], const("strict", TT)[:, 0:TT])
                    copy(ones_b[:], const("ones", TT))
                    link(tt(lg[:], pp[0][0:TT, 0, 0:180].rearrange("p (t n) -> p t n", t=NT),
                            param("b_router")[0:TT].rearrange("p (o n) -> p o n", o=1)
                            .to_broadcast([TT, NT, NG + NE]), ALU.add))
                    gl = lg[:, :, 0:NG]
                    g_top, g_first = r8[:, :, 0:1, 0], r8[:, :, 1:2, 0]
                    one4 = r8[:, :, 0:4, 1]

                    def wide(x, n):
                        return x.to_broadcast([TT, NT, n])

                    def first_top(one, src, top, tmp, desc, n):
                        d_ = const(desc, TT).rearrange("p (o n) -> p o n", o=1).to_broadcast([TT, NT, n])
                        link(nc.vector.tensor_reduce(top, src, AX.X, ALU.max))
                        link(tt(one, src, wide(top, n), ALU.is_equal))
                        link(tt(one, one, d_, ALU.mult))
                        link(nc.vector.tensor_reduce(tmp, one, AX.X, ALU.max))
                        link(tt(one, one, wide(tmp, n), ALU.is_equal))

                    first_top(one4, gl, g_top, g_first, "desc4", 4)
                    link(tt(prod32[:], lg[:, :, NG:].rearrange("p t (g x) -> p t g x", g=NG),
                            one4.rearrange("p t (g o) -> p t g o", o=1).to_broadcast([TT, NT, NG, EPG]), ALU.mult))
                    link(nc.vector.tensor_reduce(ing[:], prod32[:].rearrange("p t g x -> p t x g"), AX.X, ALU.add))
                    m1, m2, f1 = r8[:, :, 2:3, 0], r8[:, :, 3:4, 0], r8[:, :, 0:1, 3]
                    first_top(oh1[:], ing[:], m1, f1, "desc8", 8)
                    link(stt(ing2[:], oh1[:], -3.0e38, ing[:], ALU.mult, ALU.add))
                    first_top(oh2[:], ing2[:], m2, f1, "desc8", 8)
                    link(tt(r8[:, :, 0:1, 2], m2, m1, ALU.subtract))
                    tt(r8[:, :, 4:8, 1], gl, wide(g_top, 4), ALU.subtract).then_inc(lg_ready, 1)
                    dve.wait_ge(lg_exp, 1)
                    psum_, e2, w1, w2 = r8[:, :, 1:2, 2], r8[:, :, 0:1, 3], r8[:, :, 2:3, 2], r8[:, :, 3:4, 2]
                    link(nc.vector.tensor_reduce(psum_, r8[:, :, 4:8, 0], AX.X, ALU.add))
                    link(ts_(w1, e2, 1.0, None, ALU.add))
                    link(tt(w1, w1, psum_, ALU.mult))
                    link(nc.vector.reciprocal(w1, w1))
                    link(tt(w2, w1, e2, ALU.mult))
                    link(tt(w8[:], oh1[:], wide(w1, EPG), ALU.mult))
                    link(tt(ing2[:], oh2[:], wide(w2, EPG), ALU.mult))
                    link(tt(w8[:], w8[:], ing2[:], ALU.add))
                    link(tt(ing[:], oh1[:], oh2[:], ALU.add))
                    o4 = one4.rearrange("p t (g o) -> p t g o", o=1).to_broadcast([TT, NT, NG, EPG])

                    def over_groups(x):
                        return x[:].rearrange("p t (o x) -> p t o x", o=1).to_broadcast([TT, NT, NG, EPG])

                    link(tt(comb[:].rearrange("p t (g x) -> p t g x", g=NG), over_groups(w8), o4, ALU.mult))
                    tt(hit[:].rearrange("p t (g x) -> p t g x", g=NG), over_groups(ing), o4, ALU.mult)\
                        .then_inc(hit_ready, 1)
                elif e == "h_turn":
                    def low(t):
                        dve.wait_ge(ht_mid, t + 1)
                        tt(h2p[2][:, t, :], h2r[t % 2][:], h2p[1][:, t, :], ALU.subtract).then_inc(ht_lo, 1)

                    for t in range(ev[1], ev[2]):
                        dve.wait_ge(ht_hi, t + 1)
                        if t >= 2:
                            dve.wait_ge(ht_lo, t - 1)
                        tt(h2r[t % 2][:].rearrange("p (a n) -> p a n", a=2), pp[1 + t % 3][0:TT],
                           h2p[0][:, t, :].rearrange("p (a n) -> p a n", a=2), ALU.subtract).then_inc(ht_part, 1)
                        if t > ev[1]:
                            low(t - 1)
                    low(ev[2] - 1)
                elif e == "rank":
                    dve.wait_ge(rank_mm, 1)
                    link(stt(rank[:, :, 0:NE], pp[0][0:TT, 1, 0:NT * NE].rearrange("p (t n) -> p t n", t=NT), 1.0,
                             hit[:], ALU.add, ALU.mult))
                    link(ts_(rank[:, :, 0:NE], rank[:, :, 0:NE], -1.0, None, ALU.add))
                    link(ts_(rank[:, :, NE:NE + 2], rank[:, :, 0:2], -float(CAP), None, ALU.add))
                    link(nc.vector.tensor_reduce(cnt[:, 0:1], pp[0][:, 1, 160:160 + NE], AX.X, ALU.max))
                    link(ts_(cnt[:, 8:16], const("rounds"), cnt[:, 0:1], None, ALU.is_lt))
                    link(nc.vector.tensor_reduce(cnt[:, 1:2], cnt[:, 8:16], AX.X, ALU.add))
                    ts_(n_rounds[0:1, 0:1], cnt[0:1, 1:2], 1.0, None, ALU.add).then_inc(rounds_set, 1)
                    nc.vector.memset(fill[:, 0:1], 0.0).then_inc(sc_free, 2)
                elif e == "moe":
                    dve.wait_ge(rounds_set, 1)
                    dve.wait_ge(ht_mm, NT)
                    rounds = dve.value_load(n_rounds[0:1, 0:1], min_val=1, max_val=9)
                    slots = const("slots", TT).rearrange("p (o a n) -> p o a n", o=1, a=1)\
                        .to_broadcast([TT, NT, 2, CAP])
                    def one_hot(n, j, ex):
                        at_ = rank[:, :, bass.ds(ex, 2)].rearrange("p t (e o) -> p t e o", o=1)
                        tt(sel[j][:], slots, at_.to_broadcast([TT, NT, 2, CAP]), ALU.is_equal).then_inc(sel_ready, 1)

                    def add_back(n, s0_, s1_):
                        for s in range(s0_, s1_):
                            dc, hf = s // 2, s % 2
                            dve.wait_ge(sc_mm, n * SC + s + 1)
                            xs = x1[:, dc, hf * HALF:(hf + 1) * HALF]
                            tt(xs, pp[3][:, s % 2, 0:HALF], xs, ALU.add).then_inc(sc_free, 1)

                    one_hot(0, 0, 0)
                    copy(ident_b[:], const("ident"))
                    c3 = [comb3[:, :, :, i:i + 1].rearrange("p t e o -> p t (e o)") for i in range(3)]
                    link(copy(c3[0], comb[:]))
                    link(tt(comb_r[:], comb[:], c3[0], ALU.subtract))
                    link(copy(c3[1], comb_r[:]))
                    link(tt(c3[2], comb_r[:], c3[1], ALU.subtract))
                    for dst in (y_hi[:], y_lo[:], sel_t[1][:]):
                        last = ts_(dst, consts[:, 0:dst.shape[1]], 0.0, None, ALU.mult)
                    last.then_inc(y_out, 1)
                    with dve.Fori(0, rounds) as r:
                        with dve.Fori(0, NPAIR // 2) as p:
                            for j in range(2):
                                n = (r * (NPAIR // 2) + p) * 2 + j
                                ex = p * 4 + j * 2
                                dve.wait_ge(gather_mm, n + 1)
                                one_hot(n + 1, 1 - j, ex + 2)
                                copy(pair_w[:], comb3[:, :, bass.ds(ex, 2), :]).then_inc(pair_w_ready, 1)
                                add_back(n, 0, SC - 3)
                                dve.wait_ge(selt_mm, n + 1)
                                for i in range(2):
                                    rows = slice(i * CAP, (i + 1) * CAP)
                                    last = nc.vector.tensor_reduce(slot_w[rows, 0:1], pp[1][rows, 0, 3 * i:3 * i + 3],
                                                                   AX.X, ALU.add)
                                last.then_inc(slot_w_ready, 1)
                                dve.wait_ge(silu_done, n + 1)
                                dve.wait_ge(gu_mm, n + 1)
                                tt(act_r[:], pp[1][:, 1, :], sg[:], ALU.mult).then_inc(act_ready, 1)
                                add_back(n, SC - 3, SC)
                                dve.wait_ge(slot_w_ready, n + 1)
                                for hf in range(2):
                                    dve.wait_ge(y_hi_ready, n * 2 + hf + 1)
                                    cs = slice(hf * 512, (hf + 1) * 512)
                                    last = stt(y_lo[:, cs], pp[2][:, hf, :], slot_w[:, 0:1], y_hi[:, cs].bitcast(F32),
                                               ALU.mult, ALU.subtract)
                                last.then_inc(y_out, 1)
                        dve.wait_ge(sel_ready, (r + 1) * NPAIR + 1)
                        ts_(rank[:], rank[:], -float(CAP), None, ALU.add).then_inc(rank_moved, 1)
                        dve.wait_ge(rank_moved, r + 1)
                    add_back(rounds * NPAIR, 0, SC)
                elif e == "final":
                    dve.wait_ge(rstd_ready, 2)
                    normed(x1, x1, "norm_final", T, fin_done)


def kernel(**inputs):
    import numpy as _np
    import concourse.bacc as _bacc
    from concourse.bass_utils import run_bass_kernel_spmd as _run

    f = {k: _np.asarray(v) for k, v in inputs.items()}

    def chunks(x):
        return x.reshape(x.shape[0], -1, 128).transpose(2, 1, 0)

    def cols(x):
        return x.reshape(-1, 128).T

    def everywhere(x):
        return _np.broadcast_to(x.reshape(1, -1), (128, x.size))

    w_in = f["w_in"][0]
    edge = _np.cumsum([0, D, D, 3 * D, D, NH, NH, D, D, D, D])
    part = {n: w_in[:, edge[i]:edge[i + 1]] for i, n in
            enumerate(("au", "av", "qkv", "z", "beta", "alpha", "qm", "ga", "gb", "gc"))}
    part["mk"], part["mv"] = f["w_mem_kv"][0][:, :D], f["w_mem_kv"][0][:, D:]
    part["wo"] = f["w_o"][0]
    w_blk = _np.concatenate([part[n].reshape(KD, 128, -1, BLK).transpose(2, 1, 0, 3) for n, _ in BLOCKS])
    kc = f["cache_mem_k"][0].reshape(NS, NM, MH, 2, 128).transpose(0, 4, 2, 3, 1)
    vc = f["cache_mem_v"][0].reshape(NS, 2, 128, D).transpose(0, 2, 1, 3)
    x = _np.concatenate([f["x_prompt"][0], f["x_sample"][:, 0]])
    par = _np.concatenate([
        cols(f["norm_mix"]), cols(f["norm_mem"]), cols(f["norm_ffn"]), cols(f["norm_final"]),
        cols(f["norm_a_v"]), f["norm_gdn_out"].T, cols(f["b_gate"]),
        f["w_conv"][0].reshape(4, 24, 128).transpose(2, 1, 0).reshape(128, 96),
        everywhere(f["w_s"][0, :, 0, 0]), everywhere(f["b_s"][0, :, 0]), everywhere(f["a_log"][0]),
        everywhere(f["dt_bias"][0]), everywhere(f["b_router_group"][0]), everywhere(f["b_router_expert"][0])],
        axis=1)

    def rows(w, n):
        return w.reshape(NE, n, 128, -1).transpose(0, 2, 1, 3).reshape(NE, 128, -1)

    arrays = {
        "consts": make_constants(), "params": par,
        "x_t": chunks(x).reshape(128, -1), "mem_t": chunks(f["mem_prompt"][0]).reshape(128, -1),
        "w_blk": w_blk.reshape(NBLK, 128, -1),
        "w_ba": _np.concatenate([part["beta"], part["alpha"]], 1).reshape(KD, 128, 16).transpose(1, 0, 2)
                   .reshape(128, -1),
        "ws_t": f["w_s"][0].transpose(2, 0, 1).reshape(128, -1), "bs": f["b_s"][0].reshape(1, -1),
        "cache_k": kc.reshape(NS, 128, -1), "cache_v": vc.reshape(NS, 128, -1),
        "state_conv": f["state_conv"][0].reshape(NS, 3, 24, 128).transpose(3, 2, 1, 0).reshape(128, -1),
        "state_gdn": f["state_gdn"][0].transpose(2, 1, 0, 3).reshape(128, -1),
        "w_router": _np.concatenate([f["w_router_group"][0], f["w_router_expert"][0]], 1)
                       .reshape(KD, 128, NG + NE).transpose(1, 0, 2).reshape(128, -1),
        "w_gate": rows(f["w_exp_gate"], KD), "w_up": rows(f["w_exp_up"], KD), "w_down": rows(f["w_exp_down"], 4),
    }
    arrays = {k: _np.ascontiguousarray(v) for k, v in arrays.items()}
    outs = {"y": KD * T, "av": KD * NS, "mk": KD * NM, "mv": 2 * D, "conv_s": 24 * 3 * NS, "conv_p": 24 * 3,
            "gdn_s": NH * NS * 128, "gdn_p": NH * 128}

    nc = _bacc.Bacc("TRN2", target_bir_lowering=False, num_devices=1)
    a = {k: nc.dram_tensor(f"in_{k}", v.shape, mybir.dt.from_np(v.dtype), kind="ExternalInput").ap()
         for k, v in arrays.items()}
    o = {k: nc.dram_tensor(f"out_{k}", (128, n), F32, kind="ExternalOutput").ap() for k, n in outs.items()}
    build_step(nc, a, o)
    got = _run(nc, [{f"in_{k}": v for k, v in arrays.items()}], core_ids=[0]).results[0]
    r = {k: got[f"out_{k}"] for k in outs}

    y = r["y"].reshape(128, KD, T).transpose(2, 1, 0).reshape(T, D)
    return (
        y[:SEQ].reshape(1, SEQ, D), y[SEQ:].reshape(NS, 1, D),
        r["mk"].reshape(128, KD, NM).transpose(2, 1, 0).reshape(1, 1, NM, MH, D // MH),
        r["mv"].reshape(128, 2, D).transpose(1, 0, 2).reshape(1, 1, NM, MH, D // MH),
        r["gdn_p"].reshape(128, NH, 128).transpose(1, 0, 2).reshape(1, 1, NH, 128, 128),
        r["conv_p"].reshape(128, 24, 3).transpose(2, 1, 0).reshape(1, 1, 3, 3 * D),
        r["gdn_s"].reshape(128, NH, NS, 128).transpose(2, 1, 0, 3).reshape(1, NS, NH, 128, 128),
        r["conv_s"].reshape(128, 24, 3, NS).transpose(3, 2, 1, 0).reshape(1, NS, 3, 3 * D),
        r["av"].reshape(128, KD, NS).transpose(2, 1, 0).reshape(1, NS, 1, D),
    )
```
